# Optimizing a Trainium2 kernel written in Bass

```python
import jax, jax.numpy as jnp
from jax import lax
import numpy as np

D_MODEL = 1024
BATCH = 1
SEQ = 512
DEPTH = 2
DEC_BATCH = 8
DEC_SEQ = 1
PAST_LEN = 1024
PAGE_SIZE = 128

HEAD_DIM = 64
N_FOX_HEADS = 8
N_RET_HEADS = 8
FOX_WIDTH = N_FOX_HEADS * HEAD_DIM
RET_WIDTH = N_RET_HEADS * HEAD_DIM
EVEN_IN = 3 * FOX_WIDTH + N_FOX_HEADS + 4 * RET_WIDTH
CONV_WIDTH = 3
D_FF = 2816
Q_BLOCK = 128
RET_CHUNK = 128
RET_ANGLE_BASE = 10000.0
N_EVEN = (DEPTH + 1) // 2
N_ODD = DEPTH // 2
N_MOD = 9
DEEPNORM_ALPHA = (2.0 * DEPTH) ** 0.25
DEEPNORM_BETA = (8.0 * DEPTH) ** -0.25
LN_EPS = 1e-5
GN_EPS = 1e-6

kernel_name = "fox_retnet_shortconv_macaron_deepnorm_adaln_step"

def _layernorm(x, g, b):
    xf = x.astype(jnp.float32)
    mu = jnp.mean(xf, axis=-1, keepdims=True)
    var = jnp.mean(jnp.square(xf - mu), axis=-1, keepdims=True)
    return ((xf - mu) * lax.rsqrt(var + LN_EPS) * g + b).astype(x.dtype)

def _head_norm(o):
    of = o.astype(jnp.float32)
    mu = jnp.mean(of, axis=-1, keepdims=True)
    var = jnp.mean(jnp.square(of - mu), axis=-1, keepdims=True)
    return (of - mu) * lax.rsqrt(var + GN_EPS)

def _swiglu(h, w_in, w_out):
    a, b = jnp.split(h @ w_in, 2, axis=-1)
    return (jax.nn.silu(a) * b) @ w_out

def _rotary(x, pos):
    half = x.shape[-1] // 2
    inv = 1.0 / (RET_ANGLE_BASE ** jnp.linspace(0.0, 1.0, half, dtype=jnp.float32))
    ang = pos.astype(jnp.float32)[:, None] * inv[None, :]
    cos = jnp.cos(ang)[None, :, None, :]
    sin = jnp.sin(ang)[None, :, None, :]
    x1 = x[..., :half].astype(jnp.float32)
    x2 = x[..., half:].astype(jnp.float32)
    return jnp.concatenate([x1 * cos - x2 * sin, x1 * sin + x2 * cos], axis=-1).astype(x.dtype)

def _fox_attend(q, cq, qpos, k, ck, kpos, v):
    s = jnp.einsum('bqhd,bkhd->bhqk', q, k).astype(jnp.float32) * (HEAD_DIM ** -0.5)
    s = s + (jnp.transpose(cq, (0, 2, 1))[:, :, :, None] - jnp.transpose(ck, (0, 2, 1))[:, :, None, :])
    mask = kpos[None, :] <= qpos[:, None]
    s = jnp.where(mask[None, None], s, -jnp.inf)
    p = jax.nn.softmax(s, axis=-1)
    return jnp.einsum('bhqk,bkhd->bqhd', p.astype(v.dtype), v)

def _fox_prompt(q, k, v, logf):
    B, T, H, d = q.shape
    c = jnp.cumsum(logf.astype(jnp.float32), axis=1)
    nb = T // Q_BLOCK
    qb = q.reshape(B, nb, Q_BLOCK, H, d).transpose(1, 0, 2, 3, 4)
    cb = c.reshape(B, nb, Q_BLOCK, H).transpose(1, 0, 2, 3)
    pb = jnp.arange(T, dtype=jnp.int32).reshape(nb, Q_BLOCK)
    kpos = jnp.arange(T, dtype=jnp.int32)
    out = lax.map(lambda a: _fox_attend(a[0], a[1], a[2], k, c, kpos, v), (qb, cb, pb))
    return out.transpose(1, 0, 2, 3, 4).reshape(B, T, H, d)

def _fox_sample(q, k, v, logf, k_past, v_past, logf_past):
    P = k_past.shape[1]
    L = q.shape[1]
    k_all = jnp.concatenate([k_past.astype(k.dtype), k], axis=1)
    v_all = jnp.concatenate([v_past.astype(v.dtype), v], axis=1)
    c_all = jnp.cumsum(jnp.concatenate([logf_past.astype(jnp.float32), logf.astype(jnp.float32)], axis=1), axis=1)
    qpos = P + jnp.arange(L, dtype=jnp.int32)
    kpos = jnp.arange(P + L, dtype=jnp.int32)
    return _fox_attend(q, c_all[:, P:], qpos, k_all, c_all, kpos, v_all)

def _ret_log_decay():
    return jnp.log(1.0 - 2.0 ** (-5.0 - jnp.arange(N_RET_HEADS, dtype=jnp.float32)))

def _ret_chunk(S, q, k, v, lg):
    L = q.shape[1]
    i = jnp.arange(L, dtype=jnp.float32)
    diff = i[:, None] - i[None, :]
    dmask = jnp.where(diff[None] >= 0, jnp.exp(jnp.maximum(diff, 0.0)[None] * lg[:, None, None]), 0.0)
    qf = q.astype(jnp.float32)
    kf = k.astype(jnp.float32)
    vf = v.astype(jnp.float32)
    qk = jnp.einsum('bihd,bjhd->bhij', qf, kf) * dmask[None]
    inner = jnp.einsum('bhij,bjhe->bihe', qk, vf)
    cross = jnp.einsum('bihd,bhde->bihe', qf, S) * jnp.exp((i + 1.0)[:, None] * lg[None, :])[None, :, :, None]
    kd = kf * jnp.exp((L - 1.0 - i)[:, None] * lg[None, :])[None, :, :, None]
    S_new = jnp.exp(L * lg)[None, :, None, None] * S + jnp.einsum('bjhd,bjhe->bhde', kd, vf)
    return S_new, inner + cross

def _ret_scan(q, k, v, S0):
    B, T, H, _ = q.shape
    lg = _ret_log_decay()
    S0 = S0.astype(jnp.float32)
    if T % RET_CHUNK != 0:
        return _ret_chunk(S0, q, k, v, lg)
    n = T // RET_CHUNK

    def to_chunks(a):
        return a.reshape(B, n, RET_CHUNK, H, a.shape[-1]).swapaxes(0, 1)

    S, o = lax.scan(lambda s, a: _ret_chunk(s, a[0], a[1], a[2], lg), S0, (to_chunks(q), to_chunks(k), to_chunks(v)))
    return S, o.swapaxes(0, 1).reshape(B, T, H, -1)

def _even_mixer(h, pos, w_in, b_f, w_out, fox_past, S0):
    B, T, _ = h.shape
    F, R, Hf = FOX_WIDTH, RET_WIDTH, N_FOX_HEADS
    split_at = [F, 2 * F, 3 * F, 3 * F + Hf, 3 * F + Hf + R, 3 * F + Hf + 2 * R, 3 * F + Hf + 3 * R]
    qf, kf, vf, fg, qr, kr, vr, gr = jnp.split(h @ w_in, split_at, axis=-1)

    def heads(a):
        return a.reshape(B, T, -1, HEAD_DIM)

    qf, kf, vf = heads(qf), heads(kf), heads(vf)
    logf = jax.nn.log_sigmoid((fg + b_f).astype(jnp.float32))
    if fox_past is None:
        of = _fox_prompt(qf, kf, vf, logf)
    else:
        of = _fox_sample(qf, kf, vf, logf, fox_past[0], fox_past[1], fox_past[2])
    qr = _rotary(heads(qr), pos)
    kr = _rotary(heads(kr), pos) * (HEAD_DIM ** -0.5)
    S, orr = _ret_scan(qr, kr, heads(vr), S0)
    yr = jax.nn.silu(gr) * _head_norm(orr).reshape(B, T, R).astype(h.dtype)
    y = jnp.concatenate([of.reshape(B, T, F).astype(h.dtype), yr], axis=-1) @ w_out
    return y, kf, vf, logf, S

def _odd_mixer(h, w_in, conv_w, w_out, buf):
    T = h.shape[1]
    b_gate, c_gate, u = jnp.split(h @ w_in, 3, axis=-1)
    u = c_gate * u
    up = jnp.concatenate([buf.astype(u.dtype), u], axis=1)
    z = conv_w[0] * up[:, 0:T]
    for j in range(1, CONV_WIDTH):
        z = z + conv_w[j] * up[:, j:j + T]
    y = (b_gate * z) @ w_out
    return y, up[:, -(CONV_WIDTH - 1):]

def _trunk(x, c, pos, fox_cache, ret_state, conv_state, page_table, w_ada, b_ada, w_ffn_in, w_ffn_out,
           ln_g, ln_b, w_in_even, b_forget, w_out_even, w_in_odd, conv_w, w_out_odd):
    B = x.shape[0]
    ks, vs, lfs, Ss, convs = [], [], [], [], []
    for l in range(DEPTH):
        mods = (jax.nn.silu(c) @ w_ada[l] + b_ada[l]).reshape(B, 1, N_MOD, D_MODEL)
        sh, sc, g = mods[:, :, 0], mods[:, :, 1], mods[:, :, 2]
        f = _swiglu(x * (1.0 + sc) + sh, w_ffn_in[l, 0], w_ffn_out[l, 0])
        x = _layernorm(DEEPNORM_ALPHA * x + 0.5 * g * f, ln_g[l, 0], ln_b[l, 0])
        sh, sc, g = mods[:, :, 3], mods[:, :, 4], mods[:, :, 5]
        h = x * (1.0 + sc) + sh
        if l % 2 == 0:
            e = l // 2
            if fox_cache is None:
                fox_past = None
                s0 = jnp.zeros((B, N_RET_HEADS, HEAD_DIM, HEAD_DIM), jnp.float32)
            else:
                k_pool, v_pool, lf_pool = fox_cache
                fox_past = (k_pool[e][page_table].reshape(B, -1, N_FOX_HEADS, HEAD_DIM),
                            v_pool[e][page_table].reshape(B, -1, N_FOX_HEADS, HEAD_DIM),
                            lf_pool[e][page_table].reshape(B, -1, N_FOX_HEADS))
                s0 = ret_state[e]
            y, kn, vn, lfn, Sn = _even_mixer(h, pos, w_in_even[e], b_forget[e], w_out_even[e], fox_past, s0)
            ks.append(kn)
            vs.append(vn)
            lfs.append(lfn)
            Ss.append(Sn)
        else:
            o = l // 2
            buf = jnp.zeros((B, CONV_WIDTH - 1, D_MODEL), x.dtype) if conv_state is None else conv_state[o]
            y, nbuf = _odd_mixer(h, w_in_odd[o], conv_w[o], w_out_odd[o], buf)
            convs.append(nbuf)
        x = _layernorm(DEEPNORM_ALPHA * x + g * y, ln_g[l, 1], ln_b[l, 1])
        sh, sc, g = mods[:, :, 6], mods[:, :, 7], mods[:, :, 8]
        f = _swiglu(x * (1.0 + sc) + sh, w_ffn_in[l, 1], w_ffn_out[l, 1])
        x = _layernorm(DEEPNORM_ALPHA * x + 0.5 * g * f, ln_g[l, 2], ln_b[l, 2])
    return x, jnp.stack(ks), jnp.stack(vs), jnp.stack(lfs), jnp.stack(Ss), jnp.stack(convs)

def setup_inputs(seed: int = 0) -> dict:
    key = jax.random.key(seed)
    k = jax.random.split(key, 24)

    def nrm(kk, shape, scale):
        return jax.random.normal(kk, shape, jnp.float32) * scale

    n_pages = PAST_LEN // PAGE_SIZE
    used = DEC_BATCH * n_pages
    n_phys = used + max(1, used // 4)
    page_table = jax.random.permutation(k[0], n_phys)[:used].reshape(DEC_BATCH, n_pages).astype(jnp.int32)
    d = D_MODEL
    return {
        "x_prompt": nrm(k[1], (BATCH, SEQ, d), 1.0),
        "x_sample": nrm(k[2], (DEC_BATCH, DEC_SEQ, d), 1.0),
        "cache_k": nrm(k[3], (N_EVEN, n_phys, PAGE_SIZE, N_FOX_HEADS, HEAD_DIM), 1.0),
        "cache_v": nrm(k[4], (N_EVEN, n_phys, PAGE_SIZE, N_FOX_HEADS, HEAD_DIM), 1.0),
        "cache_logf": jax.nn.log_sigmoid(3.0 + nrm(k[5], (N_EVEN, n_phys, PAGE_SIZE, N_FOX_HEADS), 1.0)),
        "state_ret": nrm(k[6], (N_EVEN, DEC_BATCH, N_RET_HEADS, HEAD_DIM, HEAD_DIM), 0.5),
        "state_conv": nrm(k[7], (N_ODD, DEC_BATCH, CONV_WIDTH - 1, d), 1.0),
        "page_table": page_table,
        "c_prompt": nrm(k[8], (BATCH, d), 1.0),
        "c_sample": nrm(k[9], (DEC_BATCH, d), 1.0),
        "w_ada": nrm(k[10], (DEPTH, d, N_MOD * d), 0.5 * d ** -0.5),
        "b_ada": nrm(k[11], (DEPTH, N_MOD * d), 0.01),
        "w_ffn_in": nrm(k[12], (DEPTH, 2, d, 2 * D_FF), d ** -0.5),
        "w_ffn_out": nrm(k[13], (DEPTH, 2, D_FF, d), DEEPNORM_BETA * D_FF ** -0.5),
        "ln_g": 1.0 + nrm(k[14], (DEPTH, 3, d), 0.01),
        "ln_b": nrm(k[15], (DEPTH, 3, d), 0.01),
        "w_in_even": nrm(k[16], (N_EVEN, d, EVEN_IN), d ** -0.5),
        "b_forget": 3.0 + nrm(k[17], (N_EVEN, N_FOX_HEADS), 0.5),
        "w_out_even": nrm(k[18], (N_EVEN, d, d), DEEPNORM_BETA * d ** -0.5),
        "w_in_odd": nrm(k[19], (N_ODD, d, 3 * d), d ** -0.5),
        "conv_w": nrm(k[20], (N_ODD, CONV_WIDTH, d), CONV_WIDTH ** -0.5),
        "w_out_odd": nrm(k[21], (N_ODD, d, d), DEEPNORM_BETA * d ** -0.5),
    }

def reference(x_prompt, x_sample, cache_k, cache_v, cache_logf, state_ret, state_conv, page_table,
              c_prompt, c_sample, w_ada, b_ada, w_ffn_in, w_ffn_out, ln_g, ln_b,
              w_in_even, b_forget, w_out_even, w_in_odd, conv_w, w_out_odd):
    pos_prompt = jnp.arange(x_prompt.shape[1], dtype=jnp.int32)
    pos_sample = PAST_LEN + jnp.arange(x_sample.shape[1], dtype=jnp.int32)
    y_prompt, k_p, v_p, lf_p, ret_p, conv_p = _trunk(
        x_prompt, c_prompt, pos_prompt, None, None, None, None,
        w_ada, b_ada, w_ffn_in, w_ffn_out, ln_g, ln_b,
        w_in_even, b_forget, w_out_even, w_in_odd, conv_w, w_out_odd)
    y_sample, k_s, v_s, lf_s, ret_s, conv_s = _trunk(
        x_sample, c_sample, pos_sample, (cache_k, cache_v, cache_logf), state_ret, state_conv, page_table,
        w_ada, b_ada, w_ffn_in, w_ffn_out, ln_g, ln_b,
        w_in_even, b_forget, w_out_even, w_in_odd, conv_w, w_out_odd)
    return (y_prompt, y_sample, k_p, v_p, lf_p, ret_p, conv_p, k_s, v_s, lf_s, ret_s, conv_s)


_drawn_inputs = setup_inputs


def setup_inputs(seed=0):
    import zlib

    import numpy as np

    out = dict(_drawn_inputs(seed))
    spreads = {}
    factors = {'cache_k': 3.452, 'cache_logf': 23.76}
    for name, (base, spread) in spreads.items():
        noise = np.random.default_rng([zlib.crc32(name.encode()), seed]).standard_normal(out[name].shape)
        drawn = base * np.exp(spread * noise) if base else spread * noise
        out[name] = __import__('jax').numpy.asarray(drawn.astype(out[name].dtype))
    for name, factor in factors.items():
        out[name] = (out[name] * factor).astype(out[name].dtype)
    return out
```

```python
import concourse.bass as bass
from concourse import mybir
from contextlib import ExitStack
import numpy as np

D = 1024
KT = D // 128
SEQ = 512
NS = 8
HP, HS = SEQ // 2, NS // 2
HT = HP + HS
NTOK = SEQ + NS
DFF = 2816
FT = DFF // 128
FH = FT // 2
NSUB = 6
NMOD = 9
MT = 3 * KT
ALPHA = 4.0 ** 0.25
LN_EPS = 1e-5
GN_EPS = 1e-6
NH = 8
HD = 64
FOXW = NH * HD
PAGE = 128
NPG = 8
EVEN_IN = 3 * FOXW + NH + 4 * FOXW
QSCALE = HD ** -0.5
SQUARES_WITH = {4: (0, 1), 5: (2, 3), 6: (4, 5, 6), 7: (7,)}
LAG = 4
CENTRE = 1
NADA = 3
FFN = (0, 2, 3, 5)
EVEN, ODD = 1, 4
CH_IN = {0: 2 * FT, 1: 28, 2: 2 * FT, 3: 2 * FT, 4: 24, 5: 2 * FT}
CH_OUT = {0: 2 * KT, 1: KT, 2: 2 * KT, 3: 2 * KT, 4: KT, 5: 2 * KT}


def chunks_before(n, second=False):
    return sum(CH_IN[i] + CH_OUT[i] for i in range(n)) + (CH_IN[n] if second else 0)


def mod_steps_before(n):
    return 4 + 7 * (n - 1) if n else 0


def ffns_before(n):
    return sum(1 for i in FFN if i < n)


def host_tables():
    p = np.arange(128)
    f = np.float32
    ident = np.eye(128, dtype=f)
    ones = np.ones((128, 128), f)
    sel = np.zeros((128, 8, 128), f)
    for r in range(8):
        sel[r, r, :] = 1
    delta = np.zeros((128, 8, 8), f)
    for r in range(8):
        delta[r, r, :] = 1
    lg = np.log(f(1.0) - f(2.0) ** (f(-5.0) - np.arange(NH, dtype=f))).astype(f)
    gdec = np.zeros((128, 4), f)
    for m in range(4):
        gdec[:64, m] = np.exp(lg[2 * m])
        gdec[64:, m] = np.exp(lg[2 * m + 1])
    tail = np.zeros((128, 4, 8), f)
    for j in range(4):
        for h in range(8):
            tail[:, j, h] = np.exp((f(SEQ - 1.0) - (128 * j + p).astype(f)) * lg[h])
    bd = np.zeros((128, 128), f)
    bd[:64, :64] = bd[64:, 64:] = 1.0 / HD
    unit = np.zeros((128, 8, 8), f)
    unit[:, np.arange(8), np.arange(8)] = 1
    res = np.concatenate([ident, ones, ones / D, p[:, None].astype(f), gdec, tail.reshape(128, 32),
                          delta.reshape(128, 64), sel.reshape(128, 1024), bd, unit.reshape(128, 64)], axis=1)
    tri = np.zeros((128, 896), f)
    tri[np.arange(896)[None, :] - 384 >= p[:, None]] = 1
    strict = (p[:, None] > p[None, :]).astype(f)
    causal = np.where(p[None, :] <= p[:, None], f(0), f(-1e30)).astype(f)
    perm = np.zeros((128, 128), f)
    for d in range(128):
        perm[d, (d + 32) % 64 + 64 * (d // 64)] = 1
    inv = (f(1.0) / (f(10000.0) ** np.linspace(0.0, 1.0, 32, dtype=f))).astype(f)
    pos = np.concatenate([np.arange(SEQ), np.full(NS, NPG * PAGE)]).astype(f)
    ang = (pos[:, None] * inv[None, :]).astype(f).T
    cos = np.tile(np.cos(ang), (4, 1)).astype(f)
    sin = np.concatenate([-np.sin(ang), np.sin(ang)] * 2, axis=0).astype(f)
    even = np.concatenate([tri, strict, causal, perm, cos, sin], axis=1)
    decay = np.zeros((NH, 128, SEQ), f)
    diff = np.arange(SEQ)[None, :] - p[:, None]
    for h in range(NH):
        decay[h] = np.where(diff >= 0, np.exp(np.maximum(diff, 0).astype(f) * lg[h]), f(0))
    return res.astype(f), even.astype(f), decay


def build_step(nc, a, out, last=NSUB):
    F32 = mybir.dt.float32
    F32R = mybir.dt.float32r
    I32 = mybir.dt.int32
    ALU = mybir.AluOpType
    ACT = mybir.ActivationFunctionType
    AX = mybir.AxisListType.X
    n_phys = a["cache_k"].shape[1]

    ctx = ExitStack()
    with ctx:
        top = [(nc.sbuf_base + 31) // 32 * 32]

        def region(size):
            at = top[0]
            top[0] += (size + 31) // 32 * 32
            assert top[0] <= nc.sbuf_usable_end, (top[0], nc.sbuf_usable_end)
            return at

        def put(name, shape, dt, at):
            return nc.alloc_sbuf_tensor_at(name, shape, dt, offset=at)

        def new(name, shape, dt=F32):
            size = 4
            for s in shape[1:]:
                size *= s
            return put(name, shape, dt, region(size))

        def sem(name):
            return ctx.enter_context(nc.semaphore(name))

        x = new("x", [128, KT, 2, HT])
        R_H = region(2 * 4 * KT * NTOK)
        h_hi = put("h_hi", [128, KT, 2, HT], F32R, R_H)
        h_lo = put("h_lo", [128, KT, 2, HT], F32R, R_H + 4 * KT * NTOK)
        R_HID = region(2 * 4 * FT * NTOK)
        hid_hi = put("hid_hi", [128, FT, 2, HT], F32R, R_HID)
        hid_lo = put("hid_lo", [128, FT, 2, HT], F32R, R_HID + 4 * FT * NTOK)
        raw = new("raw", [128, 2, FH, 128])
        w_hi = new("w_hi", [128, 2, FH, 128], F32R)
        w_lo = new("w_lo", [128, 2, FH, 128], F32R)
        R_ADA = region(4 * 4096)
        ada_w = put("ada_w", [128, NADA, KT, 128], F32, R_ADA)
        R_TMP = region(5 * 4 * NTOK)
        ada_rows = put("ada_rows", [9, 4, 512], F32, R_TMP)
        x_rows = put("x_rows", [128, 4, D], F32, R_H)
        p_rows = put("p_rows", [128, 4, 128], F32, R_H + 16384)
        s_rows = put("s_rows", [NS, D], F32, R_H + 16384 + 2048)
        ada_first = put("ada_first", [128, 4, KT, 512], F32, R_HID + 4 * KT * NTOK)
        ada_fifth = put("ada_fifth", [128, KT, 512], F32, R_ADA)
        h32 = put("h32", [128, KT, 2, HT], F32, R_HID)
        y_rows = put("y_rows", [128, 4, D], F32, R_HID)
        ys_rows = put("ys_rows", [NS, D], F32, R_HID + 16384)
        silu_a = put("silu_a", [128, 2, 2, HT], F32, R_TMP)
        gated = put("gated", [128, 2, 2, HT], F32, R_TMP + 8 * NTOK)
        tile_sum = put("tile_sum", [128, 2, HT], F32, R_TMP)
        mean = put("mean", [128, 2, HT], F32, R_TMP)
        shift = put("shift", [128, 2, HT], F32, R_TMP + 4 * NTOK)
        sq_sum = put("sq_sum", [128, 2, HT], F32, R_TMP + 8 * NTOK)
        rdev = put("rdev", [128, 2, HT], F32, R_TMP + 8 * NTOK)
        sq = put("sq", [128, 2, 2, HT], F32, R_TMP + 12 * NTOK)
        dev = sq[:, 0]

        res = new("res", [128, 1701])
        ident, ones, mean_w = res[:, 0:128], res[:, 128:256], res[:, 256:384]
        lane, gdec = res[:, 384:385], res[:, 385:389]
        tail = res[:, 389:421].rearrange("p (j h) -> p j h", j=4)
        delta = res[0:8, 421:485].rearrange("p (b h) -> p b h", b=8)
        sel = res[0:8, 485:1509].rearrange("p (r c) -> p r c", r=8)
        head_mean = res[:, 1509:1637]
        unit = res[0:8, 1637:1701].rearrange("p (b c) -> p b c", b=8)
        params = new("params", [128, 4 * 128])
        c_t = new("c_t", [128, KT, 9])
        c_act = new("c_act", [128, KT, 9])
        mod = new("mod", [128, 2, MT, 9])
        mod_b = new("mod_b", [128, KT, 9])
        samp8 = new("samp8", [128, 8])
        samp_t = new("samp_t", [128, KT, 8])
        eps_ln = new("eps_ln", [128, 1])
        LN_G, LN_B, CONV_W, C_AT = 144, 192, 256, 280

        QF, KF, VF, QR, KR, VR, GR = range(0, 28, 4)
        proj = put("proj", [128, 28, NTOK], F32, R_HID)
        R_TOK = R_HID + 28 * 4 * NTOK
        kf_tok, vf_tok, vr_tok, kr_tok = (put(t, [128, 4, FOXW], F32, R_TOK + 8192 * u)
                                          for u, t in enumerate(("kf_tok", "vf_tok", "vr_tok", "kr_tok")))
        q_all = put("q_all", [128, NS, FOXW], F32, R_TOK)
        logf_pool = put("logf_pool", [n_phys, PAGE, NH], F32, R_TOK + 16384)
        page_ids = put("page_ids", [n_phys, NS * NPG], I32, R_TOK + 20480)
        page_f = put("page_f", [n_phys, NS * NPG], F32, R_TOK + 20736)
        one_hot = put("one_hot", [n_phys, NS * NPG], F32, R_TOK + 20992)
        q_s = put("q_s", [NS, FOXW], F32, R_TOK + 24576)
        s_prod = put("s_prod", [NS, FOXW], F32, R_TMP + 8192)
        R_PT = R_H + 4 * 2320
        even_t = put("even_t", [128, 2320], F32, R_H)
        tri, strict, causal, perm = even_t[:, 0:896], even_t[:, 896:1024], even_t[:, 1024:1152], even_t[:, 1152:1280]
        cos_t, sin_t = even_t[:, 1280:1800], even_t[:, 1800:2320]
        own_parts = [put(t, [NH, n, FOXW], F32, at) for t, n, at in
                     (("own_a", 4, R_TOK + 24576), ("own_b", 2, R_H), ("own_c", 2, R_H + 4 * 1280))]
        own = [part[:, i, :] for part, n in zip(own_parts, (4, 2, 2)) for i in range(n)]
        k_s, v_s, vr_s = (put(t, [NS, FOXW], F32, R_PT + 2048 * u) for u, t in enumerate(("k_s", "v_s", "vr_s")))
        p_t = put("p_t", [128, 4, SEQ], F32, R_PT)
        kv_s = put("kv_s", [128, NS, 4, HD], F32, R_PT + 8192)
        probs = put("probs", [128, 2, 1280], F32, R_PT + 8192)
        ret_a1 = put("ret_a1", [128, 1280], F32, R_PT + 8192 + 10240)
        state = put("state", [128, NS, 4, HD], F32, R_TMP)
        ret_a0 = put("ret_a0", [128, 1280], F32, R_TMP)
        ret_a = (ret_a0, ret_a1)
        rot = put("rot", [128, 2, NTOK], F32, R_PT + 8192)
        hn_sq = put("hn_sq", [128, 2, NTOK], F32, R_TMP)
        hn_dev = put("hn_dev", [128, 2, NTOK], F32, R_TMP + 8 * NTOK)
        pages = put("pages", [128, 2, 4, FOXW], F32, R_ADA)
        decay = new("decay", [128, 2, SEQ])
        c_heads = new("c_heads", [NH, SEQ])
        s_samp = new("s_samp", [128, NS, NH, NPG])
        lf_past = new("lf_past", [128, NS, NH, NPG])
        page_row = new("page_row", [1, NS * NPG], I32)
        w_fg = new("w_fg", [128, KT, NH])
        fg_hi = new("fg_hi", [128, KT, NH], F32R)
        fg_lo = new("fg_lo", [128, KT, NH], F32R)
        fg_rows = put("fg_rows", [NH, NTOK], F32, R_TMP + 8192)
        b_fg = new("b_fg", [128, NH])
        logf = new("logf", [128, 5, NH])
        lf_a = new("lf_a", [128, 5, NH])
        lf_b = new("lf_b", [128, 5, NH])
        c_cols = new("c_cols", [128, 4, NH])
        n_max = new("n_max", [128, NH * 4])
        row_sum = new("row_sum", [128, NH * 4])
        ret_state = new("ret_state", [128, 4, HD])
        sm = {t: new("sm_" + t, [128, 64]) for t in ("new", "max", "den", "col")}
        eps_gn = new("eps_gn", [128, 1])
        PJ = (0, 128, 384, 768)
        AK = (0, 512, 896, 1152)
        mix_hi = put("mix_hi", [128, KT, 2, HT], F32R, R_HID)
        mix_lo = put("mix_lo", [128, KT, 2, HT], F32R, R_HID + 4 * KT * NTOK)
        R_ODD = R_HID + 8 * KT * NTOK
        cg = put("cg", [128, 2, HT], F32, R_ODD)
        up = put("up", [128, 2 + SEQ], F32, R_ODD + 2080)
        up_s = put("up_s", [128, NS], F32, R_ODD + 4160)
        z = put("z", [128, SEQ], F32, R_ODD + 4224)
        z_s = put("z_s", [128, NS], F32, R_ODD + 6272)
        mixed = put("mixed", [128, 2, 2, HT], F32, R_ODD + 6336)
        tail_s = put("tail_s", [128, NS, 2, KT], F32, R_ODD + 10496)
        tail_p = put("tail_p", [128, 2, KT], F32, R_ODD + 11008)
        tail_rows = put("tail_rows", [128, 2, 128], F32, R_ODD + 11072)

        ps = ctx.enter_context(nc.psum_tensor("ps", [128, 8, 512], F32))

        def pair(q):
            return ps[:, 2 * q:2 * q + 2, 0:HT]

        consts_in = sem("consts_in")
        rows_in = sem("rows_in")
        x_rows_in = sem("x_rows_in")
        eps_ready = sem("eps_ready")
        params_t = sem("params_t")
        params_ready = sem("params_ready")
        c_ready = sem("c_ready")
        cond_ready = sem("cond_ready")
        x_t = sem("x_t")
        x_copied = sem("x_copied")
        raw_full = [sem(f"raw_full{k}") for k in range(2)]
        hi_cut = sem("hi_cut")
        chunk_cut = sem("chunk_cut")
        chunk_used = sem("chunk_used")
        ada_full = [sem(f"ada_full{k}") for k in range(NADA)]
        ada_used = sem("ada_used")
        mod_steps = sem("mod_steps")
        silu_done = sem("silu_done")
        gate_done = sem("gate_done")
        hid_hi_done = sem("hid_hi_done")
        hid_lo_done = sem("hid_lo_done")
        drained = sem("drained")
        samp_added = sem("samp_added")
        summed = sem("summed")
        mean_done = sem("mean_done")
        half_summed = sem("half_summed")
        shift_ready = sem("shift_ready")
        shifted = sem("shifted")
        squared = sem("squared")
        sq_added = sem("sq_added")
        mean_ready = sem("mean_ready")
        delta_steps = sem("delta_steps")
        centred = [sem("centred_dve"), sem("centred_pool")]
        first_full = [sem(f"first_full{k}") for k in range(6)]
        var_done = sem("var_done")
        dev_done = sem("dev_done")
        rdev_done = sem("rdev_done")
        normed = sem("normed")
        ln_done = sem("ln_done")
        h32_done = sem("h32_done")
        h32_samp = sem("h32_samp")
        samp_mod = sem("samp_mod")
        samp_out = sem("samp_out")
        rows_made = sem("rows_made")
        rows_copied = sem("rows_copied")
        h_hi_done = sem("h_hi_done")
        h_lo_done = sem("h_lo_done")
        y_t = sem("y_t")
        y_copied = sem("y_copied")
        stored = sem("stored")
        named = {}

        def ev(name):
            if name not in named:
                named[name] = sem(name)
            return named[name]

        page_full = [sem(f"page_full{k}") for k in range(2)]
        for name in ("copied", "k_read", "v_used", "score_read", "scores_done", "bias_done", "max_done", "exp_done",
                     "p_ready", "pt_done", "pt_copied", "fox_av", "ret_av", "c_spread", "o_read", "decay_in0",
                     "decay_in1", "chained", "conv_steps", "cg_copied", "mixed_hi", "mixed_lo", "k_prod"):
            ev(name)
        block = ctx.enter_context(nc.Block())
        n_stored = [0]

        def store(eng, dst, src):
            eng.dma_start(dst, src).then_inc(stored, 16)
            n_stored[0] += 1

        def loop(eng, first, count, body):
            if first:
                body(0)
            with eng.Fori(1 if first else 0, count) as i:
                body(i)

        def is_first(i):
            return isinstance(i, int) and i == 0

        def mixed_tile(t):
            return proj[:, (VF + t) if t < 4 else (VR + t - 4)]

        products = [(n, second) for n in range(last) for second in (False, True)]

        def tiles_of_product(n, second):
            return FH if second and n in FFN else KT

        def next_tiles(n, second):
            k = products.index((n, second)) + 1
            return tiles_of_product(*products[k]) if k < len(products) else None

        def w_view(w):
            return w.rearrange("(t p) n -> p t n", p=128)

        ffn_in = {n: w_view(a["w_ffn_in"][n // 3, (n % 3) // 2]) for n in FFN}
        ffn_out = {n: w_view(a["w_ffn_out"][n // 3, (n % 3) // 2]) for n in FFN}

        even_in = w_view(a["w_in_even"][0])
        mixer_out = {EVEN: w_view(a["w_out_even"][0]), ODD: w_view(a["w_out_odd"][0])}
        odd_in = w_view(a["w_in_odd"][0])
        cache_k = a["cache_k"][0].rearrange("g s h d -> g s (h d)")
        cache_v = a["cache_v"][0].rearrange("g s h d -> g s (h d)")

        def ada_view(n):
            return w_view(a["w_ada"][n // 3])[:, :, (n % 3) * MT * 128:(n % 3 + 1) * MT * 128]

        def ada_used_before(n):
            return MT * n

        def first_ada(g):
            return ada_fifth[:, :, :] if g == 4 else ada_first[:, g % 5]

        def centre(eng, n, part):
            eng.wait_ge(mean_ready, n + 1)
            for t in range(*((0, CENTRE), (CENTRE, KT))[part]):
                eng.tensor_tensor(x[:, t], x[:, t], mean[:, :, :], ALU.subtract).then_inc(centred[part], 1)

        two = lambda v: v.rearrange("p (h c) -> p h c", h=2)

        def modulate_samples(pool, n):
            m = n % 2
            pool.wait_ge(mod_steps, mod_steps_before(n) + (5 if n else 2))
            if n == 0:
                pool.wait_ge(x_copied, KT + 1)
            for t in range(KT):
                if n:
                    pool.wait_ge(normed, KT * (n - 1) + t + 1)
                pool.tensor_tensor(two(samp_t[:, t]), x[:, t, :, HP:HT], two(mod[:, m, KT + t, 1:9]), ALU.mult
                                   ).then_inc(samp_mod, 1)
                pool.wait_ge(samp_mod, KT * n + t + 1)
                pool.tensor_tensor(h32[:, t, :, HP:HT], two(samp_t[:, t]), two(mod[:, m, t, 1:9]), ALU.add
                                   ).then_inc(h32_samp, 1)

        @block.sync
        def _(sp):
            def chunk(c, k, src, kt):
                if not (isinstance(c, int) and c < 2):
                    sp.wait_ge(chunk_cut, c - 1)
                sp.dma_start(raw[:, k, 0:kt, :], src).then_inc(raw_full[k], 16)

            def ada(n, q, slot):
                c = ada_used_before(n) + q
                sp.wait_ge(ada_used, c - NADA + 1)
                sp.dma_start(ada_w[:, slot, :, :], ada_view(n)[:, :, bass.ds(q * 128, 128)]).then_inc(ada_full[slot], 16)

            def even_loads(chunk):
                c0 = chunks_before(EVEN)
                for k in range(2):
                    chunk(c0 + k, k, even_in[:, :, k * 128:(k + 1) * 128], KT)
                sp.dma_start(w_fg[:, :, :], even_in[:, :, 3 * FOXW:3 * FOXW + NH]).then_inc(ev("fg_in"), 16)
                sp.dma_start(b_fg[:, :], a["b_forget"][0].partition_broadcast(128)).then_inc(ev("fg_in"), 16)
                def columns(i, m0):
                    for k in range(2):
                        m = i * 2 + k
                        chunk(c0 + m, k, even_in[:, :, bass.ds(m * 128 + (NH if m0 >= 12 else 0), 128)], KT)

                def granule(cache, b, k):
                    for u in range(4):
                        page = sp.value_load(page_row[0:1, bass.ds(b * NPG + 4 * k + u, 1)], min_val=0, max_val=n_phys - 1)
                        sp.dma_start(pages[:, k, u, :], cache[bass.ds(page, 1)].rearrange("g s c -> s (g c)")
                                     ).then_inc(page_full[k], 16)

                columns(1, 0)
                sp.wait_ge(h32_done, KT * 2)
                sp.wait_ge(h_lo_done, KT * 2)
                sp.dma_start(page_row[:, :], a["page_table"].rearrange("b g -> (b g)").unsqueeze(0)).then_inc(ev("ids_in"), 16)
                sp.dma_start(page_ids[:, :], a["page_table"].rearrange("b g -> (b g)").partition_broadcast(n_phys)).then_inc(ev("gather_in"), 16)
                sp.dma_start(logf_pool[:, :, :], a["cache_logf"][0]).then_inc(ev("pool_in"), 16)
                sp.wait_ge(ev("ids_in"), 16)
                sp.wait_ge(ada_used, MT * 2)
                for k in range(2):
                    granule(cache_k, 0, k)
                columns(2, 0)
                for i0, i1, m0 in ((3, 6, 0), (6, 10, 12)):
                    with sp.Fori(i0, i1) as i:
                        columns(i, m0)
                        for k in range(2):
                            sp.wait_ge(ev("k_read"), i * 2 + k - 5)
                            granule(cache_k, i - 2, k)
                with sp.Fori(10, 14) as i:
                    columns(i, 12)
                sp.wait_ge(chunk_used, c0 + 28)
                sp.wait_ge(ev("fg_done"), 1)
                sp.dma_start(even_t[:, :], a["t_even"]).then_inc(ev("tables_in"), 16)
                st = a["state_ret"][0].rearrange("b (m t) d e -> t d b m e", t=2)
                for t in range(2):
                    sp.dma_start(state[64 * t:64 * t + 64], st[t]).then_inc(ev("state_in"), 16)
                for h in range(2):
                    sp.dma_start(decay[:, h, :], a["t_decay"][h]).then_inc(ev(f"decay_in{h}"), 16)
                for k in range(2):
                    sp.wait_ge(ev("k_read"), 15 + k)
                    granule(cache_v, 0, k)
                sp.wait_ge(ev("tok_copied"), 15)
                for name, rows in (("k_prompt", kf_tok), ("v_prompt", vf_tok)):
                    sp.dma_start(out[name][0, 0].rearrange("(j p) h d -> p j (h d)", p=128), rows[:, :, :]
                                 ).then_inc(ev("kv_stored"), 16)
                for name, rows in (("k_sample", k_s), ("v_sample", v_s)):
                    sp.dma_start(out[name][0, :, 0].rearrange("b h d -> b (h d)"), rows[:, :]
                                 ).then_inc(ev("rows_stored"), 16)
                sp.wait_ge(ev("logf_ready"), 2)
                store(sp, out["logf_prompt"][0, 0].rearrange("(j p) h -> p j h", p=128), logf[:, 0:4, :])
                store(sp, out["logf_sample"][0, :, 0], logf[0:NS, 4, :])
                sp.wait_ge(ev("kv_added"), 1)
                sn = out["ret_sample"][0].rearrange("b (m t) d e -> t d b m e", t=2)
                for t in range(2):
                    sp.dma_start(sn[t], state[64 * t:64 * t + 64]).then_inc(ev("state_stored"), 16)
                for h in range(1, NH):
                    if h >= 2:
                        sp.wait_ge(ev("score_read"), 8 * (h - 1))
                        sp.dma_start(decay[:, h % 2, :], a["t_decay"][h]).then_inc(ev(f"decay_in{h % 2}"), 16)
                    for k in range(2):
                        sp.wait_ge(ev("v_used"), 2 * h + k - 1)
                        granule(cache_v, h, k)
                sp.wait_ge(ev("ret_state_ready"), 2)
                rp = out["ret_prompt"][0, 0].rearrange("(m t) d e -> t d m e", t=2)
                for t in range(2):
                    store(sp, rp[t], ret_state[64 * t:64 * t + 64])

            sp.dma_start(res[:, :], a["t_res"]).then_inc(consts_in, 16)
            b_rows = a["b_ada"].rearrange("l (r c) -> (l r) c", c=128)
            parts = [(0, 0, b_rows[0:128]), (1, 0, b_rows[128:144]),
                     (1, 16, a["ln_g"].rearrange("l s (r c) -> (l s r) c", c=128)),
                     (1, 64, a["ln_b"].rearrange("l s (r c) -> (l s r) c", c=128)),
                     (2, 0, a["conv_w"].rearrange("o j (r c) -> (o j r) c", c=128)),
                     (2, 24, a["c_prompt"].rearrange("b (r c) -> (b r) c", c=128)),
                     (2, 32, a["c_sample"].rearrange("b (r c) -> (b r) c", c=128)),
                     (3, 0, a["state_conv"].rearrange("o b j (r c) -> (o b j r) c", c=128))]
            for k, r, src in parts:
                sp.dma_start(p_rows[r:r + src.shape[0], k, :], src).then_inc(rows_in, 16)
            def first(g):
                sp.dma_start(first_ada(g), ada_view(0)[:, :, g * 512:(g + 1) * 512]).then_inc(first_full[g], 16)

            for g in range(2):
                first(g)
            sp.dma_start(x_rows[:, :, :], a["x_prompt"][0].rearrange("(j p) n -> p j n", p=128)).then_inc(x_rows_in, 16)
            sp.dma_start(s_rows[:, :], a["x_sample"][:, 0, :]).then_inc(x_rows_in, 16)
            for g in range(2, 4):
                first(g)
            for k in range(2):
                chunk(k, k, ffn_in[0][:, :, k * DFF:k * DFF + 128], KT)
            first(4)
            sp.wait_ge(rows_made, 1)
            first(5)
            for n in range(last):
                if n in FFN:
                    def body(i):
                        for k in range(2):
                            chunk(chunks_before(n) + i * 2 + k, k, ffn_in[n][:, :, bass.ds(i * 128 + k * DFF, 128)], KT)
                    with sp.Fori(1 if n == 0 else 0, FT) as i:
                        body(i)

                    def body(i):
                        for j in range(2):
                            for k in range(2):
                                m = i * 2 + j
                                chunk(chunks_before(n, True) + i * 4 + 2 * j + k, k,
                                      ffn_out[n][:, k * FH:(k + 1) * FH, bass.ds(m * 128, 128)], FH)
                                if n + 1 < last:
                                    for q in ((0, 1), (2,), (3, 4), (5,))[2 * j + k]:
                                        ada(n + 1, i * 6 + q, q % NADA)
                    loop(sp, False, KT // 2, body)
                    continue
                if n == EVEN:
                    even_loads(chunk)
                else:
                    def body(i):
                        for j in range(2):
                            for k in range(3):
                                q = 3 * j + k
                                chunk(chunks_before(n) + i * 6 + q, q % 2,
                                      odd_in[:, :, bass.ds(i * 256 + (j * 128 + k * D), 128)], KT)
                    loop(sp, False, KT // 2, body)

                if n == EVEN:
                    sp.wait_ge(ev("v_used"), 2 * NS)

                def body(i):
                    for k in range(2):
                        chunk(chunks_before(n, True) + i * 2 + k, k, mixer_out[n][:, :, bass.ds((i * 2 + k) * 128, 128)], KT)
                        if n + 1 < last:
                            for q in range(3):
                                ada(n + 1, i * 6 + 3 * k + q, q)
                loop(sp, False, KT // 2, body)
                if n == ODD:
                    sp.wait_ge(ev("tail_rows_ready"), 2)
                    for name, rows in (("conv_sample", tail_rows[:, 0, :]), ("conv_prompt", tail_rows[0:2 * KT, 1, :])):
                        sp.dma_start(out[name].rearrange("o b j (r c) -> (o b j r) c", c=128), rows
                                     ).then_inc(ev("tails_stored"), 16)

            sp.wait_ge(y_copied, 9)
            for j in range(4):
                store(sp, out["y_prompt"][0, j * 128:(j + 1) * 128, :], y_rows[:, j, :])
            store(sp, out["y_sample"][:, 0, :], ys_rows[:, :])
            sp.wait_ge(stored, 16 * n_stored[0])
            if last > EVEN:
                sp.wait_ge(ev("kv_stored"), 32)
                sp.wait_ge(ev("rows_stored"), 32)
                sp.wait_ge(ev("state_stored"), 32)
            if last > ODD:
                sp.wait_ge(ev("tails_stored"), 32)

        @block.gpsimd
        def _(pool):
            pool.memset(eps_ln[:, :], LN_EPS / ALPHA ** 2).then_inc(eps_ready, 1)
            pool.memset(eps_gn[:, :], GN_EPS).then_inc(eps_ready, 1)

            def cut(c, k, kt):
                pool.wait_ge(hi_cut, c + 1)
                pool.tensor_tensor(w_lo[:, k, 0:kt, :], raw[:, k, 0:kt, :], w_hi[:, k, 0:kt, :].bitcast(F32),
                                   ALU.subtract).then_inc(chunk_cut, 1)

            for n in range(last):
                for second in (False, True):
                    kt = tiles_of_product(n, second)
                    count = (CH_OUT if second else CH_IN)[n]

                    def body(i):
                        for k in range(2):
                            cut(chunks_before(n, second) + i * 2 + k, k, kt)
                    if second:
                        loop(pool, False, count // 2, body)
                    else:
                        body(0)
                        if n:
                            centre(pool, n - 1, 1)
                        modulate_samples(pool, n)
                        with pool.Fori(1, count // 2) as i:
                            body(i)
            centre(pool, last - 1, 1)

        @block.tensor
        def _(pe):
            def product(c, k, q, kt, hi, lo, kt0=0, start=True, stop=True):
                pe.wait_ge(chunk_cut, c + 1)
                for t in range(kt):
                    for step, (w, v) in enumerate(((w_hi, hi), (w_hi, lo), (w_lo, hi))):
                        for half in range(2):
                            mm = pe.matmul(ps[:, 2 * q + half, 0:HT], w[:, k, t, :], v[:, kt0 + t, half, :],
                                           start=start and t == 0 and step == 0,
                                           stop=stop and t == kt - 1 and step == 2)
                mm.then_inc(chunk_used, 1)

            def ada_tile(q, w, bank=6):
                for t in range(KT):
                    mm = pe.matmul(ps[:, bank, bass.ds(q * 9, 9)], w[:, t, :], c_act[:, t, :], start=t == 0, stop=t == KT - 1)
                mm.then_inc(ada_used, 1)

            def ada(n, q, slot):
                pe.wait_ge(ada_full[slot], (n - 1) * MT // NADA * 16 + 16 + (q - slot) // NADA * 16)
                ada_tile(q, ada_w[:, slot])

            def first_products(n, q0, q1):
                c = chunks_before(n)
                pe.wait_ge(chunk_cut, c + 2)
                for u in range(KT + LAG):
                    for k, t, q in ((0, u, q0), (1, u - LAG, q1)):
                        if not 0 <= t < KT:
                            continue
                        if k == 0:
                            pe.wait_ge(h_lo_done, KT * n + t + 1)
                        for step, (w, v) in enumerate(((w_hi, h_hi), (w_hi, h_lo), (w_lo, h_hi))):
                            for half in range(2):
                                mm = pe.matmul(ps[:, 2 * q + half, 0:HT], w[:, k, t, :], v[:, t, half, :],
                                               start=t == 0 and step == 0, stop=t == KT - 1 and step == 2)
                        if t == KT - 1:
                            mm.then_inc(chunk_used, 1)
                        if n == 0 and k == 0:
                            first_rows(4 + t // 4, range(t % 4 * 2, t % 4 * 2 + 2))

            pe.wait_ge(consts_in, 16)
            pe.wait_ge(rows_in, 16 * 8)
            for k, r in ((0, 128), (1, 112), (2, 96), (3, 128)):
                mm = pe.transpose(ps[:, 0, k * 128:k * 128 + r], p_rows[0:r, k, :], ident[0:r, 0:r])
            mm.then_inc(params_t, 1)
            def first_rows(g, tiles):
                pe.wait_ge(first_full[g], 16)
                for t in tiles:
                    mm = pe.matmul(ps[0:9, (0, 1, 0, 1, 4, 5)[g], :], c_act[:, t, :], first_ada(g)[:, t, :],
                                   start=t == 0, stop=t == KT - 1)
                if t == KT - 1:
                    mm.then_inc(rows_made, 1)

            def first_turned(g):
                pe.wait_ge(rows_copied, g + 1)
                for q in range(4 * g, 4 * g + 4):
                    pe.transpose(ps[:, 6 if g < 4 else 7, q * 9:q * 9 + 9],
                                 ada_rows[:, g % 4, (q % 4) * 128:(q % 4) * 128 + 128], ident[0:9, 0:9]).then_inc(ada_used, 1)

            pe.wait_ge(cond_ready, 1)
            first_rows(0, range(KT))
            first_rows(1, range(KT))
            first_turned(0)
            first_turned(1)
            pe.wait_ge(x_rows_in, 32)
            for t in range(KT):
                if t >= 2:
                    pe.wait_ge(x_copied, t - 1)
                for j in range(4):
                    mm = pe.transpose(ps[:, 2 + t % 2, j * 128:(j + 1) * 128], x_rows[:, j, t * 128:(t + 1) * 128], ident)
                mm.then_inc(x_t, 1)
            for t in range(KT):
                mm = pe.transpose(ps[:, 4, t * 8:t * 8 + 8], s_rows[:, t * 128:(t + 1) * 128], ident[0:8, 0:8])
            mm.then_inc(x_t, 1)
            first_rows(2, range(KT))
            first_rows(3, range(KT))
            first_turned(2)
            first_turned(3)

            def shift_sums(n):
                pe.wait_ge(summed, (KT - 1) * n + KT // 2)
                for half in range(2):
                    mm = pe.matmul(ps[:, 4 + half, 0:HT], mean_w, tile_sum[:, half, :], start=True, stop=True)
                mm.then_inc(half_summed, 1)

            def norm_sums(n):
                pe.wait_ge(shift_ready, n + 1)
                pe.wait_ge(samp_added, KT * (n + 1))
                for half in range(2):
                    pe.matmul(ps[:, 4 + half, 0:HT], mean_w, tile_sum[:, half, :], start=True, stop=False)
                    mm = pe.matmul(ps[:, 4 + half, 0:HT], mean_w, x[:, KT - 1, half, :], start=False, stop=True)
                mm.then_inc(mean_done, 1)
                pe.wait_ge(sq_added, (KT - 2) * (n + 1))
                for half in range(2):
                    pe.matmul(ps[:, half, 0:HT], mean_w, sq_sum[:, half, :], start=True, stop=False)
                pe.wait_ge(squared, KT * (n + 1))
                for half in range(2):
                    mm = pe.matmul(ps[:, half, 0:HT], mean_w, sq[:, (KT - 1) % 2, half, :], start=False, stop=True)
                mm.then_inc(var_done, 1)

            def even_pe():
                c0 = chunks_before(EVEN)

                def body(i):
                    for k in range(2):
                        pe.wait_ge(ev("copied"), 2 * (i * 2 + k - 1))
                        product(c0 + i * 2 + k, k, k, KT, h_hi, h_lo)
                first_products(EVEN, 0, 1)
                body(1)
                pe.wait_ge(ev("pool_in"), 16)
                pe.wait_ge(ev("one_hot_ready"), 1)
                by_head = ps[:, 5, :].rearrange("p (b h g) -> p b h g", b=NS, h=NH)
                for h in range(NH):
                    mm = pe.matmul(by_head[:, :, h, :], logf_pool[:, :, h], one_hot[:, :], start=True, stop=True)
                mm.then_inc(ev("lf_gathered"), 1)
                pe.wait_ge(ev("copied"), 8)
                for m in range(4):
                    mm = pe.transpose(ps[0:NS, 4, m * 128:(m + 1) * 128], proj[:, QF + m, SEQ:NTOK], ident)
                mm.then_inc(ev("q_rows"), 1)
                pe.wait_ge(ev("fg_cut"), 2)
                for t in range(KT):
                    for step, (w, v) in enumerate(((fg_hi, h_hi), (fg_hi, h_lo), (fg_lo, h_hi))):
                        for half in range(2):
                            mm = pe.matmul(ps[0:NH, 6 + half, 0:HT], w[:, t, :], v[:, t, half, :],
                                           start=t == 0 and step == 0, stop=t == KT - 1 and step == 2)
                mm.then_inc(ev("fg_made"), 1)
                pe.wait_ge(ev("fg_copied"), 2)
                for j in range(5):
                    n = 128 if j < 4 else NS
                    mm = pe.transpose(ps[0:n, 7, j * NH:(j + 1) * NH], fg_rows[:, j * 128:j * 128 + n], ident[0:NH, 0:NH])
                mm.then_inc(ev("fg_done"), 1)
                pe.wait_ge(ev("q_s_ready"), 1)
                for b in range(NS):
                    if b >= 2:
                        pe.wait_ge(ev("q_spread_copied"), b - 1)
                    pe.matmul(ps[:, 4 + 2 * (b % 2), :], sel[:, b, :], q_s[:, :], start=True, stop=True
                              ).then_inc(ev("q_spread"), 1)
                with pe.Fori(2, 14) as i:
                    body(i)

                pe.wait_ge(ev("tables_in"), 16)
                pe.wait_ge(ev("logf_ready"), 2)
                pe.wait_ge(ev("q_spread_copied"), NS)
                for j in range(4):
                    for i in range(j + 1):
                        pe.matmul(ps[:, 5, j * NH:(j + 1) * NH], ones if i < j else tri[:, 384:512], logf[:, i, :],
                                  start=i == 0, stop=i == j)
                for i in range(4):
                    mm = pe.matmul(ps[0:NH, 6, :], logf[:, i, :], tri[:, 384 - 128 * i:896 - 128 * i], start=i == 0, stop=i == 3)
                mm.then_inc(ev("c_made"), 1)
                pe.wait_ge(ev("copied"), 2 * 28)
                for u in range(8):
                    if u >= 2:
                        pe.wait_ge(ev("rot_read"), u - 1)
                    for half in range(2):
                        mm = pe.matmul(ps[:, 2 * (u % 2) + half, 0:HT], perm, proj[:, QR + u, half * HT:(half + 1) * HT],
                                       start=True, stop=True)
                    mm.then_inc(ev("rot_made"), 1)
                pe.wait_ge(ev("rot_read"), 8)
                count = 0
                for tile in (KF, VF, VR, KR):
                    if tile == KR:
                        pe.wait_ge(ev("c_copied"), 2)
                        for u, first in enumerate((KF, VF, VR)):
                            for m in range(4):
                                mm = pe.transpose(ps[0:NS, 4 + u, m * 128:(m + 1) * 128], proj[:, first + m, SEQ:NTOK], ident)
                            mm.then_inc(ev("s_rows_t"), 1)
                        pe.wait_ge(ev("k_scaled"), 1)
                    for j in range(4):
                        if count >= 4:
                            pe.wait_ge(ev("tok_copied"), count - 3)
                        for m in range(4):
                            mm = pe.transpose(ps[:, count % 4, m * 128:(m + 1) * 128],
                                              proj[:, tile + m, j * 128:(j + 1) * 128], ident)
                        mm.then_inc(ev("tok_t"), 1)
                        count += 1
                pe.wait_ge(ev("kr_copied"), 4)
                pe.wait_ge(ev("fg_z"), 2)
                for m in range(4):
                    for j in range(4):
                        mm = pe.matmul(ps[:, 7, m * 128:(m + 1) * 128], kr_tok[:, j, m * 128:(m + 1) * 128],
                                       vr_tok[:, j, m * 128:(m + 1) * 128], start=j == 0, stop=j == 3)
                mm.then_inc(ev("ret_state_made"), 1)
                pe.wait_ge(ev("tok_copied"), 15)
                pe.wait_ge(ev("lfnd_ready"), 1)
                past = lf_past[:, :, :, :].rearrange("p b h g -> p (b h) g")
                after = ps[:, 6, :].rearrange("p (q g) -> p q g", g=NPG)
                pe.matmul(after, strict, past, start=True, stop=False)
                for i in range(1, NPG):
                    pe.matmul(after[:, :, 0:NPG - i], ones, past[:, :, i:NPG], start=False, stop=False)
                pe.matmul(after, ones[0:NS, :], sm["col"][0:NS, :].unsqueeze(2).to_broadcast([NS, 64, NPG]),
                          start=False, stop=True).then_inc(ev("after_made"), 1)
                pe.wait_ge(ev("s_new_rows"), 1)
                pe.matmul(ps[:, 5, 0:64], ones[0:NS, :], sm["max"][0:NS, :], start=True, stop=True).then_inc(ev("s_new_spread"), 1)
                for b in range(NS):
                    for t in range(2):
                        mm = pe.matmul(ps[64 * t:64 * t + 64, b // 2, (b % 2) * 256:(b % 2) * 256 + 256], sel[:, b, 0:64],
                                       vr_s[:, :].rearrange("b (m t e) -> b t m e", m=4, t=2)[:, t], start=True, stop=True)
                    if b % 2:
                        mm.then_inc(ev("vr_spread"), 1)
                pe.wait_ge(ev("s_max_part"), 1)
                pe.transpose(ps[0:64, 4, 0:128], sm["max"][:, :], ident).then_inc(ev("s_max_t"), 1)
                pe.wait_ge(ev("s_max_diag"), 1)
                pe.matmul(ps[:, 5, 64:128], ones[0:64, :], sm["den"][0:64, :], start=True, stop=True).then_inc(ev("s_max_spread"), 1)
                pe.wait_ge(ev("s_sums"), 1)
                pe.matmul(ps[:, 5, 128:192], ones, sm["max"][:, :], start=True, stop=True).then_inc(ev("s_den_spread"), 1)
                pe.wait_ge(ev("kv_added"), 1)
                for b in range(NS):
                    for m in range(4):
                        for t in range(2):
                            r = slice(64 * t, 64 * t + 64)
                            mm = pe.matmul(ps[r, t, 256 + m * 8 + b:257 + m * 8 + b], state[r, b, m, :],
                                           proj[r, QR + m, SEQ + b:SEQ + b + 1], start=True, stop=True)
                mm.then_inc(ev("ret_s_made"), 1)
                def score(h, j):
                    r, m = slice(64 * (h % 2), 64 * (h % 2) + 64), h // 2
                    if j == 0:
                        if h:
                            pe.wait_ge(ev("bias_done"), 4 * h)
                        pe.matmul(ps[:, 6, :], sel[:, h, :], c_heads[:, :], start=True, stop=True).then_inc(ev("c_spread"), 1)
                    u = 8 * h + j
                    if u >= 2:
                        pe.wait_ge(ev("score_read"), u - 1)
                    if j < 4:
                        pe.matmul(ps[:, u % 2, 0:(j + 1) * 128], proj[r, QF + m, j * 128:(j + 1) * 128],
                                  proj[r, KF + m, 0:(j + 1) * 128], start=True, stop=True).then_inc(ev("scores_done"), 1)
                    else:
                        k = j - 4
                        pe.matmul(ps[:, u % 2, 0:SEQ - k * 128], proj[r, KR + m, k * 128:(k + 1) * 128],
                                  proj[r, QR + m, k * 128:SEQ], start=True, stop=True).then_inc(ev("scores_done"), 1)

                def page_values(b, g):
                    k = g // 4
                    if g % 4 == 0:
                        pe.wait_ge(page_full[k], 64 * (NS + b + 1))
                    if g == 0 and b:
                        pe.wait_ge(ev("own_kept"), b)
                    mm = pe.matmul(ps[0:NH, 7, :], s_samp[:, b, :, g], pages[:, k, g % 4, :], start=g == 0, stop=g == NPG - 1)
                    if g % 4 == 3:
                        mm.then_inc(ev("v_used"), 1)

                def turned(h, j):
                    pe.wait_ge(ev("p_ready"), 4 * h + j + 1)
                    if 4 * h + j >= 2:
                        pe.wait_ge(ev("pt_copied"), 4 * h + j - 1)
                    for k in range(j + 1):
                        mm = pe.transpose(ps[:, 2 + j % 2, k * 128:(k + 1) * 128],
                                          probs[:, h % 2, PJ[j] + k * 128:PJ[j] + (k + 1) * 128], ident)
                    mm.then_inc(ev("pt_done"), 1)

                pe.wait_ge(ev("ret_s_copied"), 2)
                pe.wait_ge(ev("kv_read"), 4)
                pe.wait_ge(ev("ret_state_ready"), 2)
                pe.wait_ge(ev("p_samp"), 1)
                for j in range(8):
                    score(0, j)
                for h in range(NH):
                    r, m = slice(64 * (h % 2), 64 * (h % 2) + 64), h // 2
                    for j in range(8):
                        if h + 1 < NH:
                            score(h + 1, j)
                        page_values(h, j)
                    turned(h, 0)
                    turned(h, 1)
                    if h % 2 == 0 and h:
                        pe.wait_ge(ev("o_read"), h)
                    pe.wait_ge(ev("score_read"), 8 * h + 8)
                    for k in range(4):
                        mm = pe.matmul(ps[r, 5, k * 128:SEQ], vr_tok[:, k, h * HD:(h + 1) * HD],
                                       ret_a[h % 2][:, AK[k]:AK[k] + SEQ - k * 128], start=k == 0, stop=k == 3)
                    mm.then_inc(ev("ret_av"), 1)
                    turned(h, 2)
                    turned(h, 3)
                    pe.wait_ge(ev("pt_copied"), 4 * h + 4)
                    for k in range(4):
                        mm = pe.matmul(ps[r, 4, k * 128:SEQ], vf_tok[:, k, h * HD:(h + 1) * HD], p_t[:, k, k * 128:SEQ],
                                       start=k == 0, stop=k == 3)
                    mm.then_inc(ev("fox_av"), 1)
                pe.wait_ge(ev("own_kept"), NS)
                for b in range(NS):
                    mm = pe.matmul(ps[0:NS, 0, :], unit[:, b, :], own[b], start=b == 0, stop=b == NS - 1)
                mm.then_inc(ev("own_rows"), 1)
                pe.wait_ge(ev("fox_rows"), 1)
                for m in range(4):
                    mm = pe.transpose(ps[:, 1, m * 8:m * 8 + 8], s_prod[:, m * 128:(m + 1) * 128], ident[0:8, 0:8])
                mm.then_inc(ev("fox_s_t"), 1)
                pe.wait_ge(ev("o_read"), 8)
                pe.wait_ge(ev("fox_s_done"), 1)
                for m in range(4):
                    for half in range(2):
                        mm = pe.matmul(ps[:, 2 * (m % 2) + half, 0:HT], head_mean, proj[:, VR + m, half * HT:(half + 1) * HT],
                                       start=True, stop=True)
                    mm.then_inc(ev("hn_mean"), 1)
                    pe.wait_ge(ev("hn_sq_done"), m + 1)
                    if m >= 2:
                        pe.wait_ge(ev("hn_dev_done"), m - 1)
                    for half in range(2):
                        mm = pe.matmul(ps[:, 4 + 2 * (m % 2) + half, 0:HT], head_mean, hn_sq[:, m % 2, half * HT:(half + 1) * HT],
                                       start=True, stop=True)
                    mm.then_inc(ev("hn_var"), 1)
                pe.wait_ge(ev("cat_lo"), 10)

            def odd_pe():
                c0 = chunks_before(ODD)

                def body(i):
                    for j in range(2):
                        for k in range(3):
                            if is_first(i) and j == 0 and k < 2:
                                continue
                            m, q = i * 2 + j, 3 * j + k
                            if k == 0 and not is_first(i):
                                pe.wait_ge(ev("conv_steps"), m * 12 - 13)
                            if k == 1 and not (is_first(i) and j == 0):
                                pe.wait_ge(ev("cg_copied"), m)
                            if k == 2 and not (is_first(i) and j == 0):
                                pe.wait_ge(ev("conv_steps"), m * 12 - 9)
                            product(c0 + i * 6 + q, q % 2, (2 + j, 0, 1)[k], KT, h_hi, h_lo)
                first_products(ODD, 2, 0)
                loop(pe, True, KT // 2, body)
                pe.wait_ge(ev("conv_steps"), 12 * KT + 1)
                pe.transpose(ps[:, 7, 0:128], tail_s[:, :, :, :].rearrange("p b j t -> p (b j t)"), ident)
                pe.transpose(ps[0:2 * KT, 7, 128:256], tail_p[:, :, :].rearrange("p j t -> p (j t)"), ident).then_inc(ev("tails_t"), 1)
                pe.wait_ge(ev("mixed_lo"), KT)

            def second_product(n, body):
                loop(pe, n == 0, KT // 4, body)
                body(KT // 4)
                body(KT // 4 + 1)

            for n in range(last):
                if n in FFN:
                    f0 = FT * ffns_before(n)

                    def body(i):
                        for j in range(2):
                            for k in range(2):
                                if is_first(i) and j == 0:
                                    continue
                                if not (n == 0 and is_first(i)):
                                    pe.wait_ge(gate_done if k else silu_done, f0 + i * 2 + j - 1)
                                product(chunks_before(n) + i * 4 + 2 * j + k, k, 2 * j + k, KT, h_hi, h_lo)
                    first_products(n, 0, 1)
                    if n == 0:
                        first_turned(4)
                        first_turned(5)
                        pe.wait_ge(mod_steps, mod_steps_before(1))
                    loop(pe, True, FT // 2, body)
                    pe.wait_ge(hid_lo_done, f0 + FT)

                    def body(i):
                        for j in range(2):
                            for k in range(2):
                                if k == 0 and not (n == 0 and is_first(i)):
                                    pe.wait_ge(drained, 2 * (KT * n + i * 2 + j - 1))
                                product(chunks_before(n, True) + i * 4 + 2 * j + k, k, j, FH, hid_hi, hid_lo,
                                        kt0=k * FH, start=k == 0, stop=k == 1)
                                if isinstance(i, int) and (i, j, k) == (KT // 4, 0, 0):
                                    shift_sums(n)
                                if n + 1 < last:
                                    for q in ((0, 1), (2,), (3, 4), (5,))[2 * j + k]:
                                        ada(n + 1, i * 6 + q, q % NADA)
                    second_product(n, body)
                else:
                    if n == EVEN:
                        even_pe()
                        hi, lo = h_hi, h_lo
                    else:
                        odd_pe()
                        hi, lo = mix_hi, mix_lo

                    def body(i):
                        for k in range(2):
                            pe.wait_ge(drained, 2 * (KT * n + i * 2 + k - 1))
                            product(chunks_before(n, True) + i * 2 + k, k, k, KT, hi, lo)
                            if isinstance(i, int) and (i, k) == (KT // 4, 0):
                                shift_sums(n)
                            if n + 1 < last:
                                for q in range(3):
                                    ada(n + 1, i * 6 + 3 * k + q, q)
                    second_product(n, body)
                norm_sums(n)

            pe.wait_ge(ln_done, KT * last)
            for j in range(4):
                for g in range(2):
                    u = 2 * j + g
                    if u >= 2:
                        pe.wait_ge(y_copied, u - 1)
                    for t in range(4):
                        mm = pe.transpose(ps[:, 2 + g, t * 128:(t + 1) * 128],
                                          x[:, 4 * g + t, j // 2, (j % 2) * 128:(j % 2) * 128 + 128], ident)
                    mm.then_inc(y_t, 1)
            pe.wait_ge(samp_out, 1)
            for t in range(KT):
                mm = pe.transpose(ps[0:NS, 4 + t // 4, (t % 4) * 128:(t % 4) * 128 + 128], samp_t[:, t, :], ident)
            mm.then_inc(y_t, 1)

        @block.scalar
        def _(act):
            def squares(n, tiles):
                for t in tiles:
                    act.wait_ge(shifted, KT * n + t + 1)
                    act.activation(sq[:, t % 2] if t else sq_sum[:, :, :], sq[:, t % 2], ACT.Square).then_inc(squared, 1)

            def norm_act(n):
                act.wait_ge(mean_done, n + 1)
                act.activation(mean[:, :, :], pair(2), ACT.Identity).then_inc(mean_ready, 1)
                act.wait_ge(delta_steps, 3 * (n + 1))
                act.wait_ge(eps_ready, 2)
                act.activation(dev, dev, ACT.Sqrt, bias=eps_ln[:, :]).then_inc(dev_done, 1)

            def affine(n):
                if n + 1 < last:
                    act.wait_ge(samp_mod, KT * (n + 2))
                    act.wait_ge(h32_done, KT * (n + 2))
                for t in range(KT):
                    if n + 1 == last:
                        act.wait_ge(normed, KT * n + t + 1)
                    act.activation(x[:, t], x[:, t], ACT.Identity, scale=params[:, LN_G + n * KT + t:LN_G + n * KT + t + 1],
                                   bias=params[:, LN_B + n * KT + t:LN_B + n * KT + t + 1]).then_inc(ln_done, 1)

            def modulate_act(n):
                m = n % 2
                act.wait_ge(mod_steps, mod_steps_before(n) + (5 if n else 2))
                for t in range(KT):
                    if n:
                        act.wait_ge(normed, KT * (n - 1) + t + 1)
                    act.activation(h32[:, t, :, 0:HP], x[:, t, :, 0:HP], ACT.Identity, scale=mod[:, m, KT + t, 0:1],
                                   bias=mod[:, m, t, 0:1]).then_inc(h32_done, 1)
                    act.wait_ge(h32_done, KT * n + t + 1)
                    act.wait_ge(h32_samp, KT * n + t + 1)
                    act.activation(h_hi[:, t], h32[:, t], ACT.Identity).then_inc(h_hi_done, 1)

            def cut(c, k, kt):
                if not (isinstance(c, int) and c < 2):
                    act.wait_ge(chunk_used, c - 1)
                act.wait_ge(raw_full[k], (c - k) * 8 + 16)
                act.activation(w_hi[:, k, 0:kt, :], raw[:, k, 0:kt, :], ACT.Identity).then_inc(hi_cut, 1)

            def even_act():
                c0 = chunks_before(EVEN)

                def body(i, more=True):
                    for k in range(2):
                        m = i * 2 + k
                        if more:
                            cut(c0 + m + 2, k, KT)
                        else:
                            act.wait_ge(chunk_used, c0 + m + 1)
                        tile = proj[:, bass.ds(m, 1)].rearrange("p a c -> p (a c)")
                        act.activation(tile[:, 0:SEQ].rearrange("p (h c) -> p h c", h=2), ps[:, 2 * k:2 * k + 2, 0:HP],
                                       ACT.Identity).then_inc(ev("copied"), 1)
                        act.activation(tile[:, SEQ:NTOK].rearrange("p (h c) -> p h c", h=2), ps[:, 2 * k:2 * k + 2, HP:HT],
                                       ACT.Identity).then_inc(ev("copied"), 1)
                body(0)
                affine(EVEN - 1)
                act.wait_ge(ev("fg_in"), 32)
                act.activation(fg_hi[:, :, :], w_fg[:, :, :], ACT.Identity).then_inc(ev("fg_cut"), 1)
                body(1)
                act.wait_ge(ev("lf_gathered"), 1)
                act.activation(lf_past[:, :, :, :].rearrange("p b h g -> p (b h g)"), ps[:, 5, :], ACT.Identity
                               )
                act.wait_ge(ev("q_rows"), 1)
                act.activation(q_s[:, :], ps[0:NS, 4, :], ACT.Identity).then_inc(ev("q_s_ready"), 1)
                act.wait_ge(ev("fg_made"), 1)
                act.activation(fg_rows[:, 0:SEQ].rearrange("p (h c) -> p h c", h=2), ps[0:NH, 6:8, 0:HP], ACT.Identity
                               ).then_inc(ev("fg_copied"), 1)
                act.activation(fg_rows[:, SEQ:NTOK].rearrange("p (h c) -> p h c", h=2), ps[0:NH, 6:8, HP:HT], ACT.Identity
                               ).then_inc(ev("fg_copied"), 1)
                for b in range(NS):
                    act.wait_ge(ev("q_spread"), b + 1)
                    act.activation(q_all[:, b, :], ps[:, 4 + 2 * (b % 2), :], ACT.Identity).then_inc(ev("q_spread_copied"), 1)
                with act.Fori(2, 13) as i:
                    body(i)
                body(13, more=False)
                both = lambda v: (v[:, 0:4, :], v[0:NS, 4, :])
                act.wait_ge(ev("fg_z"), 2)
                for k, (d, v) in enumerate(zip(both(lf_b), both(lf_a))):
                    act.activation(d, v, ACT.Abs).then_inc(ev("fg_abs"), 1)
                act.wait_ge(ev("fg_abs"), 2)
                for v in both(lf_b):
                    act.activation(v, v, ACT.Exp, scale=-1.0).then_inc(ev("fg_exp"), 1)
                act.wait_ge(ev("fg_exp"), 2)
                for v in both(lf_b):
                    act.activation(v, v, ACT.Ln, bias=1.0).then_inc(ev("fg_ln"), 1)
                for m in range(4):
                    act.activation(proj[:, GR + m], proj[:, GR + m], ACT.Silu).then_inc(ev("gate_silu"), 1)
                act.wait_ge(ev("c_made"), 1)
                act.activation(c_cols[:, :, :].rearrange("p j h -> p (j h)"), ps[:, 5, 0:4 * NH], ACT.Identity).then_inc(ev("c_copied"), 1)
                act.activation(c_heads[:, :], ps[0:NH, 6, :], ACT.Identity).then_inc(ev("c_copied"), 1)
                act.wait_ge(ev("k_read"), 2 * NS)
                for count in range(12):
                    act.wait_ge(ev("tok_t"), count + 1)
                    act.activation((kf_tok, vf_tok, vr_tok)[count // 4][:, count % 4, :], ps[:, count % 4, :], ACT.Identity
                                   ).then_inc(ev("tok_copied"), 1)
                for u, rows in enumerate((k_s, v_s, vr_s)):
                    act.wait_ge(ev("s_rows_t"), u + 1)
                    act.activation(rows[:, :], ps[0:NS, 4 + u, :], ACT.Identity).then_inc(ev("tok_copied"), 1)
                act.wait_ge(ev("ret_state_made"), 1)
                for t in range(2):
                    r = slice(64 * t, 64 * t + 64)
                    act.activation(ret_state[r, :, :], ps[r, 7, :].rearrange("p (m c) -> p m c", m=4)[:, :, 64 * t:64 * t + 64],
                                   ACT.Identity).then_inc(ev("ret_state_ready"), 1)
                act.wait_ge(ev("s_shifted"), 2)
                act.activation(s_samp[:, :, :, :].rearrange("p b h g -> p (b h g)"),
                               s_samp[:, :, :, :].rearrange("p b h g -> p (b h g)"), ACT.Exp).then_inc(ev("s_exp"), 1)
                act.activation(sm["new"][:, :], sm["new"][:, :], ACT.Exp).then_inc(ev("s_exp"), 1)
                act.wait_ge(ev("ret_s_made"), 1)
                for t in range(2):
                    r = slice(64 * t, 64 * t + 64)
                    act.activation(proj[r, VR:VR + 4, SEQ:NTOK], ps[r, t, 256:288].rearrange("p (m b) -> p m b", m=4),
                                   ACT.Identity).then_inc(ev("ret_s_copied"), 1)

                def bias(h):
                    act.wait_ge(ev("c_spread"), h + 1)
                    if h >= 2:
                        act.wait_ge(ev("pt_done"), 4 * (h - 1))
                    for j in range(4):
                        act.activation(probs[:, h % 2, PJ[j]:PJ[j] + (j + 1) * 128], ps[:, 6, 0:(j + 1) * 128], ACT.Identity,
                                       scale=-1.0, bias=c_cols[:, j, h:h + 1]).then_inc(ev("bias_done"), 1)

                def exps(h):
                    for j in range(4):
                        v = probs[:, h % 2, PJ[j]:PJ[j] + (j + 1) * 128]
                        c = 4 * h + j
                        act.wait_ge(ev("max_done"), c + 1)
                        act.activation(v, v, ACT.Exp, bias=n_max[:, c:c + 1], accum_out=row_sum[:, c:c + 1]
                                       ).then_inc(ev("exp_done"), 1)

                act.wait_ge(ev("kv_added"), 1)
                bias(0)
                exps(0)
                act.wait_ge(ev("rows_stored"), 32)
                act.wait_ge(ev("new_v"), 1)
                for h in range(NH):
                    if h + 1 < NH:
                        bias(h + 1)
                    for j in range(4):
                        c = 4 * h + j
                        act.wait_ge(ev("pt_done"), c + 1)
                        if h:
                            act.wait_ge(ev("fox_av"), h)
                        act.activation(p_t[:, 0:j + 1, j * 128:(j + 1) * 128],
                                       ps[:, 2 + j % 2, 0:(j + 1) * 128].rearrange("p (k c) -> p k c", c=128), ACT.Identity
                                       ).then_inc(ev("pt_copied"), 1)
                    if h + 1 < NH:
                        exps(h + 1)
                for m in range(4):
                    act.wait_ge(ev("hn_centred"), m + 1)
                    if m >= 2:
                        act.wait_ge(ev("hn_var"), m - 1)
                    act.activation(hn_sq[:, m % 2, :], proj[:, VR + m], ACT.Square).then_inc(ev("hn_sq_done"), 1)
                    act.wait_ge(ev("hn_var"), m + 1)
                    if m >= 2:
                        act.wait_ge(ev("hn_scaled"), m - 1)
                    act.activation(hn_dev[:, m % 2, :].rearrange("p (h c) -> p h c", h=2), pair(2 + m % 2), ACT.Sqrt,
                                   bias=eps_gn[:, :]).then_inc(ev("hn_dev_done"), 1)
                for t in range(KT):
                    if t >= 4:
                        act.wait_ge(ev("hn_gated"), t - 3)
                    act.activation(h_hi[:, t, :, 0:HP], mixed_tile(t)[:, 0:SEQ].rearrange("p (h c) -> p h c", h=2),
                                   ACT.Identity).then_inc(ev("cat_hi"), 1)
                for u, first in enumerate((VF, VR)):
                    act.activation(h_hi[:, 4 * u:4 * u + 4, :, HP:HT],
                                   proj[:, first:first + 4, SEQ:NTOK].rearrange("p t (h c) -> p t h c", h=2),
                                   ACT.Identity).then_inc(ev("cat_hi"), 1)
                for k in range(2):
                    cut(chunks_before(EVEN, True) + k, k, KT)

            def odd_act():
                c0 = chunks_before(ODD)

                def body(i):
                    for j in range(2):
                        m = i * 2 + j
                        q = 3 * j
                        cut(c0 + i * 6 + q + 2, q % 2, KT)
                        cut(c0 + i * 6 + q + 3, (q + 1) % 2, KT)
                        if not (is_first(i) and j == 0):
                            act.wait_ge(ev("conv_steps"), m * 12 - 9)
                        act.activation(cg[:, :, :], pair(0), ACT.Identity).then_inc(ev("cg_copied"), 1)
                        cut(c0 + i * 6 + q + 4, q % 2, KT)
                        act.wait_ge(ev("conv_steps"), m * 12 + 11)
                        act.activation(mix_hi[:, bass.ds(m, 1)].rearrange("p a h c -> p (a h) c"), mixed[:, j],
                                       ACT.Identity).then_inc(ev("mixed_hi"), 1)
                body(0)
                affine(ODD - 1)
                with act.Fori(1, KT // 2) as i:
                    body(i)
                act.wait_ge(ev("tails_t"), 1)
                act.activation(tail_rows[:, 0, :], ps[:, 7, 0:128], ACT.Identity).then_inc(ev("tail_rows_ready"), 1)
                act.activation(tail_rows[0:2 * KT, 1, :], ps[0:2 * KT, 7, 128:256], ACT.Identity).then_inc(ev("tail_rows_ready"), 1)

            def second_product(n):
                c0 = chunks_before(n, True)
                per_tile = 2 if n in FFN else 1
                kt, next_kt = tiles_of_product(n, True), next_tiles(n, True)
                with act.Fori(0, KT // 2 * per_tile // 2) as i:
                    for k in range(2):
                        cut(c0 + i * 2 + k + 2, k, kt)
                for t in range(KT // 2, KT):
                    for u in range(t * per_tile, (t + 1) * per_tile):
                        k = u % 2
                        beyond = u + 2 >= KT * per_tile
                        if not beyond or next_kt:
                            cut(c0 + u + 2, k, next_kt if beyond else kt)
                    if t == KT // 2:
                        act.wait_ge(half_summed, n + 1)
                        act.activation(shift[:, :, :], pair(2), ACT.Identity, scale=2.0).then_inc(shift_ready, 1)
                    squares(n, SQUARES_WITH[t])

            act.wait_ge(c_ready, 1)
            act.activation(c_act[:, :, :], c_t[:, :, :], ACT.Silu).then_inc(cond_ready, 1)

            def copy_rows(g):
                act.wait_ge(rows_made, g + 1)
                act.activation(ada_rows[:, g % 4, :], ps[0:9, (0, 1, 0, 1, 4, 5)[g], :], ACT.Identity).then_inc(rows_copied, 1)

            copy_rows(0)
            copy_rows(1)
            for t in range(KT):
                act.wait_ge(x_t, t + 1)
                act.activation(x[:, t, :, 0:HP], ps[:, 2 + t % 2, :].rearrange("p (h c) -> p h c", h=2),
                               ACT.Identity).then_inc(x_copied, 1)
            act.wait_ge(x_t, KT + 1)
            act.activation(x[:, :, :, HP:HT], ps[:, 4, 0:64].rearrange("p (t h c) -> p t h c", t=KT, h=2),
                           ACT.Identity).then_inc(x_copied, 1)
            copy_rows(2)
            act.wait_ge(x_copied, KT + 1)
            for k in range(2):
                cut(k, k, KT)
            copy_rows(3)
            modulate_act(0)
            copy_rows(4)
            copy_rows(5)
            act.wait_ge(ada_used, MT)
            for n in range(last):
                if n - 1 in (EVEN, ODD):
                    act.wait_ge(*((ev("kv_stored"), 32) if n - 1 == EVEN else (ev("tails_stored"), 32)))
                if n in FFN:
                    f0 = FT * ffns_before(n)

                    def body(i, final):
                        for j in range(2):
                            c = chunks_before(n) + i * 4 + 2 * j
                            kt = next_tiles(n, False) if final and j else KT
                            cut(c + 2, 0, kt)
                            if not (n == 0 and is_first(i)):
                                act.wait_ge(gate_done, f0 + i * 2 + j - 1)
                            act.activation(silu_a[:, j], pair(2 * j), ACT.Silu).then_inc(silu_done, 1)
                            cut(c + 3, 1, kt)
                            act.wait_ge(gate_done, f0 + i * 2 + j + 1)
                            act.activation(hid_hi[:, bass.ds(i * 2 + j, 1)].rearrange("p a h c -> p (a h) c"), gated[:, j], ACT.Identity).then_inc(hid_hi_done, 1)
                    body(0, False)
                    if n:
                        affine(n - 1)
                    with act.Fori(1, FT // 2 - 1) as i:
                        body(i, False)
                    body(FT // 2 - 1, True)
                else:
                    (even_act if n == EVEN else odd_act)()
                second_product(n)
                norm_act(n)
                if n + 1 < last:
                    modulate_act(n + 1)
            affine(last - 1)
            for j in range(4):
                for g in range(2):
                    act.wait_ge(y_t, 2 * j + g + 1)
                    act.activation(y_rows[:, j, g * 512:(g + 1) * 512], ps[:, 2 + g, :], ACT.Identity).then_inc(y_copied, 1)
            act.wait_ge(y_t, 9)
            act.activation(ys_rows[:, :].rearrange("p (g c) -> p g c", g=2), ps[0:NS, 4:6, :], ACT.Identity).then_inc(y_copied, 1)

        @block.vector
        def _(dve):
            def modulation(n):
                m, s0 = n % 2, mod_steps_before(n)
                dve.wait_ge(ada_used, MT * n + (MT if n else 2 * KT))
                add_bias(n, 0, 2 * KT)
                dve.wait_ge(mod_steps, s0 + 1)
                shift_m, scale_m = mod[:, m, 0:KT], mod[:, m, KT:2 * KT]
                dve.tensor_scalar(scale_m, scale_m, 1.0, None, ALU.add).then_inc(mod_steps, 1)
                dve.wait_ge(mod_steps, s0 + 2)
                if n:
                    g, b = (params[:, v + (n - 1) * KT:v + n * KT].unsqueeze(2).to_broadcast([128, KT, 9]) for v in (LN_G, LN_B))
                    dve.tensor_tensor(mod_b[:, :, :], scale_m, b, ALU.mult).then_inc(mod_steps, 1)
                    dve.wait_ge(mod_steps, s0 + 3)
                    dve.tensor_tensor(scale_m, scale_m, g, ALU.mult).then_inc(mod_steps, 1)
                    dve.tensor_tensor(shift_m, shift_m, mod_b[:, :, :], ALU.add).then_inc(mod_steps, 1)
                    gate(n)

            def add_bias(n, q0, q1):
                bias = params[:, n * MT + q0:n * MT + q1].unsqueeze(2).to_broadcast([128, q1 - q0, 9])
                bank = 7 if n == 0 and q0 == 2 * KT else 6
                dve.tensor_tensor(mod[:, n % 2, q0:q1], ps[:, bank, 9 * q0:9 * q1].rearrange("p (q c) -> p q c", c=9), bias,
                                  ALU.add).then_inc(mod_steps, 1)

            def gate(n):
                add_bias(n, 2 * KT, MT)
                dve.wait_ge(mod_steps, mod_steps_before(n + 1) - 1)
                v = mod[:, n % 2, 2 * KT:MT]
                dve.tensor_scalar(v, v, (0.5 if n in FFN else 1.0) / ALPHA, None, ALU.mult).then_inc(mod_steps, 1)

            def modulate(n):
                for t in range(KT):
                    if n:
                        normalise_tile(n - 1, t)
                    if t:
                        low(n, t - 1)
                low(n, KT - 1)

            def normalise_tile(n, t):
                dve.wait_ge(centred[t >= CENTRE], (CENTRE if t < CENTRE else KT - CENTRE) * n
                            + (t if t < CENTRE else t - CENTRE) + 1)
                dve.tensor_tensor(x[:, t], x[:, t], rdev[:, :, :], ALU.mult).then_inc(normed, 1)

            def low(n, t):
                dve.wait_ge(h_hi_done, KT * n + t + 1)
                dve.tensor_tensor(h_lo[:, t], h32[:, t], h_hi[:, t].bitcast(F32), ALU.subtract).then_inc(h_lo_done, 1)

            def residual(n, i, j, q):
                m = n % 2
                t = i * 2 + j
                c0 = KT * n + t
                xt = x[:, bass.ds(t, 1)].rearrange("p a h c -> p (a h) c")
                g = mod[:, m, bass.ds(t + 2 * KT, 1)].rearrange("p a c -> p (a c)")
                dve.scalar_tensor_tensor(xt[:, :, 0:HP], ps[:, 2 * q:2 * q + 2, 0:HP], g[:, 0:1], xt[:, :, 0:HP],
                                         ALU.mult, ALU.add).then_inc(drained, 1)
                dve.tensor_tensor(samp8[:, :].rearrange("p (h c) -> p h c", h=2), ps[:, 2 * q:2 * q + 2, HP:HT],
                                  g[:, 1:9].rearrange("p (h c) -> p h c", h=2), ALU.mult).then_inc(drained, 1)
                dve.wait_ge(drained, c0 * 2 + 2)
                dve.tensor_tensor(xt[:, :, HP:HT], xt[:, :, HP:HT], samp8[:, :].rearrange("p (h c) -> p h c", h=2),
                                  ALU.add).then_inc(samp_added, 1)
                s0 = (KT - 1) * n + t
                if is_first(t):
                    dve.wait_ge(samp_added, c0 + 1)
                    dve.tensor_copy(tile_sum[:, :, :], xt).then_inc(summed, 1)
                elif not (isinstance(t, int) and t == KT - 1):
                    dve.wait_ge(samp_added, c0 + 1)
                    if isinstance(t, int) and t == KT // 2:
                        dve.wait_ge(half_summed, n + 1)
                    dve.wait_ge(summed, s0)
                    dve.tensor_tensor(tile_sum[:, :, :], tile_sum[:, :, :], xt, ALU.add).then_inc(summed, 1)

            def distance(n, t):
                a0 = (KT - 2) * n
                if t >= 3:
                    dve.wait_ge(sq_added, a0 + t - 2)
                elif t == 2:
                    dve.wait_ge(squared, KT * n + 1)
                dve.tensor_tensor(sq[:, t % 2], x[:, t], shift[:, :, :], ALU.subtract).then_inc(shifted, 1)
                if t >= 2:
                    dve.wait_ge(squared, KT * n + t)
                    if t >= 3:
                        dve.wait_ge(sq_added, a0 + t - 2)
                    dve.tensor_tensor(sq_sum[:, :, :], sq_sum[:, :, :], sq[:, (t - 1) % 2], ALU.add).then_inc(sq_added, 1)

            def residuals(n, product_done):
                def body(i):
                    for j in range(2):
                        product_done(i, j)
                        residual(n, i, j, j)
                dve.wait_ge(mod_steps, mod_steps_before(n + 1))
                if n:
                    dve.wait_ge(ln_done, KT * n)
                loop(dve, True, KT // 4, body)
                for t in range(KT // 2, KT):
                    product_done(t // 2, t % 2)
                    residual(n, t // 2, t % 2, t % 2)
                    if t == KT // 2:
                        dve.wait_ge(shift_ready, n + 1)
                    dve.wait_ge(samp_added, KT * n + t + 1)
                    for u in SQUARES_WITH[t]:
                        distance(n, u)

            def norm(n):
                d0 = 3 * n
                dve.wait_ge(mean_ready, n + 1)
                dve.tensor_tensor(shift[:, :, :], mean[:, :, :], shift[:, :, :], ALU.subtract).then_inc(delta_steps, 1)
                dve.wait_ge(delta_steps, d0 + 1)
                dve.tensor_tensor(shift[:, :, :], shift[:, :, :], shift[:, :, :], ALU.mult).then_inc(delta_steps, 1)
                dve.wait_ge(delta_steps, d0 + 2)
                dve.wait_ge(var_done, n + 1)
                dve.tensor_tensor(dev, pair(0), shift[:, :, :], ALU.subtract).then_inc(delta_steps, 1)
                centre(dve, n, 0)
                dve.wait_ge(dev_done, n + 1)
                dve.reciprocal(rdev[:, :, :], dev).then_inc(rdev_done, 1)
                dve.wait_ge(rdev_done, n + 1)
                if n + 1 == last:
                    for t in range(KT):
                        normalise_tile(n, t)

            def then(name, instruction, count=1):
                instruction.then_inc(ev(name), 1)
                dve.wait_ge(ev(name), count)

            chained = [0]

            def link(instruction):
                chained[0] += 1
                instruction.then_inc(ev("chained"), 1)

            def rest():
                dve.wait_ge(ev("chained"), chained[0])

            def chain(instruction):
                link(instruction)
                rest()

            def even_dve():
                dve.wait_ge(ev("fg_cut"), 1)
                dve.tensor_tensor(fg_lo[:, :, :], w_fg[:, :, :], fg_hi[:, :, :].bitcast(F32), ALU.subtract).then_inc(ev("fg_cut"), 1)
                dve.wait_ge(ev("gather_in"), 16)
                chain(dve.tensor_copy(page_f[:, :], page_ids[:, :]))
                dve.tensor_scalar(one_hot[:, :], page_f[:, :], lane[0:n_phys, :], None, ALU.is_equal).then_inc(ev("one_hot_ready"), 1)
                dve.wait_ge(ev("q_spread_copied"), NS)
                with dve.Fori(0, NS) as b:
                    for k in range(2):
                        dve.wait_ge(page_full[k], b * 64 + 64)
                        q_b = q_all[:, bass.ds(b, 1)].to_broadcast([128, 4, FOXW])
                        dve.tensor_tensor(pages[:, k], pages[:, k], q_b, ALU.mult).then_inc(ev("k_prod"), 1)
                        dve.wait_ge(ev("k_prod"), b * 2 + k + 1)
                        dve.tensor_reduce(s_samp[:, bass.ds(b, 1), :, 4 * k:4 * k + 4].rearrange("p a h g -> p (a g) h"),
                                          pages[:, k].rearrange("p g (h d) -> p g h d", h=NH), AX, ALU.add
                                          ).then_inc(ev("k_read"), 1)
                both = lambda v: (v[:, 0:4, :], v[0:NS, 4, :])
                dve.wait_ge(ev("fg_done"), 1)
                dve.wait_ge(ev("fg_in"), 32)
                dve.tensor_tensor(lf_a[:, 0:4, :], ps[:, 7, 0:4 * NH].rearrange("p (j h) -> p j h", j=4),
                                  b_fg[:, :].unsqueeze(1).to_broadcast([128, 4, NH]), ALU.add).then_inc(ev("fg_z"), 1)
                dve.tensor_tensor(lf_a[0:NS, 4, :], ps[0:NS, 7, 4 * NH:5 * NH], b_fg[0:NS, :], ALU.add).then_inc(ev("fg_z"), 1)
                dve.wait_ge(ev("fg_abs"), 2)
                dve.wait_ge(ev("fg_z"), 2)
                for v in both(lf_a):
                    link(dve.tensor_scalar(v, v, 0.0, None, ALU.min))
                rest()
                dve.wait_ge(ev("fg_ln"), 2)
                for d, v, w in zip(both(logf), both(lf_a), both(lf_b)):
                    dve.tensor_tensor(d, v, w, ALU.subtract).then_inc(ev("logf_ready"), 1)
                dve.wait_ge(ev("logf_ready"), 2)
                dve.tensor_tensor(sm["col"][0:NS, :].rearrange("p (b h) -> p b h", b=NS),
                                  logf[0:NS, 4:5, :].to_broadcast([NS, NS, NH]), delta, ALU.mult).then_inc(ev("lfnd_ready"), 1)
                for u in range(8):
                    tile = proj[:, QR + u]
                    dve.wait_ge(ev("rot_made"), u + 1)
                    dve.tensor_tensor(rot[:, u % 2, :].rearrange("p (h c) -> p h c", h=2), pair(u % 2),
                                      sin_t.rearrange("p (h c) -> p h c", h=2), ALU.mult).then_inc(ev("rot_read"), 1)
                    link(dve.tensor_tensor(tile, tile, cos_t, ALU.mult))
                    rest()
                    dve.wait_ge(ev("rot_read"), u + 1)
                    link(dve.tensor_tensor(tile, tile, rot[:, u % 2, :], ALU.add))
                rest()
                for m in range(4):
                    link(dve.tensor_scalar(proj[:, KR + m], proj[:, KR + m], QSCALE, None, ALU.mult))
                rest()
                dve.wait_ge(ev("state_in"), 32)
                dve.tensor_tensor(state[:, :, :, :], state[:, :, :, :],
                                  gdec.unsqueeze(1).unsqueeze(3).to_broadcast([128, NS, 4, HD]), ALU.mult
                                  ).then_inc(ev("k_scaled"), 1)
                dve.wait_ge(ev("tok_copied"), 15)
                chain(dve.tensor_tensor(s_prod[:, :], q_s[:, :], k_s[:, :], ALU.mult))
                chain(dve.tensor_reduce(sm["den"][0:NS, 0:NH], s_prod[:, :].rearrange("p (h d) -> p h d", h=NH), AX, ALU.add))
                chain(dve.tensor_scalar(sm["den"][0:NS, 0:NH], sm["den"][0:NS, 0:NH], QSCALE, None, ALU.mult))
                dve.tensor_tensor(sm["max"][0:NS, :].rearrange("p (b h) -> p b h", b=NS),
                                  sm["den"][0:NS, 0:NH].unsqueeze(1).to_broadcast([NS, NS, NH]), delta, ALU.mult
                                  ).then_inc(ev("s_new_rows"), 1)
                for j in range(4):
                    dve.wait_ge(ev("tok_t"), 13 + j)
                    dve.tensor_tensor(kr_tok[:, j, :].rearrange("p (h d) -> p h d", h=NH),
                                      ps[:, j, :].rearrange("p (h d) -> p h d", h=NH),
                                      tail[:, j, :].unsqueeze(2).to_broadcast([128, NH, HD]), ALU.mult).then_inc(ev("kr_copied"), 1)
                s_all = s_samp[:, :, :, :].rearrange("p b h g -> p (b h g)")
                s_pg = s_samp[:, :, :, :].rearrange("p b h g -> p (b h) g")
                wide = lambda v: v.unsqueeze(2).to_broadcast([128, 64, NPG])
                dve.wait_ge(ev("s_new_spread"), 1)
                link(dve.tensor_copy(sm["new"][:, :], ps[:, 5, 0:64]))
                dve.wait_ge(ev("after_made"), 1)
                chain(dve.scalar_tensor_tensor(s_all, s_all, QSCALE, ps[:, 6, :], ALU.mult, ALU.add))
                chain(dve.tensor_reduce(sm["max"][:, :], s_pg, AX, ALU.max))
                rest()
                dve.tensor_tensor(sm["max"][:, :], sm["max"][:, :], sm["new"][:, :], ALU.max).then_inc(ev("s_max_part"), 1)
                k_b = proj[:, KR:KR + 4, SEQ:NTOK].rearrange("p m b -> p b m")
                for g in range(4):
                    dve.wait_ge(ev("vr_spread"), g + 1)
                    dve.tensor_tensor(kv_s[:, 2 * g:2 * g + 2], ps[:, g, :].rearrange("p (b m e) -> p b m e", b=2, m=4),
                                      k_b[:, 2 * g:2 * g + 2].unsqueeze(3).to_broadcast([128, 2, 4, HD]), ALU.mult
                                      ).then_inc(ev("kv_read"), 1)
                dve.wait_ge(ev("kv_read"), 4)
                dve.wait_ge(ev("k_scaled"), 1)
                then("kv_added", dve.tensor_tensor(state[:, :, :, :], state[:, :, :, :], kv_s[:, :, :, :], ALU.add))
                dve.wait_ge(ev("s_max_t"), 1)
                chain(dve.tensor_reduce(sm["col"][0:64, 0:1], ps[0:64, 4, 0:128], AX, ALU.max))
                dve.tensor_scalar(sm["den"][0:64, :], ident[0:64, 0:64], sm["col"][0:64, 0:1], None, ALU.mult
                                  ).then_inc(ev("s_max_diag"), 1)
                dve.wait_ge(ev("s_max_spread"), 1)
                dve.tensor_tensor(s_pg, s_pg, wide(ps[:, 5, 64:128]), ALU.subtract).then_inc(ev("s_shifted"), 1)
                dve.tensor_tensor(sm["new"][:, :], sm["new"][:, :], ps[:, 5, 64:128], ALU.subtract).then_inc(ev("s_shifted"), 1)
                dve.wait_ge(ev("s_exp"), 2)
                dve.tensor_reduce(sm["max"][:, :], s_pg, AX, ALU.add).then_inc(ev("s_sums"), 1)
                dve.wait_ge(ev("s_den_spread"), 1)
                chain(dve.tensor_tensor(sm["den"][:, :], sm["new"][:, :], ps[:, 5, 128:192], ALU.add))
                chain(dve.reciprocal(sm["den"][:, :], sm["den"][:, :]))
                link(dve.tensor_tensor(sm["new"][:, :], sm["new"][:, :], sm["den"][:, :], ALU.mult))
                link(dve.tensor_tensor(s_pg, s_pg, wide(sm["den"][:, :]), ALU.mult))
                rest()
                dve.tensor_tensor(sm["col"][0:NS, :].rearrange("p (b h) -> p b h", b=NS),
                                  sm["new"][0:NS, :].rearrange("p (b h) -> p b h", b=NS), delta, ALU.mult).then_inc(ev("p_samp"), 1)
                dve.wait_ge(ev("p_samp"), 1)
                chain(dve.tensor_reduce(sm["den"][0:NS, 0:NH], sm["col"][0:NS, :].rearrange("p (b h) -> p h b", b=NS), AX, ALU.add))
                dve.tensor_tensor(s_prod[:, :].rearrange("p (h d) -> p h d", h=NH), v_s[:, :].rearrange("p (h d) -> p h d", h=NH),
                                  sm["den"][0:NS, 0:NH].unsqueeze(2).to_broadcast([NS, NH, HD]), ALU.mult).then_inc(ev("new_v"), 1)

                def masked_scores(h):
                    for j in range(4):
                        v = probs[:, h % 2, PJ[j]:PJ[j] + (j + 1) * 128]
                        c = 4 * h + j
                        dve.wait_ge(ev("scores_done"), 8 * h + j + 1)
                        dve.wait_ge(ev("bias_done"), c + 1)
                        dve.scalar_tensor_tensor(v, ps[:, j % 2, 0:(j + 1) * 128], QSCALE, v, ALU.mult, ALU.add
                                                 ).then_inc(ev("score_read"), 1)
                        dve.wait_ge(ev("score_read"), 8 * h + j + 1)
                        chain(dve.tensor_tensor(v[:, j * 128:], v[:, j * 128:], causal, ALU.add))
                        dve.tensor_reduce(n_max[:, c:c + 1], v, AX, ALU.max, negate=True).then_inc(ev("max_done"), 1)
                    dve.wait_ge(ev(f"decay_in{h % 2}"), 16 * (h // 2 + 1))
                    if h >= 2:
                        dve.wait_ge(ev("ret_av"), h - 1)
                    for k in range(4):
                        w = SEQ - k * 128
                        dve.wait_ge(ev("scores_done"), 8 * h + k + 5)
                        dve.tensor_tensor(ret_a[h % 2][:, AK[k]:AK[k] + w], ps[:, k % 2, 0:w], decay[:, h % 2, 0:w], ALU.mult
                                          ).then_inc(ev("score_read"), 1)

                def normalise(h):
                    dve.wait_ge(ev("exp_done"), 4 * h + 4)
                    chain(dve.reciprocal(row_sum[:, 4 * h:4 * h + 4], row_sum[:, 4 * h:4 * h + 4]))
                    for j in range(4):
                        v = probs[:, h % 2, PJ[j]:PJ[j] + (j + 1) * 128]
                        dve.tensor_scalar(v, v, row_sum[:, 4 * h + j:4 * h + j + 1], None, ALU.mult).then_inc(ev("p_ready"), 1)

                dve.wait_ge(ev("state_stored"), 32)
                dve.wait_ge(ev("ret_s_made"), 1)
                masked_scores(0)
                normalise(0)
                for h in range(NH):
                    if h + 1 < NH:
                        masked_scores(h + 1)
                    dve.wait_ge(ev("v_used"), 2 * h + 2)
                    dve.tensor_tensor(own[h].rearrange("p (h d) -> p h d", h=NH),
                                      ps[0:NH, 7, :].rearrange("p (h d) -> p h d", h=NH),
                                      delta[:, :, 0:1].to_broadcast([NH, NH, HD]), ALU.mult).then_inc(ev("own_kept"), 1)
                    if h + 1 < NH:
                        normalise(h + 1)
                    if h % 2:
                        m = h // 2
                        dve.wait_ge(ev("ret_av"), h + 1)
                        dve.tensor_copy(proj[:, VR + m, 0:SEQ], ps[:, 5, :]).then_inc(ev("o_read"), 1)
                        dve.wait_ge(ev("fox_av"), h + 1)
                        dve.tensor_copy(proj[:, VF + m, 0:SEQ], ps[:, 4, :]).then_inc(ev("o_read"), 1)
                dve.wait_ge(ev("own_rows"), 1)
                dve.wait_ge(ev("new_v"), 1)
                dve.tensor_tensor(s_prod[:, :], s_prod[:, :], ps[0:NS, 0, :], ALU.add).then_inc(ev("fox_rows"), 1)
                dve.wait_ge(ev("fox_s_t"), 1)
                dve.tensor_copy(proj[:, VF:VF + 4, SEQ:NTOK], ps[:, 1, 0:32].rearrange("p (m b) -> p m b", m=4)
                                ).then_inc(ev("fox_s_done"), 1)
                for m in range(4):
                    tile = proj[:, VR + m]
                    dve.wait_ge(ev("hn_mean"), m + 1)
                    dve.tensor_tensor(tile.rearrange("p (h c) -> p h c", h=2), tile.rearrange("p (h c) -> p h c", h=2),
                                      pair(m % 2), ALU.subtract).then_inc(ev("hn_centred"), 1)
                    dve.wait_ge(ev("hn_dev_done"), m + 1)
                    chain(dve.reciprocal(hn_dev[:, m % 2, :], hn_dev[:, m % 2, :]))
                    then("hn_scaled", dve.tensor_tensor(tile, tile, hn_dev[:, m % 2, :], ALU.mult), m + 1)
                    dve.wait_ge(ev("gate_silu"), m + 1)
                    dve.tensor_tensor(tile, tile, proj[:, GR + m], ALU.mult).then_inc(ev("hn_gated"), 1)
                for t in range(KT):
                    dve.wait_ge(ev("cat_hi"), t + 1)
                    dve.tensor_tensor(h_lo[:, t, :, 0:HP], mixed_tile(t)[:, 0:SEQ].rearrange("p (h c) -> p h c", h=2),
                                      h_hi[:, t, :, 0:HP].bitcast(F32), ALU.subtract).then_inc(ev("cat_lo"), 1)
                for u, first in enumerate((VF, VR)):
                    dve.wait_ge(ev("cat_hi"), KT + u + 1)
                    dve.tensor_tensor(h_lo[:, 4 * u:4 * u + 4, :, HP:HT],
                                      proj[:, first:first + 4, SEQ:NTOK].rearrange("p t (h c) -> p t h c", h=2),
                                      h_hi[:, 4 * u:4 * u + 4, :, HP:HT].bitcast(F32), ALU.subtract).then_inc(ev("cat_lo"), 1)

            def odd_dve():
                c0 = chunks_before(ODD)
                past = params[:, 384:512].rearrange("p (b j t) -> p j b t", b=NS, j=2)
                chain(dve.memset(up[:, 0:2], 0.0))
                dve.tensor_copy(tail_s[:, :, 0, :], past[:, 1]).then_inc(ev("conv_steps"), 1)
                half2 = lambda v: v.rearrange("p (h c) -> p h c", h=2)

                def body(i):
                    for j in range(2):
                        m = i * 2 + j
                        s0 = m * 12 + 1
                        w = [params[:, bass.ds(m + (CONV_W + 8 * q), 1)] for q in range(3)]

                        steps = ev("conv_steps")
                        dve.wait_ge(steps, s0)
                        dve.wait_ge(ev("cg_copied"), m + 1)
                        dve.wait_ge(chunk_used, c0 + i * 6 + 3 * j + 3)
                        dve.tensor_tensor(half2(up[:, 2:2 + SEQ]), cg[:, :, 0:HP], ps[:, 2:4, 0:HP], ALU.mult).then_inc(steps, 1)
                        dve.tensor_tensor(half2(up_s[:, :]), cg[:, :, HP:HT], ps[:, 2:4, HP:HT], ALU.mult).then_inc(steps, 1)
                        dve.wait_ge(steps, s0 + 1)
                        dve.tensor_scalar(z[:, :], up[:, 2:2 + SEQ], w[2], None, ALU.mult).then_inc(steps, 1)
                        dve.wait_ge(steps, s0 + 3)
                        dve.scalar_tensor_tensor(z[:, :], up[:, 1:1 + SEQ], w[1], z[:, :], ALU.mult, ALU.add).then_inc(steps, 1)
                        dve.wait_ge(steps, s0 + 4)
                        dve.scalar_tensor_tensor(z[:, :], up[:, 0:SEQ], w[0], z[:, :], ALU.mult, ALU.add).then_inc(steps, 1)
                        old = [past[:, q, :, bass.ds(m, 1)].rearrange("p b a -> p (b a)") for q in range(2)]
                        dve.tensor_scalar(z_s[:, :], up_s[:, :], w[2], None, ALU.mult).then_inc(steps, 1)
                        dve.wait_ge(steps, s0 + 6)
                        dve.scalar_tensor_tensor(z_s[:, :], old[1], w[1], z_s[:, :], ALU.mult, ALU.add).then_inc(steps, 1)
                        dve.wait_ge(steps, s0 + 7)
                        dve.scalar_tensor_tensor(z_s[:, :], old[0], w[0], z_s[:, :], ALU.mult, ALU.add).then_inc(steps, 1)
                        dve.wait_ge(steps, s0 + 8)
                        if not is_first(i):
                            dve.wait_ge(ev("mixed_hi"), m - 1)
                        dve.tensor_tensor(mixed[:, j, :, 0:HP], half2(z[:, :]), ps[:, 4 + 2 * j:6 + 2 * j, 0:HP], ALU.mult).then_inc(steps, 1)
                        dve.tensor_tensor(mixed[:, j, :, HP:HT], half2(z_s[:, :]), ps[:, 4 + 2 * j:6 + 2 * j, HP:HT], ALU.mult).then_inc(steps, 1)
                        dve.tensor_copy(tail_p[:, :, bass.ds(m, 1)].rearrange("p j a -> p (j a)"), up[:, SEQ:SEQ + 2]).then_inc(steps, 1)
                        dve.tensor_copy(tail_s[:, :, 1, bass.ds(m, 1)].rearrange("p b a -> p (b a)"), up_s[:, :]).then_inc(steps, 1)
                        dve.wait_ge(ev("mixed_hi"), m + 1)
                        t = bass.ds(m, 1)
                        dve.tensor_tensor(mix_lo[:, t].rearrange("p a h c -> p (a h) c"), mixed[:, j],
                                          mix_hi[:, t].rearrange("p a h c -> p (a h) c").bitcast(F32), ALU.subtract
                                          ).then_inc(ev("mixed_lo"), 1)
                loop(dve, True, KT // 2, body)

            dve.wait_ge(params_t, 1)
            for k, r in ((0, 128), (1, 112), (2, 96), (3, 128)):
                dve.tensor_copy(params[:, k * 128:k * 128 + r], ps[:, 0, k * 128:k * 128 + r]).then_inc(params_ready, 1)
            dve.wait_ge(params_ready, 4)
            dve.tensor_copy(c_t[:, :, :], params[:, C_AT:C_AT + 72].rearrange("p (b t) -> p t b", b=9)).then_inc(c_ready, 1)
            modulation(0)
            modulate(0)
            dve.wait_ge(ada_used, MT)
            gate(0)
            for n in range(last):
                if n in FFN:
                    f0 = FT * ffns_before(n)

                    def body(i):
                        for j in range(2):
                            dve.wait_ge(chunk_used, chunks_before(n) + i * 4 + 2 * j + 2)
                            dve.wait_ge(silu_done, f0 + i * 2 + j + 1)
                            if not (n == 0 and is_first(i)):
                                dve.wait_ge(hid_hi_done, f0 + i * 2 + j - 1)
                            dve.tensor_tensor(gated[:, j], silu_a[:, j], pair(2 * j + 1), ALU.mult).then_inc(gate_done, 1)
                            dve.wait_ge(hid_hi_done, f0 + i * 2 + j + 1)
                            m = bass.ds(i * 2 + j, 1)
                            dve.tensor_tensor(hid_lo[:, m].rearrange("p a h c -> p (a h) c"), gated[:, j],
                                              hid_hi[:, m].rearrange("p a h c -> p (a h) c").bitcast(F32),
                                              ALU.subtract).then_inc(hid_lo_done, 1)
                    loop(dve, n == 0, FT // 2, body)
                    residuals(n, lambda i, j: dve.wait_ge(chunk_used, chunks_before(n, True) + i * 4 + 2 * j + 2))
                else:
                    (even_dve if n == EVEN else odd_dve)()
                    residuals(n, lambda i, j: dve.wait_ge(chunk_used, chunks_before(n, True) + i * 2 + j + 1))
                if n + 1 < last:
                    modulation(n + 1)
                norm(n)
                if n + 1 < last:
                    modulate(n + 1)
            dve.wait_ge(ln_done, KT * last)
            dve.tensor_copy(samp_t[:, :, :].rearrange("p t (h c) -> p t h c", h=2), x[:, :, :, HP:HT]).then_inc(samp_out, 1)


INPUTS = ["x_prompt", "x_sample", "cache_k", "cache_v", "cache_logf", "state_ret", "state_conv", "page_table",
          "c_prompt", "c_sample", "w_ada", "b_ada", "w_ffn_in", "w_ffn_out", "ln_g", "ln_b", "w_in_even",
          "b_forget", "w_out_even", "w_in_odd", "conv_w", "w_out_odd"]
OUTPUTS = [("y_prompt", (1, SEQ, D)), ("y_sample", (NS, 1, D)),
           ("k_prompt", (1, 1, SEQ, NH, HD)), ("v_prompt", (1, 1, SEQ, NH, HD)), ("logf_prompt", (1, 1, SEQ, NH)),
           ("ret_prompt", (1, 1, NH, HD, HD)), ("conv_prompt", (1, 1, 2, D)),
           ("k_sample", (1, NS, 1, NH, HD)), ("v_sample", (1, NS, 1, NH, HD)), ("logf_sample", (1, NS, 1, NH)),
           ("ret_sample", (1, NS, NH, HD, HD)), ("conv_sample", (1, NS, 2, D))]


def kernel(**inputs):
    from concourse import bacc as _bacc
    from concourse.bass_utils import run_bass_kernel_spmd

    nc = _bacc.Bacc("TRN2", target_bir_lowering=False, num_devices=1, dynamic_dma_scratch_size=1024)
    arrays = {name: np.ascontiguousarray(inputs[name]) for name in INPUTS}
    arrays.update(zip(("t_res", "t_even", "t_decay"), host_tables()))
    a = {name: nc.dram_tensor(name, v.shape, mybir.dt.from_np(v.dtype), kind="ExternalInput").ap()
         for name, v in arrays.items()}
    out = {name: nc.dram_tensor("out_" + name, shape, mybir.dt.float32, kind="ExternalOutput").ap()
           for name, shape in OUTPUTS}
    build_step(nc, a, out)
    result = run_bass_kernel_spmd(nc, [arrays], core_ids=[0])
    return tuple(result.results[0]["out_" + name].reshape(shape) for name, shape in OUTPUTS)
```

```python
import concourse.bass as bass
from concourse import mybir
from contextlib import ExitStack
import numpy as np

D = 1024
KT = D // 128
SEQ = 512
NS = 8
HP, HS = SEQ // 2, NS // 2
HT = HP + HS
NTOK = SEQ + NS
DFF = 2816
FT = DFF // 128
FH = FT // 2
NSUB = 6
MT = 3 * KT
ALPHA = 4.0 ** 0.25
LN_EPS = 1e-5
GN_EPS = 1e-6
NH = 8
HD = 64
FOXW = NH * HD
PAGE = 128
NPG = 8
QSCALE = HD ** -0.5
SQUARES_WITH = {4: (0, 1), 5: (2, 3), 6: (4, 5, 6), 7: (7,)}
LAG = 4
CENTRE = 1
NADA = 3
ADA_W = 256
GROUPS = MT * 128 // ADA_W
PIECES = {2: ((0, 1), (2,), (3, 4), (5,)), 1: ((0, 1, 2), (3, 4, 5))}
FFN = (0, 2, 3, 5)
EVEN, ODD = 1, 4
CH_IN = {0: 2 * FT, 1: 28, 2: 2 * FT, 3: 2 * FT, 4: 24, 5: 2 * FT}
CH_OUT = {0: 2 * KT, 1: KT, 2: 2 * KT, 3: 2 * KT, 4: KT, 5: 2 * KT}


def chunks_before(n, second=False):
    return sum(CH_IN[i] + CH_OUT[i] for i in range(n)) + (CH_IN[n] if second else 0)


def mod_steps_before(n):
    return 4 + 7 * (n - 1) if n else 0


def ffns_before(n):
    return sum(1 for i in FFN if i < n)


def host_tables():
    p = np.arange(128)
    f = np.float32
    ident = np.eye(128, dtype=f)
    ones = np.ones((128, 128), f)
    sel = np.zeros((128, 8, 128), f)
    for r in range(8):
        sel[r, r, :] = 1
    delta = np.zeros((128, 8, 8), f)
    for r in range(8):
        delta[r, r, :] = 1
    lg = np.log(f(1.0) - f(2.0) ** (f(-5.0) - np.arange(NH, dtype=f))).astype(f)
    gdec = np.zeros((128, 4), f)
    for m in range(4):
        gdec[:64, m] = np.exp(lg[2 * m])
        gdec[64:, m] = np.exp(lg[2 * m + 1])
    tail = np.zeros((128, 4, 8), f)
    for j in range(4):
        for h in range(8):
            tail[:, j, h] = np.exp((f(SEQ - 1.0) - (128 * j + p).astype(f)) * lg[h])
    heads = np.zeros((128, 544), f)
    for m in range(4):
        heads[:64, m * 8 + 2 * m] = heads[64:, m * 8 + 2 * m + 1] = 1.0 / HD
        heads[2 * m, 32 + m * 128:32 + m * 128 + 64] = heads[2 * m + 1, 32 + m * 128 + 64:32 + m * 128 + 128] = 1
    bd = np.zeros((128, 128), f)
    bd[:64, :64] = bd[64:, 64:] = 1.0 / HD
    unit = np.zeros((128, 8, 8), f)
    unit[:, np.arange(8), np.arange(8)] = 1
    two_parts = np.zeros((128, 9), f)
    two_parts[np.arange(18), np.arange(18) % 9] = 1
    res = np.concatenate([ident, ones, ones / D, p[:, None].astype(f), gdec, tail.reshape(128, 32),
                          delta.reshape(128, 64), sel.reshape(128, 1024), bd, unit.reshape(128, 64), two_parts], axis=1)
    tri = np.zeros((128, 896), f)
    tri[np.arange(896)[None, :] - 384 >= p[:, None]] = 1
    strict = (p[:, None] > p[None, :]).astype(f)
    causal = np.where(p[None, :] <= p[:, None], f(0), f(-1e30)).astype(f)
    perm = np.zeros((128, 128), f)
    for d in range(128):
        perm[d, (d + 32) % 64 + 64 * (d // 64)] = 1
    inv = (f(1.0) / (f(10000.0) ** np.linspace(0.0, 1.0, 32, dtype=f))).astype(f)
    pos = np.concatenate([np.arange(SEQ), np.full(NS, NPG * PAGE)]).astype(f)
    ang = (pos[:, None] * inv[None, :]).astype(f).T
    cos = np.tile(np.cos(ang), (4, 1)).astype(f)
    sin = np.concatenate([-np.sin(ang), np.sin(ang)] * 2, axis=0).astype(f)
    even = np.concatenate([tri, strict, causal, perm, cos, sin], axis=1)
    decay = np.zeros((NH, 128, SEQ), f)
    diff = np.arange(SEQ)[None, :] - p[:, None]
    for h in range(NH):
        decay[h] = np.where(diff >= 0, np.exp(np.maximum(diff, 0).astype(f) * lg[h]), f(0))
    return res.astype(f), even.astype(f), decay, heads


def build_step(nc, a, out, last=NSUB):
    F32 = mybir.dt.float32
    F32R = mybir.dt.float32r
    I32 = mybir.dt.int32
    ALU = mybir.AluOpType
    ACT = mybir.ActivationFunctionType
    AX = mybir.AxisListType.X
    n_phys = a["cache_k"].shape[1]

    ctx = ExitStack()
    with ctx:
        top = [(nc.sbuf_base + 31) // 32 * 32]

        def region(size):
            at = top[0]
            top[0] += (size + 31) // 32 * 32
            assert top[0] <= nc.sbuf_usable_end, (top[0], nc.sbuf_usable_end)
            return at

        def put(name, shape, dt, at):
            return nc.alloc_sbuf_tensor_at(name, shape, dt, offset=at)

        def new(name, shape, dt=F32):
            size = 4
            for s in shape[1:]:
                size *= s
            return put(name, shape, dt, region(size))

        def sem(name):
            return ctx.enter_context(nc.semaphore(name))

        x = new("x", [128, KT, 2, HT])
        R_H = region(2 * 4 * KT * NTOK)
        h_hi = put("h_hi", [128, KT, 2, HT], F32R, R_H)
        h_lo = put("h_lo", [128, KT, 2, HT], F32R, R_H + 4 * KT * NTOK)
        R_HID = region(2 * 4 * FT * NTOK)
        hid_hi = put("hid_hi", [128, FT, 2, HT], F32R, R_HID)
        hid_lo = put("hid_lo", [128, FT, 2, HT], F32R, R_HID + 4 * FT * NTOK)
        raw = new("raw", [128, 2, FH, 128])
        w_hi = new("w_hi", [128, 2, FH, 128], F32R)
        w_lo = new("w_lo", [128, 2, FH, 128], F32R)
        R_ADA = region(4 * 4096)
        ada_w = put("ada_w", [128, NADA, KT // 2, ADA_W], F32, R_ADA)
        ada_sums = put("ada_sums", [18, ADA_W], F32, R_ADA + NADA * 4096)
        ada_parts = {place: tuple(put(f"ada_{part}_{name}", [128, NADA, KT // 2, ADA_W], F32R, at + u * NADA * 4096)
                                  for u, part in enumerate(("hi", "lo")))
                     for place, name, at in ((False, "h", R_H), (True, "proj", R_HID))}
        R_TMP = region(5 * 4 * NTOK)
        ada_rows = put("ada_rows", [9, 4, 512], F32, R_TMP)
        x_rows = put("x_rows", [128, 4, D], F32, R_H)
        p_rows = put("p_rows", [128, 4, 128], F32, R_H + 16384)
        s_rows = put("s_rows", [NS, D], F32, R_H + 16384 + 2048)
        ada_first = put("ada_first", [128, 4, KT, 512], F32, R_HID + 4 * KT * NTOK)
        ada_fifth = put("ada_fifth", [128, KT, 512], F32, R_ADA)
        h32 = put("h32", [128, KT, 2, HT], F32, R_HID)
        y_rows = put("y_rows", [128, 4, D], F32, R_HID)
        ys_rows = put("ys_rows", [NS, D], F32, R_HID + 16384)
        silu_a = put("silu_a", [128, 2, 2, HT], F32, R_TMP)
        gated = put("gated", [128, 2, 2, HT], F32, R_TMP + 8 * NTOK)
        tile_sum = put("tile_sum", [128, 2, HT], F32, R_TMP)
        mean = put("mean", [128, 2, HT], F32, R_TMP)
        shift = put("shift", [128, 2, HT], F32, R_TMP + 4 * NTOK)
        sq_sum = put("sq_sum", [128, 2, HT], F32, R_TMP + 8 * NTOK)
        rdev = put("rdev", [128, 2, HT], F32, R_TMP + 8 * NTOK)
        sq = put("sq", [128, 2, 2, HT], F32, R_TMP + 12 * NTOK)
        dev = sq[:, 0]

        res = new("res", [128, 1710])
        ident, ones, mean_w = res[:, 0:128], res[:, 128:256], res[:, 256:384]
        lane, gdec = res[:, 384:385], res[:, 385:389]
        tail = res[:, 389:421].rearrange("p (j h) -> p j h", j=4)
        delta = res[0:8, 421:485].rearrange("p (b h) -> p b h", b=8)
        sel = res[0:8, 485:1509].rearrange("p (r c) -> p r c", r=8)
        head_mean = res[:, 1509:1637]
        two_parts = res[0:18, 1701:1710]
        unit = res[0:8, 1637:1701].rearrange("p (b c) -> p b c", b=8)
        params = new("params", [128, 4 * 128])
        c_t = new("c_t", [128, KT, 9])
        c_act = new("c_act", [128, KT, 9])
        c_parts = new("c_parts", [128, KT, 18], F32R)
        mod = new("mod", [128, 2, MT, 9])
        mod_b = new("mod_b", [128, KT, 9])
        samp8 = new("samp8", [128, 8])
        samp_t = new("samp_t", [128, KT, 8])
        eps_ln = new("eps_ln", [128, 1])
        LN_G, LN_B, CONV_W, C_AT = 144, 192, 256, 280

        QF, KF, VF, QR, KR, VR, GR = range(0, 28, 4)
        proj = put("proj", [128, 28, NTOK], F32, R_HID)
        R_TOK = R_HID + 28 * 4 * NTOK
        kf_tok, vf_tok, vr_tok, kr_tok = (put(t, [128, 4, FOXW], F32, R_TOK + 8192 * u)
                                          for u, t in enumerate(("kf_tok", "vf_tok", "vr_tok", "kr_tok")))
        q_all = put("q_all", [128, NS, FOXW], F32, R_TOK)
        logf_pool = put("logf_pool", [n_phys, PAGE, NH], F32, R_TOK + 16384)
        page_ids = put("page_ids", [n_phys, NS * NPG], I32, R_TOK + 20480)
        page_f = put("page_f", [n_phys, NS * NPG], F32, R_TOK + 20736)
        one_hot = put("one_hot", [n_phys, NS * NPG], F32, R_TOK + 20992)
        q_s = put("q_s", [NS, FOXW], F32, R_TOK + 24576)
        s_prod = put("s_prod", [NS, FOXW], F32, R_TMP + 8192)
        R_PT = R_H + 4 * 2320
        even_t = put("even_t", [128, 2320], F32, R_H)
        tri, strict, causal, perm = even_t[:, 0:896], even_t[:, 896:1024], even_t[:, 1024:1152], even_t[:, 1152:1280]
        cos_t, sin_t = even_t[:, 1280:1800], even_t[:, 1800:2320]
        own_parts = [put(t, [NH, n, FOXW], F32, at) for t, n, at in
                     (("own_a", 4, R_TOK + 24576), ("own_b", 2, R_H), ("own_c", 2, R_H + 4 * 1280))]
        own = [part[:, i, :] for part, n in zip(own_parts, (4, 2, 2)) for i in range(n)]
        k_s, v_s, vr_s = (put(t, [NS, FOXW], F32, R_PT + 2048 * u) for u, t in enumerate(("k_s", "v_s", "vr_s")))
        later = put("later", [128, NS * NH, NPG], F32, R_PT + 6144)
        p_t = put("p_t", [128, 4, SEQ], F32, R_PT)
        kv_s = put("kv_s", [128, NS, 4, HD], F32, R_PT + 8192)
        probs = put("probs", [128, 2, 1280], F32, R_PT + 8192)
        ret_a1 = put("ret_a1", [128, 1280], F32, R_PT + 8192 + 10240)
        state = put("state", [128, NS, 4, HD], F32, R_TMP)
        ret_a0 = put("ret_a0", [128, 1280], F32, R_TMP)
        ret_a = (ret_a0, ret_a1)
        rot = put("rot", [128, 2, NTOK], F32, R_PT + 8192)
        hn_sq = put("hn_sq", [128, 2, NTOK], F32, R_TMP)
        hn_dev = put("hn_dev", [NH, NTOK], F32, R_TMP + 8 * NTOK)
        heads_t = put("heads_t", [128, 544], F32, R_TOK)
        to_row = heads_t[:, 0:32].rearrange("p (m h) -> p m h", m=4)
        from_row = heads_t[0:8, 32:544].rearrange("p (m c) -> p m c", m=4)
        pages = put("pages", [128, 2, 4, FOXW], F32, R_ADA)
        decay = new("decay", [128, 2, SEQ])
        c_heads = new("c_heads", [NH, SEQ])
        s_samp = new("s_samp", [128, NS, NH, NPG])
        lf_past = new("lf_past", [128, NS, NH, NPG])
        page_row = new("page_row", [1, NS * NPG], I32)
        w_fg = new("w_fg", [128, KT, NH])
        fg_hi = new("fg_hi", [128, KT, NH], F32R)
        fg_lo = new("fg_lo", [128, KT, NH], F32R)
        fg_rows = put("fg_rows", [NH, NTOK], F32, R_TMP + 8192)
        b_fg = new("b_fg", [128, NH])
        logf, lf_a, lf_b = (put(t, [128, 5, NH], F32, R_TOK + 32768 + 160 * u) for u, t in enumerate(("logf", "lf_a", "lf_b")))
        c_cols, n_max, row_sum = (put(t, shape, F32, R_PT + 8192 + 10240 + 5120 + 128 * u) for u, (t, shape) in enumerate(
            (("c_cols", [128, 4, NH]), ("n_max", [128, NH * 4]), ("row_sum", [128, NH * 4]))))
        ret_state = new("ret_state", [128, 4, HD])
        sm = {t: new("sm_" + t, [128, 64]) for t in ("new", "max", "den", "col")}
        eps_gn = new("eps_gn", [128, 1])
        PJ = (0, 128, 384, 768)
        AK = (0, 512, 896, 1152)
        mix_hi = put("mix_hi", [128, KT, 2, HT], F32R, R_HID)
        mix_lo = put("mix_lo", [128, KT, 2, HT], F32R, R_HID + 4 * KT * NTOK)
        R_ODD = R_HID + 8 * KT * NTOK
        cg = put("cg", [128, 2, HT], F32, R_ODD)
        up = put("up", [128, 2 + SEQ], F32, R_ODD + 2080)
        up_s = put("up_s", [128, NS], F32, R_ODD + 4160)
        z = put("z", [128, SEQ], F32, R_ODD + 4224)
        z_s = put("z_s", [128, NS], F32, R_ODD + 6272)
        mixed = put("mixed", [128, 2, 2, HT], F32, R_ODD + 6336)
        tail_s = put("tail_s", [128, NS, 2, KT], F32, R_ODD + 10496)
        tail_p = put("tail_p", [128, 2, KT], F32, R_ODD + 11008)
        tail_rows = put("tail_rows", [128, 2, 128], F32, R_ODD + 11072)

        ps = ctx.enter_context(nc.psum_tensor("ps", [128, 8, 512], F32))

        def pair(q):
            return ps[:, 2 * q:2 * q + 2, 0:HT]

        consts_in = sem("consts_in")
        rows_in = sem("rows_in")
        x_rows_in = sem("x_rows_in")
        eps_ready = sem("eps_ready")
        params_t = sem("params_t")
        params_ready = sem("params_ready")
        c_ready = sem("c_ready")
        cond_ready = sem("cond_ready")
        x_t = sem("x_t")
        x_copied = sem("x_copied")
        raw_full = [sem(f"raw_full{k}") for k in range(2)]
        hi_cut = sem("hi_cut")
        chunk_cut = sem("chunk_cut")
        chunk_used = sem("chunk_used")
        ada_full = [sem(f"ada_full{k}") for k in range(NADA)]
        ada_used = sem("ada_used")
        mod_steps = sem("mod_steps")
        silu_done = sem("silu_done")
        gate_done = sem("gate_done")
        hid_hi_done = sem("hid_hi_done")
        hid_lo_done = sem("hid_lo_done")
        drained = sem("drained")
        samp_added = sem("samp_added")
        summed = sem("summed")
        mean_done = sem("mean_done")
        half_summed = sem("half_summed")
        shift_ready = sem("shift_ready")
        shifted = sem("shifted")
        squared = sem("squared")
        sq_added = sem("sq_added")
        mean_ready = sem("mean_ready")
        delta_steps = sem("delta_steps")
        centred = [sem("centred_dve"), sem("centred_pool")]
        first_full = [sem(f"first_full{k}") for k in range(6)]
        var_done = sem("var_done")
        dev_done = sem("dev_done")
        rdev_done = sem("rdev_done")
        normed = sem("normed")
        ln_done = sem("ln_done")
        h32_done = sem("h32_done")
        h32_samp = sem("h32_samp")
        samp_mod = sem("samp_mod")
        samp_out = sem("samp_out")
        rows_made = sem("rows_made")
        rows_copied = sem("rows_copied")
        ada_hi_cut = sem("ada_hi_cut")
        ada_cut = sem("ada_cut")
        ada_turned = sem("ada_turned")
        h_hi_done = sem("h_hi_done")
        h_lo_done = sem("h_lo_done")
        y_t = sem("y_t")
        y_copied = sem("y_copied")
        stored = sem("stored")
        named = {}

        def ev(name):
            if name not in named:
                named[name] = sem(name)
            return named[name]

        page_full = [sem(f"page_full{k}") for k in range(2)]
        for name in ("copied", "k_read", "v_used", "score_read", "scores_done", "bias_done", "max_done", "exp_done",
                     "s_turned", "s_reduced", "p_ready", "pt_done", "pt_copied", "fox_av", "ret_av", "c_spread", "o_read", "decay_in0",
                     "decay_in1", "chained", "conv_steps", "cg_copied", "mixed_hi", "mixed_lo", "k_prod"):
            ev(name)
        block = ctx.enter_context(nc.Block())
        n_stored = [0]

        def store(eng, dst, src):
            eng.dma_start(dst, src).then_inc(stored, 16)
            n_stored[0] += 1

        def loop(eng, first, count, body):
            if first:
                body(0)
            with eng.Fori(1 if first else 0, count) as i:
                body(i)

        def is_first(i):
            return isinstance(i, int) and i == 0

        def mixed_tile(t):
            return proj[:, (VF + t) if t < 4 else (VR + t - 4)]

        products = [(n, second) for n in range(last) for second in (False, True)]

        def tiles_of_product(n, second):
            return FH if second and n in FFN else KT

        def next_tiles(n, second):
            k = products.index((n, second)) + 1
            return tiles_of_product(*products[k]) if k < len(products) else None

        def w_view(w):
            return w.rearrange("(t p) n -> p t n", p=128)

        ffn_in = {n: w_view(a["w_ffn_in"][n // 3, (n % 3) // 2]) for n in FFN}
        ffn_out = {n: w_view(a["w_ffn_out"][n // 3, (n % 3) // 2]) for n in FFN}

        even_in = w_view(a["w_in_even"][0])
        mixer_out = {EVEN: w_view(a["w_out_even"][0]), ODD: w_view(a["w_out_odd"][0])}
        odd_in = w_view(a["w_in_odd"][0])
        cache_k = a["cache_k"][0].rearrange("g s h d -> g s (h d)")
        cache_v = a["cache_v"][0].rearrange("g s h d -> g s (h d)")

        def ada_view(n):
            return w_view(a["w_ada"][n // 3])[:, :, (n % 3) * MT * 128:(n % 3 + 1) * MT * 128]

        def first_ada(g):
            return ada_fifth[:, :, :] if g == 4 else ada_first[:, g % 5]

        def centre(eng, n, part):
            eng.wait_ge(mean_ready, n + 1)
            for t in range(*((0, CENTRE), (CENTRE, KT if n + 1 == last else KT - 1))[part]):
                centre_tile(eng, t, part)

        def centre_tile(eng, t, part):
            eng.tensor_tensor(x[:, t], x[:, t], mean[:, :, :], ALU.subtract).then_inc(centred[part], 1)

        def low_pieces(eng, n, i, now):
            hi, lo = ada_parts[n == EVEN]
            for q in now:
                eng.wait_ge(ada_hi_cut, n * MT + i * 6 + q + 1)
                eng.tensor_tensor(lo[:, q % NADA], ada_w[:, q % NADA], hi[:, q % NADA].bitcast(F32),
                                  ALU.subtract).then_inc(ada_cut, 1)

        two = lambda v: v.rearrange("p (h c) -> p h c", h=2)

        def modulate_samples(pool, n):
            m = n % 2
            pool.wait_ge(mod_steps, mod_steps_before(n) + (5 if n else 2))
            if n == 0:
                pool.wait_ge(x_copied, KT + 1)
            for t in range(KT):
                if n:
                    pool.wait_ge(normed, KT * (n - 1) + t + 1)
                pool.tensor_tensor(two(samp_t[:, t]), x[:, t, :, HP:HT], two(mod[:, m, KT + t, 1:9]), ALU.mult
                                   ).then_inc(samp_mod, 1)
                pool.wait_ge(samp_mod, KT * n + t + 1)
                pool.tensor_tensor(h32[:, t, :, HP:HT], two(samp_t[:, t]), two(mod[:, m, t, 1:9]), ALU.add
                                   ).then_inc(h32_samp, 1)
                if n and t == 0:
                    centre_tile(pool, KT - 1, 1)

        @block.sync
        def _(sp):
            def chunk(c, k, src, kt):
                if not (isinstance(c, int) and c < 2):
                    sp.wait_ge(chunk_cut, c - 1)
                sp.dma_start(raw[:, k, 0:kt, :], src).then_inc(raw_full[k], 16)

            def pieces(n, i, pieces_now):
                for q in pieces_now:
                    c = (n - 1) * MT + i * 6 + q
                    if not (n == 1 and is_first(i) and q < NADA):
                        sp.wait_ge(ada_cut, c - NADA + 1)
                    half = q % 2 * (KT // 2)
                    sp.dma_start(ada_w[:, q % NADA, :, :],
                                 ada_view(n)[:, half:half + KT // 2, bass.ds(i * 3 * ADA_W + q // 2 * ADA_W, ADA_W)]
                                 ).then_inc(ada_full[q % NADA], 16)

            def even_loads(chunk):
                c0 = chunks_before(EVEN)
                for k in range(2):
                    chunk(c0 + k, k, even_in[:, :, k * 128:(k + 1) * 128], KT)
                sp.dma_start(w_fg[:, :, :], even_in[:, :, 3 * FOXW:3 * FOXW + NH]).then_inc(ev("fg_in"), 16)
                sp.dma_start(b_fg[:, :], a["b_forget"][0].partition_broadcast(128)).then_inc(ev("fg_in"), 16)
                def columns(i, m0):
                    for k in range(2):
                        m = i * 2 + k
                        chunk(c0 + m, k, even_in[:, :, bass.ds(m * 128 + (NH if m0 >= 12 else 0), 128)], KT)

                def granule(cache, b, k):
                    for u in range(4):
                        page = sp.value_load(page_row[0:1, bass.ds(b * NPG + 4 * k + u, 1)], min_val=0, max_val=n_phys - 1)
                        sp.dma_start(pages[:, k, u, :], cache[bass.ds(page, 1)].rearrange("g s c -> s (g c)")
                                     ).then_inc(page_full[k], 16)

                columns(1, 0)
                sp.wait_ge(h32_done, KT * 2)
                sp.wait_ge(h_lo_done, KT * 2)
                sp.dma_start(page_row[:, :], a["page_table"].rearrange("b g -> (b g)").unsqueeze(0)).then_inc(ev("ids_in"), 16)
                sp.dma_start(page_ids[:, :], a["page_table"].rearrange("b g -> (b g)").partition_broadcast(n_phys)).then_inc(ev("pool_in"), 16)
                sp.dma_start(logf_pool[:, :, :], a["cache_logf"][0]).then_inc(ev("pool_in"), 16)
                sp.wait_ge(ev("ids_in"), 16)
                sp.wait_ge(ada_used, MT * 2)
                for k in range(2):
                    granule(cache_k, 0, k)
                columns(2, 0)
                for i0, i1, m0 in ((3, 6, 0), (6, 10, 12)):
                    with sp.Fori(i0, i1) as i:
                        columns(i, m0)
                        for k in range(2):
                            sp.wait_ge(ev("k_read"), i * 2 + k - 5)
                            granule(cache_k, i - 2, k)
                with sp.Fori(10, 14) as i:
                    columns(i, 12)
                sp.wait_ge(chunk_used, c0 + 28)
                sp.wait_ge(ev("gates_pe"), 4)
                sp.dma_start(even_t[:, :], a["t_even"]).then_inc(ev("tables_in"), 16)
                st = a["state_ret"][0].rearrange("b (m t) d e -> t d b m e", t=2)
                for t in range(2):
                    sp.dma_start(state[64 * t:64 * t + 64], st[t]).then_inc(ev("state_in"), 16)
                for h in range(2):
                    sp.dma_start(decay[:, h, :], a["t_decay"][h]).then_inc(ev(f"decay_in{h}"), 16)
                for k in range(2):
                    sp.wait_ge(ev("k_read"), 15 + k)
                    granule(cache_v, 0, k)
                sp.wait_ge(ev("tok_copied"), 15)
                for name, rows in (("k_prompt", kf_tok), ("v_prompt", vf_tok)):
                    sp.dma_start(out[name][0, 0].rearrange("(j p) h d -> p j (h d)", p=128), rows[:, :, :]
                                 ).then_inc(ev("kv_stored"), 16)
                for name, rows in (("k_sample", k_s), ("v_sample", v_s)):
                    sp.dma_start(out[name][0, :, 0].rearrange("b h d -> b (h d)"), rows[:, :]
                                 ).then_inc(ev("rows_stored"), 16)
                sp.wait_ge(ev("logf_ready"), 2)
                store(sp, out["logf_prompt"][0, 0].rearrange("(j p) h -> p j h", p=128), logf[:, 0:4, :])
                store(sp, out["logf_sample"][0, :, 0], logf[0:NS, 4, :])
                sp.wait_ge(ev("kv_added"), 1)
                sn = out["ret_sample"][0].rearrange("b (m t) d e -> t d b m e", t=2)
                for t in range(2):
                    sp.dma_start(sn[t], state[64 * t:64 * t + 64]).then_inc(ev("state_stored"), 16)
                for h in range(1, NH):
                    if h >= 2:
                        sp.wait_ge(ev("score_read"), 8 * (h - 1))
                        sp.dma_start(decay[:, h % 2, :], a["t_decay"][h]).then_inc(ev(f"decay_in{h % 2}"), 16)
                    for k in range(2):
                        sp.wait_ge(ev("v_used"), 2 * h + k - 1)
                        granule(cache_v, h, k)
                sp.wait_ge(ev("kv_stored"), 32)
                sp.dma_start(heads_t[:, :], a["t_heads"]).then_inc(ev("heads_in"), 16)
                sp.wait_ge(ev("ret_state_ready"), 2)
                rp = out["ret_prompt"][0, 0].rearrange("(m t) d e -> t d m e", t=2)
                for t in range(2):
                    store(sp, rp[t], ret_state[64 * t:64 * t + 64])

            sp.dma_start(res[:, :], a["t_res"]).then_inc(consts_in, 16)
            b_rows = a["b_ada"].rearrange("l (r c) -> (l r) c", c=128)
            parts = [(0, 0, b_rows[0:128]), (1, 0, b_rows[128:144]),
                     (1, 16, a["ln_g"].rearrange("l s (r c) -> (l s r) c", c=128)),
                     (1, 64, a["ln_b"].rearrange("l s (r c) -> (l s r) c", c=128)),
                     (2, 0, a["conv_w"].rearrange("o j (r c) -> (o j r) c", c=128)),
                     (2, 24, a["c_prompt"].rearrange("b (r c) -> (b r) c", c=128)),
                     (2, 32, a["c_sample"].rearrange("b (r c) -> (b r) c", c=128)),
                     (3, 0, a["state_conv"].rearrange("o b j (r c) -> (o b j r) c", c=128))]
            for k, r, src in parts:
                sp.dma_start(p_rows[r:r + src.shape[0], k, :], src).then_inc(rows_in, 16)
            def first(g):
                sp.dma_start(first_ada(g), ada_view(0)[:, :, g * 512:(g + 1) * 512]).then_inc(first_full[g], 16)

            for g in range(2):
                first(g)
            sp.dma_start(x_rows[:, :, :], a["x_prompt"][0].rearrange("(j p) n -> p j n", p=128)).then_inc(x_rows_in, 16)
            sp.dma_start(s_rows[:, :], a["x_sample"][:, 0, :]).then_inc(x_rows_in, 16)
            for g in range(2, 4):
                first(g)
            for k in range(2):
                chunk(k, k, ffn_in[0][:, :, k * DFF:k * DFF + 128], KT)
            first(4)
            sp.wait_ge(rows_made, 1)
            first(5)
            for n in range(last):
                if n in FFN:
                    def body(i):
                        for k in range(2):
                            chunk(chunks_before(n) + i * 2 + k, k, ffn_in[n][:, :, bass.ds(i * 128 + k * DFF, 128)], KT)
                    with sp.Fori(1 if n == 0 else 0, FT) as i:
                        body(i)

                    def body(i):
                        for j in range(2):
                            for k in range(2):
                                m = i * 2 + j
                                chunk(chunks_before(n, True) + i * 4 + 2 * j + k, k,
                                      ffn_out[n][:, k * FH:(k + 1) * FH, bass.ds(m * 128, 128)], FH)
                                if n + 1 < last:
                                    pieces(n + 1, i, PIECES[2][2 * j + k])
                    if n == 0:
                        sp.wait_ge(rows_made, 6)
                    loop(sp, n == 0, KT // 2, body)
                    continue
                if n == EVEN:
                    even_loads(chunk)
                else:
                    def body(i):
                        for j in range(2):
                            for k in range(3):
                                q = 3 * j + k
                                chunk(chunks_before(n) + i * 6 + q, q % 2,
                                      odd_in[:, :, bass.ds(i * 256 + (j * 128 + k * D), 128)], KT)
                    loop(sp, False, KT // 2, body)

                if n == EVEN:
                    sp.wait_ge(ev("v_used"), 2 * NS)

                def body(i):
                    for k in range(2):
                        chunk(chunks_before(n, True) + i * 2 + k, k, mixer_out[n][:, :, bass.ds((i * 2 + k) * 128, 128)], KT)
                        if n + 1 < last:
                            pieces(n + 1, i, PIECES[1][k])
                loop(sp, False, KT // 2, body)
                if n == ODD:
                    sp.wait_ge(ev("tail_rows_ready"), 2)
                    for name, rows in (("conv_sample", tail_rows[:, 0, :]), ("conv_prompt", tail_rows[0:2 * KT, 1, :])):
                        sp.dma_start(out[name].rearrange("o b j (r c) -> (o b j r) c", c=128), rows
                                     ).then_inc(ev("tails_stored"), 16)

            sp.wait_ge(y_copied, 9)
            for j in range(4):
                store(sp, out["y_prompt"][0, j * 128:(j + 1) * 128, :], y_rows[:, j, :])
            store(sp, out["y_sample"][:, 0, :], ys_rows[:, :])
            sp.wait_ge(stored, 16 * n_stored[0])
            if last > EVEN:
                sp.wait_ge(ev("kv_stored"), 32)
                sp.wait_ge(ev("rows_stored"), 32)
                sp.wait_ge(ev("state_stored"), 32)
            if last > ODD:
                sp.wait_ge(ev("tails_stored"), 32)

        @block.gpsimd
        def _(pool):
            def even_pool():
                pool.wait_ge(chunk_used, chunks_before(EVEN) + 28)
                pool.wait_ge(ev("lf_past_ready"), 1)
                past = lf_past[:, :, :, :].rearrange("p b h g -> p (b h) g")
                pool.memset(later[:, :, NPG - 1:NPG], 0.0).then_inc(ev("later_ready"), 1)
                for g in range(NPG - 2, -1, -1):
                    pool.wait_ge(ev("later_ready"), NPG - 1 - g)
                    pool.tensor_tensor(later[:, :, g:g + 1], later[:, :, g + 1:g + 2], past[:, :, g + 1:g + 2], ALU.add
                                       ).then_inc(ev("later_ready"), 1)
                pool.wait_ge(ev("tables_in"), 16)
                for u in range(8):
                    pool.wait_ge(ev("rot_made"), u + 1)
                    pool.tensor_tensor(proj[:, QR + u], proj[:, QR + u], cos_t, ALU.mult).then_inc(ev("rot_cos"), 1)

            pool.memset(eps_ln[:, :], LN_EPS / ALPHA ** 2).then_inc(eps_ready, 1)
            pool.memset(eps_gn[:, :], GN_EPS).then_inc(eps_ready, 1)

            def cut(c, k, kt):
                pool.wait_ge(hi_cut, c + 1)
                pool.tensor_tensor(w_lo[:, k, 0:kt, :], raw[:, k, 0:kt, :], w_hi[:, k, 0:kt, :].bitcast(F32),
                                   ALU.subtract).then_inc(chunk_cut, 1)

            for n in range(last):
                for second in (False, True):
                    kt = tiles_of_product(n, second)
                    count = (CH_OUT if second else CH_IN)[n]

                    def body(i):
                        for k in range(2):
                            cut(chunks_before(n, second) + i * 2 + k, k, kt)
                    if second:
                        if n == EVEN:
                            for m in range(4):
                                pool.wait_ge(ev("hn_sq_done"), m + 1)
                                pool.wait_ge(ev("gate_silu"), m + 1)
                                pool.tensor_tensor(proj[:, VR + m], proj[:, VR + m], proj[:, GR + m], ALU.mult
                                                   ).then_inc(ev("hn_gated"), 1)
                        per_tile = count // KT

                        def second_body(i):
                            for u, now in enumerate(PIECES[per_tile]):
                                c = chunks_before(n, True) + i * 2 * per_tile + u
                                cut(c, u % 2, kt)
                                if n in FFN and n + 1 < last:
                                    low_pieces(pool, n, i, now)
                        loop(pool, False, KT // 2, second_body)
                    else:
                        body(0)
                        if n:
                            centre(pool, n - 1, 1)
                        modulate_samples(pool, n)
                        with pool.Fori(1, count // 2) as i:
                            body(i)
                        if n == EVEN:
                            even_pool()
            centre(pool, last - 1, 1)

        @block.tensor
        def _(pe):
            def product(c, k, q, kt, hi, lo, kt0=0, start=True, stop=True, between=None):
                pe.wait_ge(chunk_cut, c + 1)
                for t in range(kt):
                    if between:
                        between(t)
                    for step, (w, v) in enumerate(((w_hi, hi), (w_hi, lo), (w_lo, hi))):
                        for half in range(2):
                            mm = pe.matmul(ps[:, 2 * q + half, 0:HT], w[:, k, t, :], v[:, kt0 + t, half, :],
                                           start=start and t == 0 and step == 0,
                                           stop=stop and t == kt - 1 and step == 2)
                mm.then_inc(chunk_used, 1)

            def turn_group(n, g):
                pe.wait_ge(rows_copied, 6 + (n - 1) * GROUPS + g + 1)
                for u in range(2):
                    mm = pe.matmul(ps[:, 6, bass.ds(g * 18 + u * 9, 9)], ada_sums[:, u * 128:(u + 1) * 128], two_parts,
                                   start=True, stop=True)
                mm.then_inc(ada_turned, 1)

            def pieces(n, i, pieces_now):
                hi, lo = ada_parts[n - 1 == EVEN]
                for q in pieces_now:
                    if q % 2 == 0 and not (is_first(i) and q == 0):
                        turn_group(n, i * 3 + (q // 2 - 1))
                    pe.wait_ge(ada_cut, (n - 1) * MT + i * 6 + q + 1)
                    for t in range(KT // 2):
                        at = q % 2 * (KT // 2) + t
                        pe.matmul(ps[0:18, 7, 0:ADA_W], c_parts[:, at, :], hi[:, q % NADA, t, :],
                                  start=at == 0, stop=False)
                        mm = pe.matmul(ps[0:9, 7, 0:ADA_W], c_parts[:, at, 0:9], lo[:, q % NADA, t, :],
                                       start=False, stop=at == KT - 1)
                    mm.then_inc(ada_used, 1)

            def first_products(n, q0, q1):
                c = chunks_before(n)
                pe.wait_ge(chunk_cut, c + 2)
                for u in range(KT + LAG):
                    for k, t, q in ((0, u, q0), (1, u - LAG, q1)):
                        if not 0 <= t < KT:
                            continue
                        if k == 0:
                            pe.wait_ge(h_lo_done, KT * n + t + 1)
                        for step, (w, v) in enumerate(((w_hi, h_hi), (w_hi, h_lo), (w_lo, h_hi))):
                            for half in range(2):
                                mm = pe.matmul(ps[:, 2 * q + half, 0:HT], w[:, k, t, :], v[:, t, half, :],
                                               start=t == 0 and step == 0, stop=t == KT - 1 and step == 2)
                        if t == KT - 1:
                            mm.then_inc(chunk_used, 1)
                        if n == 0 and k == 0:
                            first_rows(4 + t // 4, range(t % 4 * 2, t % 4 * 2 + 2))

            pe.wait_ge(consts_in, 16)
            pe.wait_ge(rows_in, 16 * 8)
            for k, r in ((0, 128), (1, 112), (2, 96), (3, 128)):
                mm = pe.transpose(ps[:, 0, k * 128:k * 128 + r], p_rows[0:r, k, :], ident[0:r, 0:r])
            mm.then_inc(params_t, 1)
            def first_rows(g, tiles):
                pe.wait_ge(first_full[g], 16)
                for t in tiles:
                    mm = pe.matmul(ps[0:9, (0, 1, 0, 1, 4, 5)[g], :], c_act[:, t, :], first_ada(g)[:, t, :],
                                   start=t == 0, stop=t == KT - 1)
                if t == KT - 1:
                    mm.then_inc(rows_made, 1)

            def first_turned(g):
                pe.wait_ge(rows_copied, g + 1)
                for q in range(4 * g, 4 * g + 4):
                    pe.transpose(ps[:, 6 if g < 4 else 7, q * 9:q * 9 + 9],
                                 ada_rows[:, g % 4, (q % 4) * 128:(q % 4) * 128 + 128], ident[0:9, 0:9]).then_inc(ada_used, 1)

            pe.wait_ge(cond_ready, 1)
            first_rows(0, range(KT))
            first_rows(1, range(KT))
            first_turned(0)
            first_turned(1)
            pe.wait_ge(x_rows_in, 32)
            for t in range(KT):
                if t >= 2:
                    pe.wait_ge(x_copied, t - 1)
                for j in range(4):
                    mm = pe.transpose(ps[:, 2 + t % 2, j * 128:(j + 1) * 128], x_rows[:, j, t * 128:(t + 1) * 128], ident)
                mm.then_inc(x_t, 1)
            for t in range(KT):
                mm = pe.transpose(ps[:, 4, t * 8:t * 8 + 8], s_rows[:, t * 128:(t + 1) * 128], ident[0:8, 0:8])
            mm.then_inc(x_t, 1)
            first_rows(2, range(KT))
            first_rows(3, range(KT))
            first_turned(2)
            first_turned(3)

            def shift_sums(n):
                pe.wait_ge(summed, (KT - 1) * n + KT // 2)
                for half in range(2):
                    mm = pe.matmul(ps[:, 4 + half, 0:HT], mean_w, tile_sum[:, half, :], start=True, stop=True)
                mm.then_inc(half_summed, 1)

            def norm_sums(n):
                pe.wait_ge(shift_ready, n + 1)
                pe.wait_ge(samp_added, KT * (n + 1))
                for half in range(2):
                    pe.matmul(ps[:, 4 + half, 0:HT], mean_w, tile_sum[:, half, :], start=True, stop=False)
                    mm = pe.matmul(ps[:, 4 + half, 0:HT], mean_w, x[:, KT - 1, half, :], start=False, stop=True)
                mm.then_inc(mean_done, 1)
                pe.wait_ge(sq_added, (KT - 2) * (n + 1))
                for half in range(2):
                    pe.matmul(ps[:, half, 0:HT], mean_w, sq_sum[:, half, :], start=True, stop=False)
                pe.wait_ge(squared, KT * (n + 1))
                for half in range(2):
                    mm = pe.matmul(ps[:, half, 0:HT], mean_w, sq[:, (KT - 1) % 2, half, :], start=False, stop=True)
                mm.then_inc(var_done, 1)

            def even_pe():
                c0 = chunks_before(EVEN)

                def body(i):
                    for k in range(2):
                        pe.wait_ge(ev("copied"), 2 * (i * 2 + k - 1))
                        product(c0 + i * 2 + k, k, k, KT, h_hi, h_lo)
                first_products(EVEN, 0, 1)
                body(1)
                pe.wait_ge(ev("pool_in"), 32)
                pe.wait_ge(ev("one_hot_ready"), 1)
                by_head = ps[:, 5, :].rearrange("p (b h g) -> p b h g", b=NS, h=NH)
                for h in range(NH):
                    mm = pe.matmul(by_head[:, :, h, :], logf_pool[:, :, h], one_hot[:, :], start=True, stop=True)
                mm.then_inc(ev("gates_pe"), 1)
                pe.wait_ge(ev("copied"), 8)
                for m in range(4):
                    mm = pe.transpose(ps[0:NS, 4, m * 128:(m + 1) * 128], proj[:, QF + m, SEQ:NTOK], ident)
                mm.then_inc(ev("gates_pe"), 1)
                pe.wait_ge(ev("fg_cut"), 2)
                for t in range(KT):
                    for step, (w, v) in enumerate(((fg_hi, h_hi), (fg_hi, h_lo), (fg_lo, h_hi))):
                        for half in range(2):
                            mm = pe.matmul(ps[0:NH, 6 + half, 0:HT], w[:, t, :], v[:, t, half, :],
                                           start=t == 0 and step == 0, stop=t == KT - 1 and step == 2)
                mm.then_inc(ev("gates_pe"), 1)
                pe.wait_ge(ev("fg_copied"), 2)
                for j in range(5):
                    n = 128 if j < 4 else NS
                    mm = pe.transpose(ps[0:n, 7, j * NH:(j + 1) * NH], fg_rows[:, j * 128:j * 128 + n], ident[0:NH, 0:NH])
                mm.then_inc(ev("gates_pe"), 1)
                pe.wait_ge(ev("q_s_ready"), 1)
                for b in range(NS):
                    if b >= 2:
                        pe.wait_ge(ev("q_spread_copied"), b - 1)
                    pe.matmul(ps[:, 4 + 2 * (b % 2), :], sel[:, b, :], q_s[:, :], start=True, stop=True
                              ).then_inc(ev("q_spread"), 1)
                with pe.Fori(2, 14) as i:
                    body(i)

                pe.wait_ge(ev("copied"), 2 * 28)

                def by_token(tile, count0):
                    for j in range(4):
                        count = count0 + j
                        if count >= 4:
                            pe.wait_ge(ev("tok_copied"), count - 3)
                        for m in range(4):
                            mm = pe.transpose(ps[:, count % 4, m * 128:(m + 1) * 128],
                                              proj[:, tile + m, j * 128:(j + 1) * 128], ident)
                        mm.then_inc(ev("tok_t"), 1)

                for count0, tile in ((0, KF), (4, VF), (8, VR)):
                    by_token(tile, count0)
                pe.wait_ge(ev("tables_in"), 16)
                for u in range(8):
                    if u >= 2:
                        pe.wait_ge(ev("rot_read"), u - 1)
                    for half in range(2):
                        mm = pe.matmul(ps[:, 4 + 2 * (u % 2) + half, 0:HT], perm, proj[:, QR + u, half * HT:(half + 1) * HT],
                                       start=True, stop=True)
                    mm.then_inc(ev("rot_made"), 1)
                pe.wait_ge(ev("logf_ready"), 2)
                pe.wait_ge(ev("rot_read"), 8)
                for j in range(4):
                    for i in range(j + 1):
                        pe.matmul(ps[:, 5, j * NH:(j + 1) * NH], ones if i < j else tri[:, 384:512], logf[:, i, :],
                                  start=i == 0, stop=i == j)
                for i in range(4):
                    mm = pe.matmul(ps[0:NH, 6, :], logf[:, i, :], tri[:, 384 - 128 * i:896 - 128 * i], start=i == 0, stop=i == 3)
                mm.then_inc(ev("c_made"), 1)
                pe.wait_ge(ev("c_copied"), 2)
                for u, first in enumerate((KF, VF, VR)):
                    for m in range(4):
                        mm = pe.transpose(ps[0:NS, 4 + u, m * 128:(m + 1) * 128], proj[:, first + m, SEQ:NTOK], ident)
                    mm.then_inc(ev("s_rows_t"), 1)
                pe.wait_ge(ev("k_scaled"), 1)
                by_token(KR, 12)
                pe.wait_ge(ev("kr_copied"), 4)
                pe.wait_ge(ev("fg_z"), 2)
                for m in range(4):
                    for j in range(4):
                        mm = pe.matmul(ps[:, 7, m * 128:(m + 1) * 128], kr_tok[:, j, m * 128:(m + 1) * 128],
                                       vr_tok[:, j, m * 128:(m + 1) * 128], start=j == 0, stop=j == 3)
                mm.then_inc(ev("ret_state_made"), 1)
                pe.wait_ge(ev("tok_copied"), 15)
                pe.wait_ge(ev("lfnd_ready"), 1)
                past = lf_past[:, :, :, :].rearrange("p b h g -> p (b h) g")
                after = ps[:, 6, :].rearrange("p (q g) -> p q g", g=NPG)
                pe.matmul(after, strict, past, start=True, stop=False)
                pe.wait_ge(ev("later_ready"), NPG)
                pe.matmul(after, ones, later[:, :, :], start=False, stop=False)
                pe.matmul(after, ones[0:NS, :], sm["col"][0:NS, :].unsqueeze(2).to_broadcast([NS, 64, NPG]),
                          start=False, stop=True).then_inc(ev("after_made"), 1)
                pe.wait_ge(ev("s_reduced"), 1)
                pe.matmul(ps[:, 5, 0:64], ones[0:NS, :], sm["max"][0:NS, :], start=True, stop=True).then_inc(ev("s_turned"), 1)
                for b in range(NS):
                    for t in range(2):
                        mm = pe.matmul(ps[64 * t:64 * t + 64, b // 2, (b % 2) * 256:(b % 2) * 256 + 256], sel[:, b, 0:64],
                                       vr_s[:, :].rearrange("b (m t e) -> b t m e", m=4, t=2)[:, t], start=True, stop=True)
                    if b % 2:
                        mm.then_inc(ev("vr_spread"), 1)
                pe.wait_ge(ev("s_reduced"), 2)
                pe.transpose(ps[0:64, 4, 0:128], sm["max"][:, :], ident).then_inc(ev("s_turned"), 1)
                pe.wait_ge(ev("s_reduced"), 3)
                pe.matmul(ps[:, 5, 64:128], ones[0:64, :], sm["den"][0:64, :], start=True, stop=True).then_inc(ev("s_turned"), 1)
                pe.wait_ge(ev("s_reduced"), 4)
                pe.matmul(ps[:, 5, 128:192], ones, sm["max"][:, :], start=True, stop=True).then_inc(ev("s_turned"), 1)
                pe.wait_ge(ev("kv_added"), 1)
                for b in range(NS):
                    for m in range(4):
                        for t in range(2):
                            r = slice(64 * t, 64 * t + 64)
                            mm = pe.matmul(ps[r, t, 256 + m * 8 + b:257 + m * 8 + b], state[r, b, m, :],
                                           proj[r, QR + m, SEQ + b:SEQ + b + 1], start=True, stop=True)
                mm.then_inc(ev("ret_s_made"), 1)
                def score(h, j):
                    r, m = slice(64 * (h % 2), 64 * (h % 2) + 64), h // 2
                    if j == 0:
                        if h:
                            pe.wait_ge(ev("bias_done"), 4 * h)
                        pe.matmul(ps[:, 6, :], sel[:, h, :], c_heads[:, :], start=True, stop=True).then_inc(ev("c_spread"), 1)
                    u = 8 * h + j
                    if u >= 2:
                        pe.wait_ge(ev("score_read"), u - 1)
                    if j < 4:
                        pe.matmul(ps[:, u % 2, 0:(j + 1) * 128], proj[r, QF + m, j * 128:(j + 1) * 128],
                                  proj[r, KF + m, 0:(j + 1) * 128], start=True, stop=True).then_inc(ev("scores_done"), 1)
                    else:
                        k = j - 4
                        pe.matmul(ps[:, u % 2, 0:SEQ - k * 128], proj[r, KR + m, k * 128:(k + 1) * 128],
                                  proj[r, QR + m, k * 128:SEQ], start=True, stop=True).then_inc(ev("scores_done"), 1)

                def page_values(b, g):
                    k = g // 4
                    if g % 4 == 0:
                        pe.wait_ge(page_full[k], 64 * (NS + b + 1))
                    if g == 0 and b:
                        pe.wait_ge(ev("own_kept"), b)
                    mm = pe.matmul(ps[0:NH, 7, :], s_samp[:, b, :, g], pages[:, k, g % 4, :], start=g == 0, stop=g == NPG - 1)
                    if g % 4 == 3:
                        mm.then_inc(ev("v_used"), 1)

                def turned(h, j):
                    pe.wait_ge(ev("p_ready"), 4 * h + j + 1)
                    if 4 * h + j >= 2:
                        pe.wait_ge(ev("pt_copied"), 4 * h + j - 1)
                    for k in range(j + 1):
                        mm = pe.transpose(ps[:, 2 + j % 2, k * 128:(k + 1) * 128],
                                          probs[:, h % 2, PJ[j] + k * 128:PJ[j] + (k + 1) * 128], ident)
                    mm.then_inc(ev("pt_done"), 1)

                pe.wait_ge(ev("ret_s_copied"), 2)
                pe.wait_ge(ev("kv_read"), 4)
                pe.wait_ge(ev("ret_state_ready"), 2)
                pe.wait_ge(ev("p_samp"), 1)
                for j in range(8):
                    score(0, j)
                for h in range(NH):
                    r, m = slice(64 * (h % 2), 64 * (h % 2) + 64), h // 2
                    for j in range(8):
                        if h + 1 < NH:
                            score(h + 1, j)
                        page_values(h, j)
                    turned(h, 0)
                    turned(h, 1)
                    if h % 2 == 0 and h:
                        pe.wait_ge(ev("o_read"), h)
                    pe.wait_ge(ev("score_read"), 8 * h + 8)
                    for k in range(4):
                        mm = pe.matmul(ps[r, 5, k * 128:SEQ], vr_tok[:, k, h * HD:(h + 1) * HD],
                                       ret_a[h % 2][:, AK[k]:AK[k] + SEQ - k * 128], start=k == 0, stop=k == 3)
                    mm.then_inc(ev("ret_av"), 1)
                    turned(h, 2)
                    turned(h, 3)
                    pe.wait_ge(ev("pt_copied"), 4 * h + 4)
                    for k in range(4):
                        mm = pe.matmul(ps[r, 4, k * 128:SEQ], vf_tok[:, k, h * HD:(h + 1) * HD], p_t[:, k, k * 128:SEQ],
                                       start=k == 0, stop=k == 3)
                    mm.then_inc(ev("fox_av"), 1)
                pe.wait_ge(ev("o_read"), 8)
                for m in range(4):
                    for half in range(2):
                        mm = pe.matmul(ps[:, 2 * m + half, 0:HT], head_mean, proj[:, VR + m, half * HT:(half + 1) * HT],
                                       start=True, stop=True)
                    mm.then_inc(ev("hn_mean"), 1)
                pe.wait_ge(ev("heads_in"), 16)
                for m in range(4):
                    pe.wait_ge(ev("hn_sq_done"), m + 1)
                    for half in range(2):
                        mm = pe.matmul(ps[0:NH, half, 0:HT], to_row[:, m, :], hn_sq[:, m % 2, half * HT:(half + 1) * HT],
                                       start=m == 0, stop=m == 3)
                    mm.then_inc(ev("hn_var"), 1)
                pe.wait_ge(ev("own_kept"), NS)
                for b in range(NS):
                    mm = pe.matmul(ps[0:NS, 2, :], unit[:, b, :], own[b], start=b == 0, stop=b == NS - 1)
                mm.then_inc(ev("fox_turned"), 1)
                pe.wait_ge(ev("hn_recip"), 1)
                for m, q in enumerate((2, 3, 0)):
                    for half in range(2):
                        mm = pe.matmul(ps[:, 2 * q + half, 0:HT], from_row[:, m, :], hn_dev[:, half * HT:(half + 1) * HT],
                                       start=True, stop=True)
                    mm.then_inc(ev("hn_spread"), 1)
                pe.wait_ge(ev("fox_rows"), 1)
                for m in range(4):
                    mm = pe.transpose(ps[:, 3, m * 8:m * 8 + 8], s_prod[:, m * 128:(m + 1) * 128], ident[0:8, 0:8])
                mm.then_inc(ev("fox_turned"), 1)
                pe.wait_ge(ev("hn_scaled"), 1)
                for half in range(2):
                    mm = pe.matmul(ps[:, 4 + half, 0:HT], from_row[:, 3, :], hn_dev[:, half * HT:(half + 1) * HT],
                                   start=True, stop=True)
                mm.then_inc(ev("hn_spread"), 1)
                pe.wait_ge(ev("cat_lo"), 10)

            def odd_pe():
                c0 = chunks_before(ODD)

                def body(i):
                    for j in range(2):
                        for k in range(3):
                            if is_first(i) and j == 0 and k < 2:
                                continue
                            m, q = i * 2 + j, 3 * j + k
                            if k == 0 and not is_first(i):
                                pe.wait_ge(ev("conv_steps"), m * 12 - 13)
                            if k == 1 and not (is_first(i) and j == 0):
                                pe.wait_ge(ev("cg_copied"), m)
                            if k == 2 and not (is_first(i) and j == 0):
                                pe.wait_ge(ev("conv_steps"), m * 12 - 9)
                            product(c0 + i * 6 + q, q % 2, (2 + j, 0, 1)[k], KT, h_hi, h_lo)
                first_products(ODD, 2, 0)
                loop(pe, True, KT // 2, body)
                pe.wait_ge(ev("conv_steps"), 12 * KT + 1)
                pe.transpose(ps[:, 7, 0:128], tail_s[:, :, :, :].rearrange("p b j t -> p (b j t)"), ident)
                pe.transpose(ps[0:2 * KT, 7, 128:256], tail_p[:, :, :].rearrange("p j t -> p (j t)"), ident).then_inc(ev("tails_t"), 1)
                pe.wait_ge(ev("mixed_lo"), KT)

            def second_product(n, body):
                loop(pe, True, KT // 4, body)
                body(KT // 4)
                body(KT // 4 + 1)
                if n + 1 < last:
                    turn_group(n + 1, GROUPS - 1)

            for n in range(last):
                if n in FFN:
                    f0 = FT * ffns_before(n)

                    def body(i):
                        for j in range(2):
                            for k in range(2):
                                if is_first(i) and j == 0:
                                    continue
                                if not (n == 0 and is_first(i)):
                                    pe.wait_ge(gate_done if k else silu_done, f0 + i * 2 + j - 1)
                                product(chunks_before(n) + i * 4 + 2 * j + k, k, 2 * j + k, KT, h_hi, h_lo)
                    first_products(n, 0, 1)
                    if n == 0:
                        first_turned(4)
                        first_turned(5)
                        pe.wait_ge(mod_steps, mod_steps_before(1))
                    loop(pe, True, FT // 2, body)
                    pe.wait_ge(hid_lo_done, f0 + FT)

                    def body(i):
                        for j in range(2):
                            for k in range(2):
                                if k == 0 and not (n == 0 and is_first(i)):
                                    pe.wait_ge(drained, 2 * (KT * n + i * 2 + j - 1))
                                now = PIECES[2][2 * j + k] if n + 1 < last else ()
                                product(chunks_before(n, True) + i * 4 + 2 * j + k, k, j, FH, hid_hi, hid_lo,
                                        kt0=k * FH, start=k == 0, stop=k == 1,
                                        between=lambda t: pieces(n + 1, i, now[:1]) if t == FH // 2 else None)
                                if isinstance(i, int) and (i, j, k) == (KT // 4, 0, 0):
                                    shift_sums(n)
                                pieces(n + 1, i, now[1:])
                    second_product(n, body)
                else:
                    if n == EVEN:
                        even_pe()
                        hi, lo = h_hi, h_lo
                    else:
                        odd_pe()
                        hi, lo = mix_hi, mix_lo

                    def body(i):
                        for k in range(2):
                            pe.wait_ge(drained, 2 * (KT * n + i * 2 + k - 1))
                            now = PIECES[1][k] if n + 1 < last else ()
                            product(chunks_before(n, True) + i * 2 + k, k, k, KT, hi, lo,
                                    between=lambda t: pieces(n + 1, i, now[t // 3 - 1:t // 3]) if t in (3, 6) else None)
                            if isinstance(i, int) and (i, k) == (KT // 4, 0):
                                shift_sums(n)
                            pieces(n + 1, i, now[2:])
                    second_product(n, body)
                norm_sums(n)

            pe.wait_ge(ln_done, KT * last)
            for j in range(4):
                for g in range(2):
                    u = 2 * j + g
                    if u >= 2:
                        pe.wait_ge(y_copied, u - 1)
                    for t in range(4):
                        mm = pe.transpose(ps[:, 2 + g, t * 128:(t + 1) * 128],
                                          x[:, 4 * g + t, j // 2, (j % 2) * 128:(j % 2) * 128 + 128], ident)
                    mm.then_inc(y_t, 1)
            pe.wait_ge(samp_out, 1)
            for t in range(KT):
                mm = pe.transpose(ps[0:NS, 4 + t // 4, (t % 4) * 128:(t % 4) * 128 + 128], samp_t[:, t, :], ident)
            mm.then_inc(y_t, 1)

        @block.scalar
        def _(act):
            def squares(n, tiles):
                for t in tiles:
                    act.wait_ge(shifted, KT * n + t + 1)
                    act.activation(sq[:, t % 2] if t else sq_sum[:, :, :], sq[:, t % 2], ACT.Square).then_inc(squared, 1)

            def norm_act(n):
                act.wait_ge(mean_done, n + 1)
                act.activation(mean[:, :, :], pair(2), ACT.Identity).then_inc(mean_ready, 1)
                act.wait_ge(delta_steps, 3 * (n + 1))
                act.wait_ge(eps_ready, 2)
                act.activation(dev, dev, ACT.Sqrt, bias=eps_ln[:, :]).then_inc(dev_done, 1)

            def affine(n):
                if n + 1 < last:
                    act.wait_ge(samp_mod, KT * (n + 2))
                    act.wait_ge(h32_done, KT * (n + 2))
                for t in range(KT):
                    if n + 1 == last:
                        act.wait_ge(normed, KT * n + t + 1)
                    act.activation(x[:, t], x[:, t], ACT.Identity, scale=params[:, LN_G + n * KT + t:LN_G + n * KT + t + 1],
                                   bias=params[:, LN_B + n * KT + t:LN_B + n * KT + t + 1]).then_inc(ln_done, 1)

            def modulate_act(n):
                m = n % 2
                act.wait_ge(mod_steps, mod_steps_before(n) + (5 if n else 2))
                for t in range(KT):
                    if n:
                        act.wait_ge(normed, KT * (n - 1) + t + 1)
                    act.activation(h32[:, t, :, 0:HP], x[:, t, :, 0:HP], ACT.Identity, scale=mod[:, m, KT + t, 0:1],
                                   bias=mod[:, m, t, 0:1]).then_inc(h32_done, 1)
                    act.wait_ge(h32_done, KT * n + t + 1)
                    act.wait_ge(h32_samp, KT * n + t + 1)
                    act.activation(h_hi[:, t], h32[:, t], ACT.Identity).then_inc(h_hi_done, 1)

            def cut(c, k, kt):
                if not (isinstance(c, int) and c < 2):
                    act.wait_ge(chunk_used, c - 1)
                act.wait_ge(raw_full[k], (c - k) * 8 + 16)
                act.activation(w_hi[:, k, 0:kt, :], raw[:, k, 0:kt, :], ACT.Identity).then_inc(hi_cut, 1)

            def even_act():
                c0 = chunks_before(EVEN)

                def body(i, more=True):
                    for k in range(2):
                        m = i * 2 + k
                        if more:
                            cut(c0 + m + 2, k, KT)
                        else:
                            act.wait_ge(chunk_used, c0 + m + 1)
                        tile = proj[:, bass.ds(m, 1)].rearrange("p a c -> p (a c)")
                        act.activation(tile[:, 0:SEQ].rearrange("p (h c) -> p h c", h=2), ps[:, 2 * k:2 * k + 2, 0:HP],
                                       ACT.Identity).then_inc(ev("copied"), 1)
                        act.activation(tile[:, SEQ:NTOK].rearrange("p (h c) -> p h c", h=2), ps[:, 2 * k:2 * k + 2, HP:HT],
                                       ACT.Identity).then_inc(ev("copied"), 1)
                body(0)
                affine(EVEN - 1)
                act.wait_ge(ev("fg_in"), 32)
                act.activation(fg_hi[:, :, :], w_fg[:, :, :], ACT.Identity).then_inc(ev("fg_cut"), 1)
                body(1)
                act.wait_ge(ev("gates_pe"), 1)
                act.activation(lf_past[:, :, :, :].rearrange("p b h g -> p (b h g)"), ps[:, 5, :], ACT.Identity
                               ).then_inc(ev("lf_past_ready"), 1)
                act.wait_ge(ev("gates_pe"), 2)
                act.activation(q_s[:, :], ps[0:NS, 4, :], ACT.Identity).then_inc(ev("q_s_ready"), 1)
                act.wait_ge(ev("gates_pe"), 3)
                act.activation(fg_rows[:, 0:SEQ].rearrange("p (h c) -> p h c", h=2), ps[0:NH, 6:8, 0:HP], ACT.Identity
                               ).then_inc(ev("fg_copied"), 1)
                act.activation(fg_rows[:, SEQ:NTOK].rearrange("p (h c) -> p h c", h=2), ps[0:NH, 6:8, HP:HT], ACT.Identity
                               ).then_inc(ev("fg_copied"), 1)
                for b in range(NS):
                    act.wait_ge(ev("q_spread"), b + 1)
                    act.activation(q_all[:, b, :], ps[:, 4 + 2 * (b % 2), :], ACT.Identity).then_inc(ev("q_spread_copied"), 1)
                both = lambda v: (v[:, 0:4, :], v[0:NS, 4, :])
                act.wait_ge(ev("fg_z"), 2)
                for k, (d, v) in enumerate(zip(both(lf_b), both(lf_a))):
                    act.activation(d, v, ACT.Abs).then_inc(ev("fg_abs"), 1)
                act.wait_ge(ev("fg_abs"), 2)
                for v in both(lf_b):
                    act.activation(v, v, ACT.Exp, scale=-1.0).then_inc(ev("fg_exp"), 1)
                act.wait_ge(ev("fg_exp"), 2)
                for v in both(lf_b):
                    act.activation(v, v, ACT.Ln, bias=1.0).then_inc(ev("fg_ln"), 1)
                with act.Fori(2, 13) as i:
                    body(i)
                body(13, more=False)
                act.wait_ge(ev("k_read"), 2 * NS)
                for count in range(12):
                    act.wait_ge(ev("tok_t"), count + 1)
                    act.activation((kf_tok, vf_tok, vr_tok)[count // 4][:, count % 4, :], ps[:, count % 4, :], ACT.Identity
                                   ).then_inc(ev("tok_copied"), 1)
                for m in range(4):
                    act.activation(proj[:, GR + m], proj[:, GR + m], ACT.Silu).then_inc(ev("gate_silu"), 1)
                act.wait_ge(ev("c_made"), 1)
                act.activation(c_cols[:, :, :].rearrange("p j h -> p (j h)"), ps[:, 5, 0:4 * NH], ACT.Identity).then_inc(ev("c_copied"), 1)
                act.activation(c_heads[:, :], ps[0:NH, 6, :], ACT.Identity).then_inc(ev("c_copied"), 1)
                for u, rows in enumerate((k_s, v_s, vr_s)):
                    act.wait_ge(ev("s_rows_t"), u + 1)
                    act.activation(rows[:, :], ps[0:NS, 4 + u, :], ACT.Identity).then_inc(ev("tok_copied"), 1)
                act.wait_ge(ev("ret_state_made"), 1)
                for t in range(2):
                    r = slice(64 * t, 64 * t + 64)
                    act.activation(ret_state[r, :, :], ps[r, 7, :].rearrange("p (m c) -> p m c", m=4)[:, :, 64 * t:64 * t + 64],
                                   ACT.Identity).then_inc(ev("ret_state_ready"), 1)
                act.wait_ge(ev("s_shifted"), 2)
                act.activation(s_samp[:, :, :, :].rearrange("p b h g -> p (b h g)"),
                               s_samp[:, :, :, :].rearrange("p b h g -> p (b h g)"), ACT.Exp).then_inc(ev("s_exp"), 1)
                act.activation(sm["new"][:, :], sm["new"][:, :], ACT.Exp).then_inc(ev("s_exp"), 1)
                act.wait_ge(ev("ret_s_made"), 1)
                for t in range(2):
                    r = slice(64 * t, 64 * t + 64)
                    act.activation(proj[r, VR:VR + 4, SEQ:NTOK], ps[r, t, 256:288].rearrange("p (m b) -> p m b", m=4),
                                   ACT.Identity).then_inc(ev("ret_s_copied"), 1)

                def bias(h):
                    act.wait_ge(ev("c_spread"), h + 1)
                    if h >= 2:
                        act.wait_ge(ev("pt_done"), 4 * (h - 1))
                    for j in range(4):
                        act.activation(probs[:, h % 2, PJ[j]:PJ[j] + (j + 1) * 128], ps[:, 6, 0:(j + 1) * 128], ACT.Identity,
                                       scale=-1.0, bias=c_cols[:, j, h:h + 1]).then_inc(ev("bias_done"), 1)

                def exps(h):
                    for j in range(4):
                        v = probs[:, h % 2, PJ[j]:PJ[j] + (j + 1) * 128]
                        c = 4 * h + j
                        act.wait_ge(ev("max_done"), c + 1)
                        act.activation(v, v, ACT.Exp, bias=n_max[:, c:c + 1], accum_out=row_sum[:, c:c + 1]
                                       ).then_inc(ev("exp_done"), 1)

                act.wait_ge(ev("kv_added"), 1)
                bias(0)
                exps(0)
                act.wait_ge(ev("rows_stored"), 32)
                act.wait_ge(ev("new_v"), 1)
                for h in range(NH):
                    if h + 1 < NH:
                        bias(h + 1)
                    for j in range(4):
                        c = 4 * h + j
                        act.wait_ge(ev("pt_done"), c + 1)
                        if h:
                            act.wait_ge(ev("fox_av"), h)
                        act.activation(p_t[:, 0:j + 1, j * 128:(j + 1) * 128],
                                       ps[:, 2 + j % 2, 0:(j + 1) * 128].rearrange("p (k c) -> p k c", c=128), ACT.Identity
                                       ).then_inc(ev("pt_copied"), 1)
                    if h + 1 < NH:
                        exps(h + 1)
                for m in range(4):
                    act.wait_ge(ev("hn_centred"), m + 1)
                    if m >= 2:
                        act.wait_ge(ev("hn_var"), m - 1)
                    act.activation(hn_sq[:, m % 2, :], proj[:, VR + m], ACT.Square).then_inc(ev("hn_sq_done"), 1)
                act.wait_ge(ev("hn_var"), 4)
                act.activation(hn_dev[:, :].rearrange("p (h c) -> p h c", h=2), ps[0:NH, 0:2, 0:HT], ACT.Sqrt,
                               bias=eps_gn[0:NH, :]).then_inc(ev("hn_dev_done"), 1)
                act.wait_ge(ev("fox_turned"), 1)
                for t in range(KT):
                    if t >= 4:
                        act.wait_ge(ev("hn_scaled"), t - 3)
                    act.activation(h_hi[:, t, :, 0:HP], mixed_tile(t)[:, 0:SEQ].rearrange("p (h c) -> p h c", h=2),
                                   ACT.Identity).then_inc(ev("cat_hi"), 1)
                act.wait_ge(ev("fox_s_done"), 1)
                for u, first in enumerate((VF, VR)):
                    act.activation(h_hi[:, 4 * u:4 * u + 4, :, HP:HT],
                                   proj[:, first:first + 4, SEQ:NTOK].rearrange("p t (h c) -> p t h c", h=2),
                                   ACT.Identity).then_inc(ev("cat_hi"), 1)
                for k in range(2):
                    cut(chunks_before(EVEN, True) + k, k, KT)

            def odd_act():
                c0 = chunks_before(ODD)

                def body(i):
                    for j in range(2):
                        m = i * 2 + j
                        q = 3 * j
                        cut(c0 + i * 6 + q + 2, q % 2, KT)
                        cut(c0 + i * 6 + q + 3, (q + 1) % 2, KT)
                        if not (is_first(i) and j == 0):
                            act.wait_ge(ev("conv_steps"), m * 12 - 9)
                        act.activation(cg[:, :, :], pair(0), ACT.Identity).then_inc(ev("cg_copied"), 1)
                        cut(c0 + i * 6 + q + 4, q % 2, KT)
                        act.wait_ge(ev("conv_steps"), m * 12 + 11)
                        act.activation(mix_hi[:, bass.ds(m, 1)].rearrange("p a h c -> p (a h) c"), mixed[:, j],
                                       ACT.Identity).then_inc(ev("mixed_hi"), 1)
                body(0)
                affine(ODD - 1)
                with act.Fori(1, KT // 2) as i:
                    body(i)
                act.wait_ge(ev("tails_t"), 1)
                act.activation(tail_rows[:, 0, :], ps[:, 7, 0:128], ACT.Identity).then_inc(ev("tail_rows_ready"), 1)
                act.activation(tail_rows[0:2 * KT, 1, :], ps[0:2 * KT, 7, 128:256], ACT.Identity).then_inc(ev("tail_rows_ready"), 1)

            def second_product(n):
                c0 = chunks_before(n, True)
                per_tile = 2 if n in FFN else 1
                kt, next_kt = tiles_of_product(n, True), next_tiles(n, True)
                steps = PIECES[per_tile]
                hi = ada_parts[n == EVEN][0]

                def high_piece(i, q):
                    if not (is_first(i) and q < NADA):
                        act.wait_ge(ada_used, (n + 1) * MT + i * 6 + q - NADA + 1)
                    act.wait_ge(ada_full[q % NADA], n * MT // NADA * 16 + i * 32 + q // NADA * 16 + 16)
                    act.activation(hi[:, q % NADA], ada_w[:, q % NADA], ACT.Identity).then_inc(ada_hi_cut, 1)

                def group_sums(i, q):
                    act.wait_ge(ada_used, (n + 1) * MT + i * 6 + q + 1)
                    act.activation(ada_sums[:, :], ps[0:18, 7, 0:ADA_W], ACT.Identity).then_inc(rows_copied, 1)

                def modulation_parts(i, now, then, chunk=None):
                    cuts = [((now[-1] if len(now) > 1 else now[-1] + 1) - 0.5, 2, 0)] if chunk else []
                    for _, what, q in sorted([(q, 0, q) for q in now if q % 2] + [(q - NADA, 1, q) for q in then] + cuts):
                        if what == 2:
                            cut(*chunk)
                        elif what == 0:
                            group_sums(i, q)
                        elif q < 6:
                            high_piece(i, q)
                        else:
                            high_piece(i + 1, q - 6)

                def body(i):
                    for u, now in enumerate(steps):
                        static = isinstance(i, int)
                        beyond = static and i * 2 * per_tile + u + 2 >= KT * per_tile
                        chunk = None
                        if not beyond or next_kt:
                            chunk = (c0 + i * 2 * per_tile + u + 2, u % 2, next_kt if beyond else kt)
                        if n + 1 == last and chunk:
                            cut(*chunk)
                        if n + 1 < last:
                            then = (steps + (tuple(q + 6 for q in steps[0]),))[u + 1]
                            if static and i == KT // 2 - 1 and then[0] >= 6:
                                then = ()
                            modulation_parts(i, now, then, chunk)
                        t, tile_ends = 0, (u + 1) % per_tile == 0
                        if static and i >= KT // 4 and tile_ends:
                            t = i * 2 + u // per_tile
                            if t == KT // 2:
                                act.wait_ge(half_summed, n + 1)
                                act.activation(shift[:, :, :], pair(2), ACT.Identity, scale=2.0).then_inc(shift_ready, 1)
                            squares(n, SQUARES_WITH[t])

                act.wait_ge(chunk_used, c0)
                if n == EVEN:
                    act.wait_ge(ev("cat_lo"), 10)
                if n + 1 < last:
                    modulation_parts(0, (), steps[0])
                loop(act, True, KT // 4, body)
                body(KT // 4)
                body(KT // 4 + 1)

            act.wait_ge(c_ready, 1)
            act.activation(c_act[:, :, :], c_t[:, :, :], ACT.Silu).then_inc(cond_ready, 1)

            act.wait_ge(cond_ready, 1)
            act.activation(c_parts[:, :, 0:9], c_act[:, :, :], ACT.Identity).then_inc(cond_ready, 1)

            def copy_rows(g):
                act.wait_ge(rows_made, g + 1)
                act.activation(ada_rows[:, g % 4, :], ps[0:9, (0, 1, 0, 1, 4, 5)[g], :], ACT.Identity).then_inc(rows_copied, 1)

            copy_rows(0)
            copy_rows(1)
            for t in range(KT):
                act.wait_ge(x_t, t + 1)
                act.activation(x[:, t, :, 0:HP], ps[:, 2 + t % 2, :].rearrange("p (h c) -> p h c", h=2),
                               ACT.Identity).then_inc(x_copied, 1)
            act.wait_ge(x_t, KT + 1)
            act.activation(x[:, :, :, HP:HT], ps[:, 4, 0:64].rearrange("p (t h c) -> p t h c", t=KT, h=2),
                           ACT.Identity).then_inc(x_copied, 1)
            copy_rows(2)
            act.wait_ge(x_copied, KT + 1)
            for k in range(2):
                cut(k, k, KT)
            copy_rows(3)
            modulate_act(0)
            copy_rows(4)
            copy_rows(5)
            act.wait_ge(ada_used, MT)
            for n in range(last):
                if n - 1 in (EVEN, ODD):
                    act.wait_ge(*((ev("kv_stored"), 32) if n - 1 == EVEN else (ev("tails_stored"), 32)))
                if n in FFN:
                    f0 = FT * ffns_before(n)

                    def body(i, final):
                        for j in range(2):
                            c = chunks_before(n) + i * 4 + 2 * j
                            kt = next_tiles(n, False) if final and j else KT
                            cut(c + 2, 0, kt)
                            if not (n == 0 and is_first(i)):
                                act.wait_ge(gate_done, f0 + i * 2 + j - 1)
                            act.activation(silu_a[:, j], pair(2 * j), ACT.Silu).then_inc(silu_done, 1)
                            cut(c + 3, 1, kt)
                            act.wait_ge(gate_done, f0 + i * 2 + j + 1)
                            act.activation(hid_hi[:, bass.ds(i * 2 + j, 1)].rearrange("p a h c -> p (a h) c"), gated[:, j], ACT.Identity).then_inc(hid_hi_done, 1)
                    body(0, False)
                    if n:
                        affine(n - 1)
                    with act.Fori(1, FT // 2 - 1) as i:
                        body(i, False)
                    body(FT // 2 - 1, True)
                else:
                    (even_act if n == EVEN else odd_act)()
                second_product(n)
                norm_act(n)
                if n + 1 < last:
                    modulate_act(n + 1)
            affine(last - 1)
            for j in range(4):
                for g in range(2):
                    act.wait_ge(y_t, 2 * j + g + 1)
                    act.activation(y_rows[:, j, g * 512:(g + 1) * 512], ps[:, 2 + g, :], ACT.Identity).then_inc(y_copied, 1)
            act.wait_ge(y_t, 9)
            act.activation(ys_rows[:, :].rearrange("p (g c) -> p g c", g=2), ps[0:NS, 4:6, :], ACT.Identity).then_inc(y_copied, 1)

        @block.vector
        def _(dve):
            def modulation(n):
                m, s0 = n % 2, mod_steps_before(n)
                if n:
                    dve.wait_ge(ada_turned, GROUPS * n)
                else:
                    dve.wait_ge(ada_used, 2 * KT)
                add_bias(n, 0, 2 * KT)
                dve.wait_ge(mod_steps, s0 + 1)
                shift_m, scale_m = mod[:, m, 0:KT], mod[:, m, KT:2 * KT]
                dve.tensor_scalar(scale_m, scale_m, 1.0, None, ALU.add).then_inc(mod_steps, 1)
                dve.wait_ge(mod_steps, s0 + 2)
                if n:
                    g, b = (params[:, v + (n - 1) * KT:v + n * KT].unsqueeze(2).to_broadcast([128, KT, 9]) for v in (LN_G, LN_B))
                    dve.tensor_tensor(mod_b[:, :, :], scale_m, b, ALU.mult).then_inc(mod_steps, 1)
                    dve.wait_ge(mod_steps, s0 + 3)
                    dve.tensor_tensor(scale_m, scale_m, g, ALU.mult).then_inc(mod_steps, 1)
                    dve.tensor_tensor(shift_m, shift_m, mod_b[:, :, :], ALU.add).then_inc(mod_steps, 1)
                    gate(n)

            def add_bias(n, q0, q1):
                bias = params[:, n * MT + q0:n * MT + q1].unsqueeze(2).to_broadcast([128, q1 - q0, 9])
                bank = 7 if n == 0 and q0 == 2 * KT else 6
                dve.tensor_tensor(mod[:, n % 2, q0:q1], ps[:, bank, 9 * q0:9 * q1].rearrange("p (q c) -> p q c", c=9), bias,
                                  ALU.add).then_inc(mod_steps, 1)

            def gate(n):
                add_bias(n, 2 * KT, MT)
                dve.wait_ge(mod_steps, mod_steps_before(n + 1) - 1)
                v = mod[:, n % 2, 2 * KT:MT]
                dve.tensor_scalar(v, v, (0.5 if n in FFN else 1.0) / ALPHA, None, ALU.mult).then_inc(mod_steps, 1)

            def modulate(n):
                for t in range(KT):
                    if n:
                        normalise_tile(n - 1, t)
                    if t:
                        low(n, t - 1)
                low(n, KT - 1)

            def normalise_tile(n, t):
                dve.wait_ge(centred[t >= CENTRE], (CENTRE if t < CENTRE else KT - CENTRE) * n
                            + (t if t < CENTRE else t - CENTRE) + 1)
                dve.tensor_tensor(x[:, t], x[:, t], rdev[:, :, :], ALU.mult).then_inc(normed, 1)

            def low(n, t):
                dve.wait_ge(h_hi_done, KT * n + t + 1)
                dve.tensor_tensor(h_lo[:, t], h32[:, t], h_hi[:, t].bitcast(F32), ALU.subtract).then_inc(h_lo_done, 1)

            def residual(n, i, j, q):
                m = n % 2
                t = i * 2 + j
                c0 = KT * n + t
                xt = x[:, bass.ds(t, 1)].rearrange("p a h c -> p (a h) c")
                g = mod[:, m, bass.ds(t + 2 * KT, 1)].rearrange("p a c -> p (a c)")
                dve.scalar_tensor_tensor(xt[:, :, 0:HP], ps[:, 2 * q:2 * q + 2, 0:HP], g[:, 0:1], xt[:, :, 0:HP],
                                         ALU.mult, ALU.add).then_inc(drained, 1)
                dve.tensor_tensor(samp8[:, :].rearrange("p (h c) -> p h c", h=2), ps[:, 2 * q:2 * q + 2, HP:HT],
                                  g[:, 1:9].rearrange("p (h c) -> p h c", h=2), ALU.mult).then_inc(drained, 1)
                dve.wait_ge(drained, c0 * 2 + 2)
                dve.tensor_tensor(xt[:, :, HP:HT], xt[:, :, HP:HT], samp8[:, :].rearrange("p (h c) -> p h c", h=2),
                                  ALU.add).then_inc(samp_added, 1)
                s0 = (KT - 1) * n + t
                if is_first(t):
                    dve.wait_ge(samp_added, c0 + 1)
                    dve.tensor_copy(tile_sum[:, :, :], xt).then_inc(summed, 1)
                elif not (isinstance(t, int) and t == KT - 1):
                    dve.wait_ge(samp_added, c0 + 1)
                    if isinstance(t, int) and t == KT // 2:
                        dve.wait_ge(half_summed, n + 1)
                    dve.wait_ge(summed, s0)
                    dve.tensor_tensor(tile_sum[:, :, :], tile_sum[:, :, :], xt, ALU.add).then_inc(summed, 1)

            def distance(n, t):
                a0 = (KT - 2) * n
                if t >= 3:
                    dve.wait_ge(sq_added, a0 + t - 2)
                elif t == 2:
                    dve.wait_ge(squared, KT * n + 1)
                dve.tensor_tensor(sq[:, t % 2], x[:, t], shift[:, :, :], ALU.subtract).then_inc(shifted, 1)
                if t >= 2:
                    dve.wait_ge(squared, KT * n + t)
                    if t >= 3:
                        dve.wait_ge(sq_added, a0 + t - 2)
                    dve.tensor_tensor(sq_sum[:, :, :], sq_sum[:, :, :], sq[:, (t - 1) % 2], ALU.add
                                      ).then_inc(sq_added, 1)

            def residuals(n, product_done):
                def body(i):
                    for j in range(2):
                        if n not in FFN and n + 1 < last:
                            low_pieces(dve, n, i, PIECES[1][j])
                        product_done(i, j)
                        residual(n, i, j, j)
                dve.wait_ge(mod_steps, mod_steps_before(n + 1))
                if n:
                    dve.wait_ge(ln_done, KT * n)
                loop(dve, True, KT // 4, body)
                for t in range(KT // 2, KT):
                    if n not in FFN and n + 1 < last:
                        low_pieces(dve, n, t // 2, PIECES[1][t % 2])
                    product_done(t // 2, t % 2)
                    residual(n, t // 2, t % 2, t % 2)
                    if t == KT // 2:
                        dve.wait_ge(shift_ready, n + 1)
                    dve.wait_ge(samp_added, KT * n + t + 1)
                    for u in SQUARES_WITH[t]:
                        distance(n, u)

            def norm(n):
                d0 = 3 * n
                dve.wait_ge(mean_ready, n + 1)
                dve.tensor_tensor(shift[:, :, :], mean[:, :, :], shift[:, :, :], ALU.subtract).then_inc(delta_steps, 1)
                dve.wait_ge(delta_steps, d0 + 1)
                dve.tensor_tensor(shift[:, :, :], shift[:, :, :], shift[:, :, :], ALU.mult).then_inc(delta_steps, 1)
                dve.wait_ge(delta_steps, d0 + 2)
                dve.wait_ge(var_done, n + 1)
                dve.tensor_tensor(dev, pair(0), shift[:, :, :], ALU.subtract).then_inc(delta_steps, 1)
                centre(dve, n, 0)
                dve.wait_ge(dev_done, n + 1)
                dve.reciprocal(rdev[:, :, :], dev).then_inc(rdev_done, 1)
                dve.wait_ge(rdev_done, n + 1)
                if n + 1 == last:
                    for t in range(KT):
                        normalise_tile(n, t)

            def then(name, instruction, count=1):
                instruction.then_inc(ev(name), 1)
                dve.wait_ge(ev(name), count)

            chained = [0]

            def link(instruction):
                chained[0] += 1
                instruction.then_inc(ev("chained"), 1)

            def rest():
                dve.wait_ge(ev("chained"), chained[0])

            def chain(instruction):
                link(instruction)
                rest()

            def even_dve():
                dve.wait_ge(ev("fg_cut"), 1)
                dve.tensor_tensor(fg_lo[:, :, :], w_fg[:, :, :], fg_hi[:, :, :].bitcast(F32), ALU.subtract).then_inc(ev("fg_cut"), 1)
                dve.wait_ge(ev("pool_in"), 32)
                chain(dve.tensor_copy(page_f[:, :], page_ids[:, :]))
                dve.tensor_scalar(one_hot[:, :], page_f[:, :], lane[0:n_phys, :], None, ALU.is_equal).then_inc(ev("one_hot_ready"), 1)
                both = lambda v: (v[:, 0:4, :], v[0:NS, 4, :])
                dve.wait_ge(ev("gates_pe"), 4)
                dve.wait_ge(ev("fg_in"), 32)
                dve.tensor_tensor(lf_a[:, 0:4, :], ps[:, 7, 0:4 * NH].rearrange("p (j h) -> p j h", j=4),
                                  b_fg[:, :].unsqueeze(1).to_broadcast([128, 4, NH]), ALU.add).then_inc(ev("fg_z"), 1)
                dve.tensor_tensor(lf_a[0:NS, 4, :], ps[0:NS, 7, 4 * NH:5 * NH], b_fg[0:NS, :], ALU.add).then_inc(ev("fg_z"), 1)
                dve.wait_ge(ev("fg_abs"), 2)
                dve.wait_ge(ev("fg_z"), 2)
                for v in both(lf_a):
                    link(dve.tensor_scalar(v, v, 0.0, None, ALU.min))
                rest()
                dve.wait_ge(ev("fg_ln"), 2)
                for d, v, w in zip(both(logf), both(lf_a), both(lf_b)):
                    dve.tensor_tensor(d, v, w, ALU.subtract).then_inc(ev("logf_ready"), 1)
                dve.wait_ge(ev("logf_ready"), 2)
                dve.tensor_tensor(sm["col"][0:NS, :].rearrange("p (b h) -> p b h", b=NS),
                                  logf[0:NS, 4:5, :].to_broadcast([NS, NS, NH]), delta, ALU.mult).then_inc(ev("lfnd_ready"), 1)
                dve.wait_ge(ev("q_spread_copied"), NS)
                with dve.Fori(0, NS) as b:
                    for k in range(2):
                        dve.wait_ge(page_full[k], b * 64 + 64)
                        q_b = q_all[:, bass.ds(b, 1)].to_broadcast([128, 4, FOXW])
                        dve.tensor_tensor(pages[:, k], pages[:, k], q_b, ALU.mult).then_inc(ev("k_prod"), 1)
                        dve.wait_ge(ev("k_prod"), b * 2 + k + 1)
                        dve.tensor_reduce(s_samp[:, bass.ds(b, 1), :, 4 * k:4 * k + 4].rearrange("p a h g -> p (a g) h"),
                                          pages[:, k].rearrange("p g (h d) -> p g h d", h=NH), AX, ALU.add
                                          ).then_inc(ev("k_read"), 1)
                for u in range(8):
                    tile = proj[:, QR + u]
                    dve.wait_ge(ev("rot_made"), u + 1)
                    dve.tensor_tensor(rot[:, u % 2, :].rearrange("p (h c) -> p h c", h=2), pair(2 + u % 2),
                                      sin_t.rearrange("p (h c) -> p h c", h=2), ALU.mult).then_inc(ev("rot_read"), 1)
                    rest()
                    dve.wait_ge(ev("rot_read"), u + 1)
                    dve.wait_ge(ev("rot_cos"), u + 1)
                    link(dve.tensor_tensor(tile, tile, rot[:, u % 2, :], ALU.add))
                rest()
                for m in range(4):
                    link(dve.tensor_scalar(proj[:, KR + m], proj[:, KR + m], QSCALE, None, ALU.mult))
                rest()
                dve.wait_ge(ev("state_in"), 32)
                dve.tensor_tensor(state[:, :, :, :], state[:, :, :, :],
                                  gdec.unsqueeze(1).unsqueeze(3).to_broadcast([128, NS, 4, HD]), ALU.mult
                                  ).then_inc(ev("k_scaled"), 1)
                dve.wait_ge(ev("tok_copied"), 15)
                chain(dve.tensor_tensor(s_prod[:, :], q_s[:, :], k_s[:, :], ALU.mult))
                chain(dve.tensor_reduce(sm["den"][0:NS, 0:NH], s_prod[:, :].rearrange("p (h d) -> p h d", h=NH), AX, ALU.add))
                chain(dve.tensor_scalar(sm["den"][0:NS, 0:NH], sm["den"][0:NS, 0:NH], QSCALE, None, ALU.mult))
                dve.tensor_tensor(sm["max"][0:NS, :].rearrange("p (b h) -> p b h", b=NS),
                                  sm["den"][0:NS, 0:NH].unsqueeze(1).to_broadcast([NS, NS, NH]), delta, ALU.mult
                                  ).then_inc(ev("s_reduced"), 1)
                for j in range(4):
                    dve.wait_ge(ev("tok_t"), 13 + j)
                    dve.tensor_tensor(kr_tok[:, j, :].rearrange("p (h d) -> p h d", h=NH),
                                      ps[:, j, :].rearrange("p (h d) -> p h d", h=NH),
                                      tail[:, j, :].unsqueeze(2).to_broadcast([128, NH, HD]), ALU.mult).then_inc(ev("kr_copied"), 1)
                s_all = s_samp[:, :, :, :].rearrange("p b h g -> p (b h g)")
                s_pg = s_samp[:, :, :, :].rearrange("p b h g -> p (b h) g")
                wide = lambda v: v.unsqueeze(2).to_broadcast([128, 64, NPG])
                dve.wait_ge(ev("s_turned"), 1)
                link(dve.tensor_copy(sm["new"][:, :], ps[:, 5, 0:64]))
                dve.wait_ge(ev("after_made"), 1)
                chain(dve.scalar_tensor_tensor(s_all, s_all, QSCALE, ps[:, 6, :], ALU.mult, ALU.add))
                chain(dve.tensor_reduce(sm["max"][:, :], s_pg, AX, ALU.max))
                rest()
                dve.tensor_tensor(sm["max"][:, :], sm["max"][:, :], sm["new"][:, :], ALU.max).then_inc(ev("s_reduced"), 1)
                k_b = proj[:, KR:KR + 4, SEQ:NTOK].rearrange("p m b -> p b m")
                for g in range(4):
                    dve.wait_ge(ev("vr_spread"), g + 1)
                    dve.tensor_tensor(kv_s[:, 2 * g:2 * g + 2], ps[:, g, :].rearrange("p (b m e) -> p b m e", b=2, m=4),
                                      k_b[:, 2 * g:2 * g + 2].unsqueeze(3).to_broadcast([128, 2, 4, HD]), ALU.mult
                                      ).then_inc(ev("kv_read"), 1)
                dve.wait_ge(ev("kv_read"), 4)
                dve.wait_ge(ev("k_scaled"), 1)
                then("kv_added", dve.tensor_tensor(state[:, :, :, :], state[:, :, :, :], kv_s[:, :, :, :], ALU.add))
                dve.wait_ge(ev("s_turned"), 2)
                chain(dve.tensor_reduce(sm["col"][0:64, 0:1], ps[0:64, 4, 0:128], AX, ALU.max))
                dve.tensor_scalar(sm["den"][0:64, :], ident[0:64, 0:64], sm["col"][0:64, 0:1], None, ALU.mult
                                  ).then_inc(ev("s_reduced"), 1)
                dve.wait_ge(ev("s_turned"), 3)
                dve.tensor_tensor(s_pg, s_pg, wide(ps[:, 5, 64:128]), ALU.subtract).then_inc(ev("s_shifted"), 1)
                dve.tensor_tensor(sm["new"][:, :], sm["new"][:, :], ps[:, 5, 64:128], ALU.subtract).then_inc(ev("s_shifted"), 1)
                dve.wait_ge(ev("s_exp"), 2)
                dve.tensor_reduce(sm["max"][:, :], s_pg, AX, ALU.add).then_inc(ev("s_reduced"), 1)
                dve.wait_ge(ev("s_turned"), 4)
                chain(dve.tensor_tensor(sm["den"][:, :], sm["new"][:, :], ps[:, 5, 128:192], ALU.add))
                chain(dve.reciprocal(sm["den"][:, :], sm["den"][:, :]))
                link(dve.tensor_tensor(sm["new"][:, :], sm["new"][:, :], sm["den"][:, :], ALU.mult))
                link(dve.tensor_tensor(s_pg, s_pg, wide(sm["den"][:, :]), ALU.mult))
                rest()
                dve.tensor_tensor(sm["col"][0:NS, :].rearrange("p (b h) -> p b h", b=NS),
                                  sm["new"][0:NS, :].rearrange("p (b h) -> p b h", b=NS), delta, ALU.mult).then_inc(ev("p_samp"), 1)
                dve.wait_ge(ev("p_samp"), 1)
                chain(dve.tensor_reduce(sm["den"][0:NS, 0:NH], sm["col"][0:NS, :].rearrange("p (b h) -> p h b", b=NS), AX, ALU.add))
                dve.tensor_tensor(s_prod[:, :].rearrange("p (h d) -> p h d", h=NH), v_s[:, :].rearrange("p (h d) -> p h d", h=NH),
                                  sm["den"][0:NS, 0:NH].unsqueeze(2).to_broadcast([NS, NH, HD]), ALU.mult).then_inc(ev("new_v"), 1)

                def masked_scores(h):
                    for j in range(4):
                        v = probs[:, h % 2, PJ[j]:PJ[j] + (j + 1) * 128]
                        c = 4 * h + j
                        dve.wait_ge(ev("scores_done"), 8 * h + j + 1)
                        dve.wait_ge(ev("bias_done"), c + 1)
                        dve.scalar_tensor_tensor(v, ps[:, j % 2, 0:(j + 1) * 128], QSCALE, v, ALU.mult, ALU.add
                                                 ).then_inc(ev("score_read"), 1)
                        dve.wait_ge(ev("score_read"), 8 * h + j + 1)
                        chain(dve.tensor_tensor(v[:, j * 128:], v[:, j * 128:], causal, ALU.add))
                        dve.tensor_reduce(n_max[:, c:c + 1], v, AX, ALU.max, negate=True).then_inc(ev("max_done"), 1)
                    dve.wait_ge(ev(f"decay_in{h % 2}"), 16 * (h // 2 + 1))
                    if h >= 2:
                        dve.wait_ge(ev("ret_av"), h - 1)
                    for k in range(4):
                        w = SEQ - k * 128
                        dve.wait_ge(ev("scores_done"), 8 * h + k + 5)
                        dve.tensor_tensor(ret_a[h % 2][:, AK[k]:AK[k] + w], ps[:, k % 2, 0:w], decay[:, h % 2, 0:w], ALU.mult
                                          ).then_inc(ev("score_read"), 1)

                def normalise(h):
                    dve.wait_ge(ev("exp_done"), 4 * h + 4)
                    chain(dve.reciprocal(row_sum[:, 4 * h:4 * h + 4], row_sum[:, 4 * h:4 * h + 4]))
                    for j in range(4):
                        v = probs[:, h % 2, PJ[j]:PJ[j] + (j + 1) * 128]
                        dve.tensor_scalar(v, v, row_sum[:, 4 * h + j:4 * h + j + 1], None, ALU.mult).then_inc(ev("p_ready"), 1)

                dve.wait_ge(ev("state_stored"), 32)
                dve.wait_ge(ev("ret_s_made"), 1)
                masked_scores(0)
                normalise(0)
                for h in range(NH):
                    if h + 1 < NH:
                        masked_scores(h + 1)
                    dve.wait_ge(ev("v_used"), 2 * h + 2)
                    dve.tensor_tensor(own[h].rearrange("p (h d) -> p h d", h=NH),
                                      ps[0:NH, 7, :].rearrange("p (h d) -> p h d", h=NH),
                                      delta[:, :, 0:1].to_broadcast([NH, NH, HD]), ALU.mult).then_inc(ev("own_kept"), 1)
                    if h + 1 < NH:
                        normalise(h + 1)
                    if h % 2:
                        m = h // 2
                        dve.wait_ge(ev("ret_av"), h + 1)
                        dve.tensor_copy(proj[:, VR + m, 0:SEQ], ps[:, 5, :]).then_inc(ev("o_read"), 1)
                        dve.wait_ge(ev("fox_av"), h + 1)
                        dve.tensor_copy(proj[:, VF + m, 0:SEQ], ps[:, 4, :]).then_inc(ev("o_read"), 1)
                for m in range(4):
                    tile = proj[:, VR + m]
                    dve.wait_ge(ev("hn_mean"), m + 1)
                    dve.tensor_tensor(tile.rearrange("p (h c) -> p h c", h=2), tile.rearrange("p (h c) -> p h c", h=2),
                                      pair(m), ALU.subtract).then_inc(ev("hn_centred"), 1)
                dve.wait_ge(ev("hn_dev_done"), 1)
                dve.reciprocal(hn_dev[:, :], hn_dev[:, :]).then_inc(ev("hn_recip"), 1)
                dve.wait_ge(ev("fox_turned"), 1)
                dve.wait_ge(ev("new_v"), 1)
                dve.tensor_tensor(s_prod[:, :], s_prod[:, :], ps[0:NS, 2, :], ALU.add).then_inc(ev("fox_rows"), 1)

                def low_part(t):
                    dve.wait_ge(ev("cat_hi"), t + 1)
                    dve.tensor_tensor(h_lo[:, t, :, 0:HP], mixed_tile(t)[:, 0:SEQ].rearrange("p (h c) -> p h c", h=2),
                                      h_hi[:, t, :, 0:HP].bitcast(F32), ALU.subtract).then_inc(ev("cat_lo"), 1)

                low_part(0)
                low_part(1)
                for m in range(4):
                    tile = proj[:, VR + m]
                    dve.wait_ge(ev("hn_spread"), m + 1)
                    dve.wait_ge(ev("hn_gated"), m + 1)
                    dve.tensor_tensor(tile.rearrange("p (h c) -> p h c", h=2), tile.rearrange("p (h c) -> p h c", h=2),
                                      pair((2, 3, 0, 2)[m]), ALU.mult).then_inc(ev("hn_scaled"), 1)
                    if m == 1:
                        dve.wait_ge(ev("fox_turned"), 2)
                        dve.tensor_copy(proj[:, VF:VF + 4, SEQ:NTOK], ps[:, 3, 0:32].rearrange("p (m b) -> p m b", m=4)
                                        ).then_inc(ev("fox_s_done"), 1)
                for t in range(2, KT):
                    low_part(t)
                for u, first in enumerate((VF, VR)):
                    dve.wait_ge(ev("cat_hi"), KT + u + 1)
                    dve.tensor_tensor(h_lo[:, 4 * u:4 * u + 4, :, HP:HT],
                                      proj[:, first:first + 4, SEQ:NTOK].rearrange("p t (h c) -> p t h c", h=2),
                                      h_hi[:, 4 * u:4 * u + 4, :, HP:HT].bitcast(F32), ALU.subtract).then_inc(ev("cat_lo"), 1)

            def odd_dve():
                c0 = chunks_before(ODD)
                past = params[:, 384:512].rearrange("p (b j t) -> p j b t", b=NS, j=2)
                chain(dve.memset(up[:, 0:2], 0.0))
                dve.tensor_copy(tail_s[:, :, 0, :], past[:, 1]).then_inc(ev("conv_steps"), 1)
                half2 = lambda v: v.rearrange("p (h c) -> p h c", h=2)

                def body(i):
                    for j in range(2):
                        m = i * 2 + j
                        s0 = m * 12 + 1
                        w = [params[:, bass.ds(m + (CONV_W + 8 * q), 1)] for q in range(3)]

                        steps = ev("conv_steps")
                        dve.wait_ge(steps, s0)
                        dve.wait_ge(ev("cg_copied"), m + 1)
                        dve.wait_ge(chunk_used, c0 + i * 6 + 3 * j + 3)
                        dve.tensor_tensor(half2(up[:, 2:2 + SEQ]), cg[:, :, 0:HP], ps[:, 2:4, 0:HP], ALU.mult).then_inc(steps, 1)
                        dve.tensor_tensor(half2(up_s[:, :]), cg[:, :, HP:HT], ps[:, 2:4, HP:HT], ALU.mult).then_inc(steps, 1)
                        dve.wait_ge(steps, s0 + 1)
                        dve.tensor_scalar(z[:, :], up[:, 2:2 + SEQ], w[2], None, ALU.mult).then_inc(steps, 1)
                        dve.wait_ge(steps, s0 + 3)
                        dve.scalar_tensor_tensor(z[:, :], up[:, 1:1 + SEQ], w[1], z[:, :], ALU.mult, ALU.add).then_inc(steps, 1)
                        dve.wait_ge(steps, s0 + 4)
                        dve.scalar_tensor_tensor(z[:, :], up[:, 0:SEQ], w[0], z[:, :], ALU.mult, ALU.add).then_inc(steps, 1)
                        old = [past[:, q, :, bass.ds(m, 1)].rearrange("p b a -> p (b a)") for q in range(2)]
                        dve.tensor_scalar(z_s[:, :], up_s[:, :], w[2], None, ALU.mult).then_inc(steps, 1)
                        dve.wait_ge(steps, s0 + 6)
                        dve.scalar_tensor_tensor(z_s[:, :], old[1], w[1], z_s[:, :], ALU.mult, ALU.add).then_inc(steps, 1)
                        dve.wait_ge(steps, s0 + 7)
                        dve.scalar_tensor_tensor(z_s[:, :], old[0], w[0], z_s[:, :], ALU.mult, ALU.add).then_inc(steps, 1)
                        dve.wait_ge(steps, s0 + 8)
                        if not is_first(i):
                            dve.wait_ge(ev("mixed_hi"), m - 1)
                        dve.tensor_tensor(mixed[:, j, :, 0:HP], half2(z[:, :]), ps[:, 4 + 2 * j:6 + 2 * j, 0:HP], ALU.mult).then_inc(steps, 1)
                        dve.tensor_tensor(mixed[:, j, :, HP:HT], half2(z_s[:, :]), ps[:, 4 + 2 * j:6 + 2 * j, HP:HT], ALU.mult).then_inc(steps, 1)
                        dve.tensor_copy(tail_p[:, :, bass.ds(m, 1)].rearrange("p j a -> p (j a)"), up[:, SEQ:SEQ + 2]).then_inc(steps, 1)
                        dve.tensor_copy(tail_s[:, :, 1, bass.ds(m, 1)].rearrange("p b a -> p (b a)"), up_s[:, :]).then_inc(steps, 1)
                        dve.wait_ge(ev("mixed_hi"), m + 1)
                        t = bass.ds(m, 1)
                        dve.tensor_tensor(mix_lo[:, t].rearrange("p a h c -> p (a h) c"), mixed[:, j],
                                          mix_hi[:, t].rearrange("p a h c -> p (a h) c").bitcast(F32), ALU.subtract
                                          ).then_inc(ev("mixed_lo"), 1)
                loop(dve, True, KT // 2, body)

            dve.wait_ge(params_t, 1)
            for k, r in ((0, 128), (1, 112), (2, 96), (3, 128)):
                dve.tensor_copy(params[:, k * 128:k * 128 + r], ps[:, 0, k * 128:k * 128 + r]).then_inc(params_ready, 1)
            dve.wait_ge(params_ready, 4)
            dve.tensor_copy(c_t[:, :, :], params[:, C_AT:C_AT + 72].rearrange("p (b t) -> p t b", b=9)).then_inc(c_ready, 1)
            dve.wait_ge(cond_ready, 2)
            dve.tensor_tensor(c_parts[:, :, 9:18], c_act[:, :, :], c_parts[:, :, 0:9].bitcast(F32), ALU.subtract
                              ).then_inc(cond_ready, 1)
            modulation(0)
            modulate(0)
            dve.wait_ge(ada_used, MT)
            gate(0)
            for n in range(last):
                if n in FFN:
                    f0 = FT * ffns_before(n)

                    def body(i):
                        for j in range(2):
                            dve.wait_ge(chunk_used, chunks_before(n) + i * 4 + 2 * j + 2)
                            dve.wait_ge(silu_done, f0 + i * 2 + j + 1)
                            if not (n == 0 and is_first(i)):
                                dve.wait_ge(hid_hi_done, f0 + i * 2 + j - 1)
                            dve.tensor_tensor(gated[:, j], silu_a[:, j], pair(2 * j + 1), ALU.mult).then_inc(gate_done, 1)
                            dve.wait_ge(hid_hi_done, f0 + i * 2 + j + 1)
                            m = bass.ds(i * 2 + j, 1)
                            dve.tensor_tensor(hid_lo[:, m].rearrange("p a h c -> p (a h) c"), gated[:, j],
                                              hid_hi[:, m].rearrange("p a h c -> p (a h) c").bitcast(F32),
                                              ALU.subtract).then_inc(hid_lo_done, 1)
                    loop(dve, n == 0, FT // 2, body)
                    residuals(n, lambda i, j: dve.wait_ge(chunk_used, chunks_before(n, True) + i * 4 + 2 * j + 2))
                else:
                    (even_dve if n == EVEN else odd_dve)()
                    residuals(n, lambda i, j: dve.wait_ge(chunk_used, chunks_before(n, True) + i * 2 + j + 1))
                if n + 1 < last:
                    modulation(n + 1)
                norm(n)
                if n + 1 < last:
                    modulate(n + 1)
            dve.wait_ge(ln_done, KT * last)
            dve.tensor_copy(samp_t[:, :, :].rearrange("p t (h c) -> p t h c", h=2), x[:, :, :, HP:HT]).then_inc(samp_out, 1)


INPUTS = ["x_prompt", "x_sample", "cache_k", "cache_v", "cache_logf", "state_ret", "state_conv", "page_table",
          "c_prompt", "c_sample", "w_ada", "b_ada", "w_ffn_in", "w_ffn_out", "ln_g", "ln_b", "w_in_even",
          "b_forget", "w_out_even", "w_in_odd", "conv_w", "w_out_odd"]
OUTPUTS = [("y_prompt", (1, SEQ, D)), ("y_sample", (NS, 1, D)),
           ("k_prompt", (1, 1, SEQ, NH, HD)), ("v_prompt", (1, 1, SEQ, NH, HD)), ("logf_prompt", (1, 1, SEQ, NH)),
           ("ret_prompt", (1, 1, NH, HD, HD)), ("conv_prompt", (1, 1, 2, D)),
           ("k_sample", (1, NS, 1, NH, HD)), ("v_sample", (1, NS, 1, NH, HD)), ("logf_sample", (1, NS, 1, NH)),
           ("ret_sample", (1, NS, NH, HD, HD)), ("conv_sample", (1, NS, 2, D))]


def kernel(**inputs):
    from concourse import bacc as _bacc
    from concourse.bass_utils import run_bass_kernel_spmd

    nc = _bacc.Bacc("TRN2", target_bir_lowering=False, num_devices=1, dynamic_dma_scratch_size=1024)
    arrays = {name: np.ascontiguousarray(inputs[name]) for name in INPUTS}
    arrays.update(zip(("t_res", "t_even", "t_decay", "t_heads"), host_tables()))
    a = {name: nc.dram_tensor(name, v.shape, mybir.dt.from_np(v.dtype), kind="ExternalInput").ap()
         for name, v in arrays.items()}
    out = {name: nc.dram_tensor("out_" + name, shape, mybir.dt.float32, kind="ExternalOutput").ap()
           for name, shape in OUTPUTS}
    build_step(nc, a, out)
    result = run_bass_kernel_spmd(nc, [arrays], core_ids=[0])
    return tuple(result.results[0]["out_" + name].reshape(shape) for name, shape in OUTPUTS)
```
